# Optimizing a Trainium2 kernel written in Bass

```python
import jax, jax.numpy as jnp
from jax import lax
import numpy as np

D_MODEL = 1024
BATCH = 1
SEQ = 2048
DEPTH = 2
DEC_BATCH = 8
DEC_SEQ = 8
PAST_LEN = 2048
PAGE_SIZE = 128

N_A_LAYERS = DEPTH // 2
N_B_LAYERS = DEPTH - N_A_LAYERS
HEAD_DIM = 64
POOL_W = (3 * D_MODEL) // 4
POOL_WINDOWS = (2, 4, 8, 16)
POOL_GROUPS = len(POOL_WINDOWS)
POOL_GW = POOL_W // POOL_GROUPS
POOL_PAD = max(POOL_WINDOWS) - 1
N_Q_HEADS = POOL_W // HEAD_DIM
N_KV_HEADS = 4
GROUP = N_Q_HEADS // N_KV_HEADS
SWA_W = N_Q_HEADS * HEAD_DIM
KV_W = N_KV_HEADS * HEAD_DIM
WINDOW = 128
BLOCK = WINDOW
N_MEM = 256
MEM_HEADS = 4
MEM_W = MEM_HEADS * HEAD_DIM
ROT_DIM = HEAD_DIM // 4
ROPE_THETA = 500000.0
EPS = 1e-6

kernel_name = "yoco_pool_swa_sink_memxattn_step"

def rms_norm(x, g):
    xf = x.astype(jnp.float32)
    y = xf * lax.rsqrt(jnp.mean(xf * xf, axis=-1, keepdims=True) + EPS)
    return (y * g.astype(jnp.float32)).astype(x.dtype)

def rope_partial(x, pos):
    half = ROT_DIM // 2
    inv = ROPE_THETA ** (-jnp.arange(half, dtype=jnp.float32) * 2.0 / ROT_DIM)
    ang = pos.astype(jnp.float32)[:, None] * inv[None, :]
    cos = jnp.cos(ang)[:, None, :]
    sin = jnp.sin(ang)[:, None, :]
    xf = x.astype(jnp.float32)
    x1, x2, rest = xf[..., :half], xf[..., half:ROT_DIM], xf[..., ROT_DIM:]
    out = jnp.concatenate([x1 * cos - x2 * sin, x2 * cos + x1 * sin, rest], axis=-1)
    return out.astype(x.dtype)

def pool_mixer(u_ext, pos, mix_w, scale):
    T = u_ext.shape[1] - POOL_PAD
    uf = u_ext.astype(jnp.float32)
    cs = jnp.concatenate([jnp.zeros_like(uf[:, :1]), jnp.cumsum(uf, axis=1)], axis=1)
    u_new = uf[:, POOL_PAD:]
    outs = []
    for g, w in enumerate(POOL_WINDOWS):
        sl = slice(g * POOL_GW, (g + 1) * POOL_GW)
        win = cs[:, POOL_PAD + 1:POOL_PAD + 1 + T, sl] - cs[:, POOL_PAD + 1 - w:POOL_PAD + 1 - w + T, sl]
        cnt = jnp.minimum(pos + 1, w).astype(jnp.float32)[None, :, None]
        d = win / cnt - u_new[:, :, sl]
        outs.append(jnp.einsum('btc,cd->btd', d, mix_w[g].astype(jnp.float32)))
    y = jnp.concatenate(outs, axis=-1) * scale.astype(jnp.float32)
    return y.astype(u_ext.dtype)

def memory_kv(mem, g, w, k_gain):
    B, M, _ = mem.shape
    k, v = jnp.split(rms_norm(mem, g) @ w, [MEM_W], axis=-1)
    k = rms_norm(k.reshape(B, M, MEM_HEADS, HEAD_DIM), k_gain)
    return k, v.reshape(B, M, MEM_HEADS, HEAD_DIM)

def memory_branch(qm, gm, q_gain, mk, mv):
    B, T, _ = qm.shape
    q = rms_norm(qm.reshape(B, T, MEM_HEADS, HEAD_DIM), q_gain)
    s = jnp.einsum('bthd,bmhd->bhtm', q.astype(jnp.float32), mk.astype(jnp.float32)) * HEAD_DIM ** -0.5
    p = jax.nn.softmax(s, axis=-1)
    o = jnp.einsum('bhtm,bmhd->bthd', p, mv.astype(jnp.float32)).astype(qm.dtype)
    return o.reshape(B, T, MEM_W) * jax.nn.silu(gm)

def sink_softmax(s, mask, sinks):
    s = jnp.where(mask, s, -jnp.inf)
    sk = sinks.astype(jnp.float32).reshape(N_KV_HEADS, GROUP, 1, 1)
    m = jnp.maximum(jnp.max(s, axis=-1, keepdims=True), sk)
    p = jnp.exp(s - m)
    return p / (jnp.sum(p, axis=-1, keepdims=True) + jnp.exp(sk - m))

def swa_banded(q, k, v, sinks):
    B, S = q.shape[:2]
    nb = S // BLOCK
    qb = q.reshape(B, nb, BLOCK, N_KV_HEADS, GROUP, HEAD_DIM).astype(jnp.float32)

    def band(t):
        tb = t.reshape(B, nb, BLOCK, N_KV_HEADS, HEAD_DIM).astype(jnp.float32)
        prev = jnp.concatenate([jnp.zeros_like(tb[:, :1]), tb[:, :-1]], axis=1)
        return jnp.concatenate([prev, tb], axis=2)

    kk, vv = band(k), band(v)
    s = jnp.einsum('bnqhgd,bnkhd->bnhgqk', qb, kk) * HEAD_DIM ** -0.5
    qpos = jnp.arange(BLOCK)
    kpos = jnp.arange(2 * BLOCK) - BLOCK
    diff = qpos[:, None] - kpos[None, :]
    blk = jnp.arange(nb)[:, None, None] * BLOCK
    mask = (diff >= 0) & (diff < WINDOW) & (blk + kpos[None, None, :] >= 0)
    p = sink_softmax(s, mask[None, :, None, None], sinks)
    o = jnp.einsum('bnhgqk,bnkhd->bnqhgd', p, vv)
    return o.reshape(B, S, SWA_W).astype(q.dtype)

def swa_window(q, k_all, v_all, q_pos, k_pos, sinks):
    B, T = q.shape[:2]
    qg = q.reshape(B, T, N_KV_HEADS, GROUP, HEAD_DIM).astype(jnp.float32)
    s = jnp.einsum('bqhgd,bkhd->bhgqk', qg, k_all.astype(jnp.float32)) * HEAD_DIM ** -0.5
    diff = q_pos[:, None] - k_pos[None, :]
    mask = (diff >= 0) & (diff < WINDOW)
    p = sink_softmax(s, mask, sinks)
    o = jnp.einsum('bhgqk,bkhd->bqhgd', p, v_all.astype(jnp.float32))
    return o.reshape(B, T, SWA_W).astype(q.dtype)

def forward(x, pos, pool_prefix, swa_past_k, swa_past_v, mem_k, mem_v,
            norm_a, w_in_a, pool_mix_w, pool_scale, w_out_a, kv_norm, w_kv, k_norm,
            norm_b, w_in_b, q_norm, sinks, w_out_b, mem_q_norm):
    B, T, _ = x.shape
    new_pool = []
    for i in range(N_A_LAYERS):
        z = rms_norm(x, norm_a[i]) @ w_in_a[i]
        u, gp, qm, gm = jnp.split(z, [POOL_W, 2 * POOL_W, 2 * POOL_W + MEM_W], axis=-1)
        u_ext = jnp.concatenate([pool_prefix[i].astype(u.dtype), u], axis=1)
        yp = pool_mixer(u_ext, pos, pool_mix_w[i], pool_scale[i]) * jax.nn.silu(gp)
        ym = memory_branch(qm, gm, mem_q_norm[i], mem_k[i], mem_v[i])
        x = x + jnp.concatenate([yp, ym], axis=-1) @ w_out_a[i]
        new_pool.append(u_ext[:, -POOL_PAD:])
    k, v = jnp.split(rms_norm(x, kv_norm) @ w_kv, [KV_W], axis=-1)
    k = rope_partial(rms_norm(k.reshape(B, T, N_KV_HEADS, HEAD_DIM), k_norm), pos)
    v = v.reshape(B, T, N_KV_HEADS, HEAD_DIM)
    if swa_past_k is None:
        keep = min(WINDOW, T)
        new_k, new_v = k[:, -keep:], v[:, -keep:]
    else:
        L = swa_past_k.shape[1]
        k_all = jnp.concatenate([swa_past_k.astype(k.dtype), k], axis=1)
        v_all = jnp.concatenate([swa_past_v.astype(v.dtype), v], axis=1)
        k_pos = pos[0] - L + jnp.arange(L + T)
        new_k, new_v = k_all[:, -L:], v_all[:, -L:]
    for j in range(N_B_LAYERS):
        li = N_A_LAYERS + j
        z = rms_norm(x, norm_b[j]) @ w_in_b[j]
        q, gq, qm, gm = jnp.split(z, [SWA_W, 2 * SWA_W, 2 * SWA_W + MEM_W], axis=-1)
        q = rope_partial(rms_norm(q.reshape(B, T, N_Q_HEADS, HEAD_DIM), q_norm[j]), pos)
        if swa_past_k is None:
            o = swa_banded(q, k, v, sinks[j])
        else:
            o = swa_window(q, k_all, v_all, pos, k_pos, sinks[j])
        ys = o * jax.nn.silu(gq)
        ym = memory_branch(qm, gm, mem_q_norm[li], mem_k[li], mem_v[li])
        x = x + jnp.concatenate([ys, ym], axis=-1) @ w_out_b[j]
    return x, jnp.stack(new_pool), new_k, new_v

def setup_inputs(seed: int = 0) -> dict:
    key = jax.random.key(seed)
    ks = jax.random.split(key, 26)
    f32 = jnp.float32

    def nrm(k, shape, scale=1.0):
        return jax.random.normal(k, shape, f32) * scale

    def gain(k, shape):
        return 1.0 + 0.02 * jax.random.normal(k, shape, f32)

    w_buf = min(WINDOW, PAST_LEN)
    return {
        "x_prompt": nrm(ks[0], (BATCH, SEQ, D_MODEL)),
        "x_sample": nrm(ks[1], (DEC_BATCH, DEC_SEQ, D_MODEL)),
        "state_pool": nrm(ks[2], (N_A_LAYERS, DEC_BATCH, POOL_PAD, POOL_W)),
        "cache_swa_k": nrm(ks[3], (DEC_BATCH, w_buf, N_KV_HEADS, HEAD_DIM)),
        "cache_swa_v": nrm(ks[4], (DEC_BATCH, w_buf, N_KV_HEADS, HEAD_DIM)),
        "cache_mem_k": nrm(ks[5], (DEPTH, DEC_BATCH, N_MEM, MEM_HEADS, HEAD_DIM)),
        "cache_mem_v": nrm(ks[6], (DEPTH, DEC_BATCH, N_MEM, MEM_HEADS, HEAD_DIM)),
        "mem_prompt": nrm(ks[7], (BATCH, N_MEM, D_MODEL)),
        "norm_a": gain(ks[8], (N_A_LAYERS, D_MODEL)),
        "w_in_a": nrm(ks[9], (N_A_LAYERS, D_MODEL, 2 * POOL_W + 2 * MEM_W), D_MODEL ** -0.5),
        "pool_mix_w": nrm(ks[10], (N_A_LAYERS, POOL_GROUPS, POOL_GW, POOL_GW), POOL_GW ** -0.5),
        "pool_scale": 1.0 + 0.1 * jax.random.normal(ks[11], (N_A_LAYERS, POOL_W), f32),
        "w_out_a": nrm(ks[12], (N_A_LAYERS, POOL_W + MEM_W, D_MODEL), (POOL_W + MEM_W) ** -0.5),
        "kv_norm": gain(ks[13], (D_MODEL,)),
        "w_kv": nrm(ks[14], (D_MODEL, 2 * KV_W), D_MODEL ** -0.5),
        "k_norm": gain(ks[15], (HEAD_DIM,)),
        "norm_b": gain(ks[16], (N_B_LAYERS, D_MODEL)),
        "w_in_b": nrm(ks[17], (N_B_LAYERS, D_MODEL, 2 * SWA_W + 2 * MEM_W), D_MODEL ** -0.5),
        "q_norm": gain(ks[18], (N_B_LAYERS, HEAD_DIM)),
        "sinks": nrm(ks[19], (N_B_LAYERS, N_Q_HEADS), 1.0),
        "w_out_b": nrm(ks[20], (N_B_LAYERS, SWA_W + MEM_W, D_MODEL), (SWA_W + MEM_W) ** -0.5),
        "mem_norm": gain(ks[21], (DEPTH, D_MODEL)),
        "w_mem_kv": nrm(ks[22], (DEPTH, D_MODEL, 2 * MEM_W), D_MODEL ** -0.5),
        "mem_q_norm": gain(ks[23], (DEPTH, HEAD_DIM)),
        "mem_k_norm": gain(ks[24], (DEPTH, HEAD_DIM)),
    }

def reference(x_prompt, x_sample, state_pool, cache_swa_k, cache_swa_v, cache_mem_k, cache_mem_v, mem_prompt,
              norm_a, w_in_a, pool_mix_w, pool_scale, w_out_a, kv_norm, w_kv, k_norm,
              norm_b, w_in_b, q_norm, sinks, w_out_b, mem_norm, w_mem_kv, mem_q_norm, mem_k_norm):
    mk_list, mv_list = [], []
    for l in range(DEPTH):
        mk, mv = memory_kv(mem_prompt, mem_norm[l], w_mem_kv[l], mem_k_norm[l])
        mk_list.append(mk)
        mv_list.append(mv)
    mem_k_prompt = jnp.stack(mk_list)
    mem_v_prompt = jnp.stack(mv_list)

    weights = (norm_a, w_in_a, pool_mix_w, pool_scale, w_out_a, kv_norm, w_kv, k_norm,
               norm_b, w_in_b, q_norm, sinks, w_out_b, mem_q_norm)

    bp, s_len, _ = x_prompt.shape
    pool_zero = jnp.zeros((N_A_LAYERS, bp, POOL_PAD, POOL_W), x_prompt.dtype)
    y_prompt, pool_p, swa_k_p, swa_v_p = forward(
        x_prompt, jnp.arange(s_len), pool_zero, None, None, mem_k_prompt, mem_v_prompt, *weights)

    pos_s = PAST_LEN + jnp.arange(x_sample.shape[1])
    y_sample, pool_s, swa_k_s, swa_v_s = forward(
        x_sample, pos_s, state_pool, cache_swa_k, cache_swa_v, cache_mem_k, cache_mem_v, *weights)

    return (y_prompt, y_sample, pool_p, pool_s, swa_k_p, swa_v_p, swa_k_s, swa_v_s, mem_k_prompt, mem_v_prompt)


_drawn_inputs = setup_inputs


def setup_inputs(seed=0):
    import zlib

    import numpy as np

    out = dict(_drawn_inputs(seed))
    spreads = {}
    factors = {'norm_a': 2.954,
     'kv_norm': 2.71,
     'k_norm': 3.023,
     'norm_b': 8.0,
     'q_norm': 8.0,
     'sinks': 44.62,
     'mem_norm': 2.739,
     'mem_q_norm': 8.0,
     'mem_k_norm': 2.907}
    for name, (base, spread) in spreads.items():
        noise = np.random.default_rng([zlib.crc32(name.encode()), seed]).standard_normal(out[name].shape)
        drawn = base * np.exp(spread * noise) if base else spread * noise
        out[name] = __import__('jax').numpy.asarray(drawn.astype(out[name].dtype))
    for name, factor in factors.items():
        out[name] = (out[name] * factor).astype(out[name].dtype)
    return out
```

```python
from contextlib import ExitStack

import numpy as np
import concourse.bass as bass
from concourse import mybir

F32 = mybir.dt.float32
ALU = mybir.AluOpType
ACT = mybir.ActivationFunctionType
AX = mybir.AxisListType

P = 128
D = 1024
KC = D // P
NT = 256
SEQ = 2048
TILES = SEQ // NT
BLK = 128
NBLK = NT // BLK
HD = 64
DB, DS = 8, 8
NS = DB * DS
NMEM = 256
MC = NMEM // P
POOLC = 6
PAD = 15
UW = 16 + NT
US = 16 + DS
QH = 12
EPS = 1e-6
BIG = 1e30
SCALE = HD ** -0.5
WINDOWS = (2, 4, 8, 16)

SMALL = {}


def _small_layout():
    at = 0
    for name, n in (
        ("gain", 5 * KC),
        ("pscale", POOLC),
        ("row", 6 * HD),
        ("sink", QH),
        ("sinkcol", 1),
        ("invw", POOLC),
        ("corr", POOLC * 16),
        ("cos", 16 * 16),
        ("sin", 16 * 16),
        ("cos_s", 16),
        ("sin_s", 16),
        ("ident", P),
        ("cur_hi", P),
        ("prev_hi", P),
        ("prev_now", P),
        ("curT", P),
        ("prevT", P),
        ("new_hi", DS),
        ("old_hi", DS),
        ("oldT", 96),
        ("newT", 96),
    ):
        SMALL[name] = (at, n)
        at += n
    return at


NSMALL = _small_layout()

ROW_MEMQ, ROW_MEMK, ROW_K, ROW_Q = 0, 2, 4, 5


class Signal:

    TRIPS = {"pre": 1, "A": TILES, "SA": 1, "B": TILES, "SB": 1}

    def __init__(self, sem, per_tile, step=1, primed=0):
        self.sem, self.n, self.step = sem, per_tile, step
        self.base, at = {}, primed
        for part, trips in self.TRIPS.items():
            self.base[part] = at
            at += per_tile.get(part, 0) * trips
        self.total = at * step

    def after(self, part, tile, k=0):
        return (tile * self.n.get(part, 0) + (self.base[part] + k + 1)) * self.step


class Ring:

    def __init__(self, full, free, groups, primed=0):
        self.full, self.free, self.groups, self.primed = full, free, groups, primed
        self.nb = len(full)
        self.base, at = {}, 0
        for part, trips in Signal.TRIPS.items():
            self.base[part] = at
            n = len(groups.get(part, ()))
            assert trips == 1 or n % self.nb == 0, (part, n)
            at += n * trips

    def bank(self, part, name):
        return (self.base[part] + self.groups[part].index(name)) % self.nb

    def before(self, part, tile, name):
        at = self.base[part] + self.groups[part].index(name)
        return tile * (len(self.groups[part]) // self.nb) + at // self.nb

    def wait_free(self, eng, part, tile, name):
        n = self.before(part, tile, name)
        if not (isinstance(n, int) and n + self.primed == 0):
            eng.wait_ge(self.free[self.bank(part, name)], n + self.primed)
        return self.bank(part, name)

    def wait_full(self, eng, part, tile, name):
        eng.wait_ge(self.full[self.bank(part, name)], self.before(part, tile, name) + 1)
        return self.bank(part, name)

    def wait_read(self, eng, part, tile, name):
        eng.wait_ge(self.free[self.bank(part, name)], self.before(part, tile, name) + 1 + self.primed)


class Steps:

    def __init__(self, eng, sem):
        self.eng, self.sem = eng, sem
        self.before_loop = self.k = self.per = 0
        self.tile_ = 0

    def loop(self, per):
        self.before_loop, self.k, self.per = self.before_loop + self.k, per, per

    def tile(self, t):
        assert self.k == self.per, ("steps of a tile", self.k)
        self.k, self.tile_ = 0, t

    def end_loop(self, tiles):
        assert self.k == self.per, ("steps of a tile", self.k)
        self.before_loop, self.k, self.per, self.tile_ = self.before_loop + tiles * self.per, 0, 0, 0

    def __call__(self, ins):
        ins.then_inc(self.sem, 1)
        self.k += 1

    def wait(self):
        self.eng.wait_ge(self.sem, self.tile_ * self.per + (self.before_loop + self.k))


def build(nc, io):
    with ExitStack() as ctx:
        def sb(name, shape):
            return ctx.enter_context(nc.sbuf_tensor(name + "_sb", [P, *shape], F32))

        def sem(name):
            return ctx.enter_context(nc.semaphore(name))

        w_in = sb("w_in", [8, KC, 256])
        w_out = sb("w_out", [4, KC, 256])
        w_x = sb("w_x", [4096])
        x_buf = sb("x_buf", [2, KC, NT])
        xn = sb("xn", [KC, NT])
        big = sb("big", [8, NT])
        pm = sb("pm", [NBLK, 4, NMEM])
        gate = sb("gate", [KC, NT])
        scr = sb("scr", [2, 512])
        kTm = sb("kTm", [2, NMEM])
        vm = sb("vm", [MC, 256])
        ph = sb("ph", [6656])
        small = sb("small", [NSMALL])
        ones = sb("ones", [P])
        diag = sb("diag", [NBLK, P])
        tiny = sb("tiny", [232])

        def sm(name):
            a, n = SMALL[name]
            return small[:, a:a + n]

        gain = sm("gain").rearrange("p (g k) -> p g k", g=5)
        ident = sm("ident")
        invw, pscale = sm("invw"), sm("pscale")
        corr = sm("corr").rearrange("p (c t) -> p c t", c=POOLC)

        def row(n, heads, parts=P):
            a = SMALL["row"][0] + n * HD
            return small[0:parts, a:a + HD].rearrange("p (h d) -> p h d", h=1).to_broadcast([parts, heads, HD])

        x_var, x_rstd = tiny[:, 0:2], tiny[:, 2:4]
        q_ss = tiny[:, 4:20]
        q_rstds = [tiny[:, 20:36], tiny[:, 212:228]]
        k_ss = tiny[:, 36:44]
        k_rstds = [tiny[:, 44:52], q_rstds[1][:, 0:8]]
        m_max = tiny[:, 52:60].rearrange("p (b e) -> p b e", b=2)
        m_neg = tiny[:, 60:68].rearrange("p (b e) -> p b e", b=2)
        m_sum = tiny[:, 68:76].rearrange("p (b e) -> p b e", b=2)
        m_inv = tiny[:, 76:84].rearrange("p (b e) -> p b e", b=2)
        w_max = tiny[:, 84:92].rearrange("p (b e) -> p b e", b=2)
        w_neg = tiny[:, 92:100].rearrange("p (b e) -> p b e", b=2)
        w_sum = tiny[:, 100:108].rearrange("p (b e) -> p b e", b=2)
        w_inv = tiny[:, 108:116].rearrange("p (b e) -> p b e", b=2)
        w_sd = tiny[:, 116:124].rearrange("p (b e) -> p b e", b=2)
        w_se = tiny[:, 124:132].rearrange("p (b e) -> p b e", b=2)
        power = tiny[:, 192:208]
        half_scale = tiny[:, 134:134 + POOLC]
        s_max, s_neg, s_sum, s_inv = (tiny[0:96, 144 + 8 * i:152 + 8 * i] for i in range(4))
        s_sd, s_se = tiny[0:96, 176:184], tiny[0:96, 184:192]
        rot = sb("rot", [QH, 16])

        def flat(a):
            return a.rearrange("p e n -> p (e n)")

        def q_of(blk):
            return flat(pm[:, blk]).rearrange("p (h d) -> p h d", h=16)

        quarters = [flat(pm[:, i // 2])[:, (i % 2) * 512:(i % 2 + 1) * 512].rearrange("p (c n) -> p c n", c=2)
                    for i in range(4)]
        k_mem = quarters[0:2]
        kT_mem, v_mem = [kTm[:, :, :], quarters[2]], [vm[:, :, :], quarters[3]]

        qT_a = ph[:, 0:512].rearrange("p (c t) -> p c t", c=2)
        u = ph[:, 512:512 + POOLC * UW].rearrange("p (c t) -> p c t", c=POOLC)
        win_a = ph[:, 2144:2144 + POOLC * UW].rearrange("p (c t) -> p c t", c=POOLC)
        win_b = ph[:, 3776:3776 + POOLC * UW].rearrange("p (c t) -> p c t", c=POOLC)
        mix_w = w_x[:, 0:14 * P].rearrange("p (n m) -> p n m", n=14)
        qT_b = ph[:, 0:2048].rearrange("p (c t) -> p c t", c=8)
        ptc = ph[:, 2048:2560].rearrange("p (e t) -> p e t", e=4)
        ptp = ph[:, 2560:3072].rearrange("p (e t) -> p e t", e=4)
        kT = ph[:, 3072:4096].rearrange("p (k s t) -> p k s t", k=2, s=4)
        v = ph[:, 4096:5120].rearrange("p (s n) -> p s n", s=4)
        sw = ph[:, 5120:6144].rearrange("p (b e t) -> p b e t", b=2, e=4)
        k_tok = ph[:, 6144:6656].rearrange("p (b h d) -> p b h d", b=2, h=4)
        w_kv = w_x[:, :].rearrange("p (g k n) -> p g k n", g=2, k=KC)
        lo = sb("lo", [4, BLK])

        ps_z = ctx.enter_context(nc.psum_tensor("ps_z", [P, 2, 512], F32))
        ps_s = ctx.enter_context(nc.psum_tensor("ps_s", [P, 2, 2, 512], F32))
        ps_t = ctx.enter_context(nc.psum_tensor("ps_t", [P, 512], F32))
        ps_p = ctx.enter_context(nc.psum_tensor("ps_p", [P, 512], F32))


        qbd_a = ph[:, 0:512].rearrange("p (c b n) -> p c b n", c=2, b=DB)
        state_tmp = pm[:, 1, :, :].rearrange("p e n -> p (e n)")[:, 0:POOLC * DB * PAD]\
            .rearrange("p (c b t) -> p c b t", c=POOLC, b=DB)
        pt_s = big[:, 0:2, :]
        w_flat = w_in[:, :, :, :].rearrange("p g k n -> p (g k n)")
        qbd_w = w_flat[:, 0:1536].rearrange("p (k b n) -> p k b n", k=2, b=DB)
        qbd_b = w_flat[:, 1536:2048].rearrange("p (c b n) -> p c b n", c=2, b=DB)
        v_new = w_flat[0:DS, 2048:4096].rearrange("p (b n) -> p b n", b=DB)
        sw_s = w_flat[0:96, 4096:5120].rearrange("p (b t) -> p b t", b=DB)
        pt_old = w_flat[:, 5120:5888].rearrange("p (b n) -> p b n", b=DB)
        pt_new = w_flat[0:DS, 5888:6656].rearrange("p (b n) -> p b n", b=DB)
        lo_s = w_flat[0:96, 6656:6720].rearrange("p (b t) -> p b t", b=DB)
        kT_new = ph[:, 3072:3200].rearrange("p (k t) -> p k t", k=2)
        kT_old = w_x[:, 0:2048].rearrange("p (k b t) -> p k b t", k=2, b=DB)
        v_old = w_x[:, 2048:4096].rearrange("p (b n) -> p b n", b=DB)

        def pooled(c):
            return win_a[:, c] if c in (0, 3) else win_b[:, c]

        def by_batch(x):
            return x[:, 0:DB * US].rearrange("p (b t) -> p b t", b=DB)

        def slot(xb, n):
            return x_buf[:, xb].rearrange("p k n -> p (k n)")[:, (n % 4) * 512:(n % 4 + 1) * 512]\
                .rearrange("p (c n) -> p c n", c=2)

        def tile_of(d, t):
            return d[t] if isinstance(t, int) else d[bass.ds(t, 1)].rearrange("a p k n -> (a p) k n")

        U3, G3 = ["u0", "u1", "u2"], ["g0", "g1", "g2"]
        OUT = ["out0", "out1", "out2", "out3"]
        PTM = ["ptm00", "ptm01", "ptm10", "ptm11"]
        OUTS = ["out0", "out1", "rb", "out2", "out3"]
        W6 = [(0, 0), (1, 0), (0, 1), (1, 1), (0, 2), (1, 2)]
        Z = Ring([sem("z_full0"), sem("z_full1")], [sem("z_free0"), sem("z_free1")], {
            "pre": ["rb_mem", "mem00", "mem01", "mem10", "mem11", "rb"],
            "A": ["qm", *U3, *G3, "gm", "mix0", "mix1", "mix2", *OUTS],
            "SA": ["qm", *U3, *G3, "gm", "mix0", "mix1", "mix2", *OUT, "rb"],
            "B": ["kv0", "kv1", "qa0", "qb0", "qa1", "qb1", "gm", "g0", "g1", "g2", "out0", "ss", *OUTS[1:]],
            "SB": ["kv0", "qa0", "qb0", "gm", *G3, *OUT],
        })
        T = Ring([sem("t_full")], [sem("t_free")], {
            "pre": ["ss_mem", "kt0", "kt1", "ss"],
            "A": ["qT", *PTM, "ss"],
            "SA": ["qT", "pt0", "pt1", "ss"],
            "B": ["kT", "qT00", "qT01", "qT10", "qT11", "ptw0", "ptm00", "ptm01", "ptw1", "ptm10", "ptm11",
                  "ptw2", "ptw3", "ptw4", "ptw5"],
            "SB": ["kT", "qT00", "qT01", "pt0", "pt1", "ptw0", "ptw1"],
        })
        S = Ring([sem("s_full0"), sem("s_full1")], [sem("s_free0"), sem("s_free1")], {
            "A": ["m0", "m1"],
            "SA": ["m"],
            "B": ["m0", "w0", "w1", "m1", "w2", "w3", "w4", "w5"],
            "SB": ["m", "wn", "wc"],
        }, primed=1)
        V = Ring([sem("p_full")], [sem("p_free")], {
            "A": ["pvm"], "SA": ["pvm"],
            "B": ["pvw0", "pvw1", "pvm", "pvw2", "pvw3", "pvw4", "pvw5"],
            "SB": ["pvm", "pvw0", "pvw1"],
        }, primed=1)

        one = {"pre": 2, "A": 1, "SA": 1, "B": 1}
        small_in = sem("small_in")
        win_in = [sem(f"win_in{g}") for g in range(8)]
        wout_in = [sem(f"wout_in{g}") for g in range(4)]
        wx_in = [sem("wx_in0"), sem("wx_in1")]
        x_in = [sem("x_in0"), sem("x_in1")]
        x_stored = Signal(sem("x_stored"), {"pre": 1, "A": 1, "SA": 1, "B": 1, "SB": 1}, 16)
        outputs = sem("outputs")
        state_in = sem("state_in")
        state_out = sem("state_out")
        mem_reload = sem("mem_reload")
        vnew_in = sem("vnew_in")
        slot_in = [sem(f"slot_in{i}") for i in range(4)]
        slot_used = Signal(sem("slot_used"), {"SA": 14, "SB": 14})
        sq_x = Signal(sem("sq_x"), one)
        sums_x = Signal(sem("sums_x"), one)
        rstd_x = Signal(sem("rstd_x"), one)
        diag_x = Signal(sem("diag_x"), one)
        scr_in = Signal(sem("scr_in"), {"pre": 4, "A": 5, "SA": 5, "B": 10, "SB": 7})
        heads_var = Signal(sem("heads_var"), {"pre": 2, "A": 1, "SA": 1, "B": 3, "SB": 2})
        heads_norm = Signal(sem("heads_norm"), {"pre": 2, "A": 1, "SA": 1, "B": 3, "SB": 2})
        m_neg_in = Signal(sem("m_neg_in"), {"A": 2, "SA": 1, "B": 2, "SB": 1})
        m_inv_in = Signal(sem("m_inv_in"), {"A": 2, "SA": 1, "B": 2, "SB": 1})
        pm_norm = Signal(sem("pm_norm"), {"A": 2, "SA": 1, "B": 2, "SB": 1})
        w_neg_in = Signal(sem("w_neg_in"), {"B": 6, "SB": 1})
        w_exp = Signal(sem("w_exp"), {"B": 6, "SB": 1})
        w_inv_in = Signal(sem("w_inv_in"), {"B": 6, "SB": 1})
        pw_norm = Signal(sem("pw_norm"), {"B": 6, "SB": 1})
        u_free = Signal(sem("u_free"), {"pre": 1, "A": 1, "SA": 1})
        win_sums = Signal(sem("win_sums"), {"A": 1, "SA": 1})
        d_in = Signal(sem("d_in"), {"A": 1, "SA": 1})
        pool_out = sem("pool_out")
        state_set = sem("state_set")
        qbd_zero = Signal(sem("qbd_zero"), {"SA": 1, "SB": 1})
        consts = sem("consts")
        kv_folded = sem("kv_folded")
        in_folded = [sem("in_folded_v"), sem("in_folded_p")]
        acts, dves, pools = sem("act_steps"), sem("dve_steps"), sem("pool_steps")
        FOLD_V, FOLD_P = range(0, 4), range(4, 8)

        def load_slot(sp, part, n, layer, xb):
            if n >= 4:
                m = n - 4
                if m == 7:
                    S.wait_full(sp, part, 0, "m")
                else:
                    sp.wait_ge(slot_used.sem, slot_used.after(part, 0, m if m < 7 else m - 1))
            src = io["mem_ks"][layer, n] if n < DB else io["mem_vs"][layer, n - DB]
            nc.sync.dma_start(slot(xb, n), src).then_inc(slot_in[n % 4], 16)

        def wait_slot(pe, part, n):
            pe.wait_ge(slot_in[n % 4], 16 * ((4 if part == "SB" else 0) + n // 4 + 1))

        block = ctx.enter_context(nc.Block())
        xd, x1d, yd = io["x"], io["x1"], io["y"]

        @block.sync
        def _(sp):
            dma = nc.sync.dma_start
            dma(small[:, :], io["small"]).then_inc(small_in, 16)
            dma(x_buf[:, 1], io["memx"]).then_inc(x_in[1], 16)
            for g in range(4):
                dma(w_out[:, g], io["w_mem"][g]).then_inc(wout_in[g], 16)
            dma(x_buf[:, 0], xd[0]).then_inc(x_in[0], 16)
            for g in range(8):
                dma(w_in[:, g], io["w_in_a"][g]).then_inc(win_in[g], 16)
            dma(w_x[:, 0:14 * P], io["mix"]).then_inc(wx_in[0], 16)

            for l in range(2):
                sp.wait_ge(heads_norm.sem, heads_norm.after("pre", 0, l))
                dma(io["mem_k"][l], k_mem[l]).then_inc(outputs, 16)
                T.wait_read(sp, "pre", 0, f"kt{l}")
                dma(io["mem_v"][l], v_mem[l]).then_inc(outputs, 16)
            dma(io["kt1"], kT_mem[1]).then_inc(x_stored.sem, 16)
            for g in range(4):
                dma(w_out[:, g], io["w_out_a"][g]).then_inc(wout_in[g], 16)

            with sp.Fori(0, TILES // 2) as it:
                for p in range(2):
                    t = it * 2 + p
                    sp.wait_ge(x_stored.sem, x_stored.after("A", t, -1))
                    dma(x_buf[:, 1 - p], tile_of(xd, t + 1)).then_inc(x_in[1 - p], 16)
                    Z.wait_read(sp, "A", t, "out3")
                    dma(tile_of(x1d, t), x_buf[:, p]).then_inc(x_stored.sem, 16)

            sp.wait_ge(u_free.sem, u_free.after("A", TILES - 1))
            dma(io["pool_p"], u[:, :, 1:16]).then_inc(state_out, 16)
            V.wait_full(sp, "A", TILES - 1, "pvm")
            dma(state_tmp, io["state"]).then_inc(state_in, 16)
            sp.wait_ge(outputs, 4 * 16)
            dma(kTm[:, :, :], io["kt1"]).then_inc(mem_reload, 16)
            dma(vm[:, :, :], io["mem_v"][1]).then_inc(mem_reload, 16)
            sp.wait_ge(x_stored.sem, x_stored.after("A", TILES - 1))
            for n in range(12):
                load_slot(sp, "SA", n, 0, 1)
            Z.wait_full(sp, "SA", 0, "gm")
            for g in (0, 1):
                dma(w_in[:, g], io["w_in_b"][g]).then_inc(win_in[g], 16)
            for n in range(12, 16):
                load_slot(sp, "SA", n, 0, 1)
            sp.wait_ge(pool_out, 1)
            dma(io["pool_s"], state_tmp).then_inc(state_out, 16)
            Z.wait_full(sp, "SA", 0, "mix2")
            for g in range(2):
                dma(w_x[:, g * 2048:(g + 1) * 2048].rearrange("p (k n) -> p k n", k=KC), io["w_kv"][g])\
                    .then_inc(wx_in[g], 16)
            V.wait_full(sp, "SA", 0, "pvm")
            dma(x_buf[:, 1], x1d[0]).then_inc(x_in[1], 16)
            for g in range(2, 8):
                dma(w_in[:, g], io["w_in_b"][g]).then_inc(win_in[g], 16)
            Z.wait_full(sp, "SA", 0, "out3")
            for g in range(4):
                dma(w_out[:, g], io["w_out_b"][g]).then_inc(wout_in[g], 16)
            Z.wait_read(sp, "SA", 0, "out3")
            dma(x1d[TILES], x_buf[:, 0]).then_inc(x_stored.sem, 16)
            dma(io["swa_k_s"][:, 0:BLK - DS], io["kc_tok"][:, DS:BLK]).then_inc(outputs, 16)
            dma(io["swa_v_s"][:, 0:BLK - DS], io["vc_tok"][:, DS:BLK]).then_inc(outputs, 16)

            with sp.Fori(0, TILES // 2) as it:
                for p in range(2):
                    t = it * 2 + p
                    sp.wait_ge(x_stored.sem, x_stored.after("B", t, -1))
                    dma(x_buf[:, p], tile_of(x1d, t + 1)).then_inc(x_in[p], 16)
                    Z.wait_read(sp, "B", t, "out3")
                    dma(tile_of(yd, t), x_buf[:, 1 - p]).then_inc(x_stored.sem, 16)

            dma(io["swa_k_p"], k_tok[:, 1].rearrange("p h d -> p (h d)")).then_inc(outputs, 16)
            dma(io["swa_v_p"], v[:, 3]).then_inc(outputs, 16)
            sp.wait_ge(x_stored.sem, x_stored.after("B", TILES - 1))
            for n in range(8):
                load_slot(sp, "SB", n, 1, 0)
            Z.wait_full(sp, "SB", 0, "kv0")
            dma(kT_old, io["kc"]).then_inc(wx_in[0], 16)
            dma(v_old, io["vc"]).then_inc(wx_in[1], 16)
            Z.wait_full(sp, "SB", 0, "g2")
            for b in range(DB):
                dma(v_new[:, b], v[b * DS:(b + 1) * DS, 0]).then_inc(vnew_in, 16)
            sp.wait_ge(heads_norm.sem, heads_norm.after("SB", 0, 0))
            for b in range(DB):
                rows = slice(b * DS, (b + 1) * DS)
                dma(io["swa_k_s"][b, BLK - DS:BLK], k_tok[rows, 0].rearrange("p h d -> p (h d)")).then_inc(outputs, 16)
                dma(io["swa_v_s"][b, BLK - DS:BLK], v[rows, 0]).then_inc(outputs, 16)
            for n in range(8, 16):
                load_slot(sp, "SB", n, 1, 0)
            Z.wait_read(sp, "SB", 0, "out3")
            dma(yd[TILES], x_buf[:, 1]).then_inc(x_stored.sem, 16)
            sp.wait_ge(x_stored.sem, x_stored.total)
            sp.wait_ge(state_out, 32)
            sp.wait_ge(outputs, 16 * (4 + 2 + 2 + 2 * DB))

        @block.tensor
        def _(pe):
            mm, tr = nc.tensor.matmul, nc.tensor.transpose

            def square_sums(ring, part, t, name, k, n=2):
                pe.wait_ge(sums_x.sem, sums_x.after(part, t, k))
                b = ring.wait_free(pe, part, t, name)
                out = ps_t if ring is T else ps_z[:, b]
                for blk in range(NBLK):
                    last = mm(out[:, blk:blk + 1], big[:, 0, blk * P:(blk + 1) * P], ones[:, 0:1],
                              start=True, stop=True)
                last.then_inc(ring.full[b], 1)

            def rstd_rows(part, t, name, k):
                pe.wait_ge(diag_x.sem, diag_x.after(part, t, k))
                b = Z.wait_free(pe, part, t, name)
                for blk in range(NBLK):
                    last = mm(ps_z[:, b, blk * P:(blk + 1) * P], ones[:, :], diag[:, blk, :], start=True, stop=True)
                last.then_inc(Z.full[b], 1)

            def by_token(part, t, name, src, tok, w, g, n=P):
                b = Z.wait_free(pe, part, t, name)
                for kc in range(KC):
                    last = mm(ps_z[0:n, b, :].rearrange("p (g n) -> p g n", g=2), src[:, kc, tok:tok + n],
                              w[:, g:g + 2, kc, :], start=(kc == 0), stop=(kc == KC - 1))
                last.then_inc(Z.full[b], 1)

            def by_feature(part, t, name, src, w, g, n=NT, halves=(0, 1)):
                b = Z.wait_free(pe, part, t, name) if 0 in halves else Z.bank(part, name)
                for half in halves:
                    for kc in range(KC):
                        last = mm(ps_z[:, b, half * NT:half * NT + n], w[:, g, kc, half * P:(half + 1) * P],
                                  src[:, kc, 0:n], start=(kc == 0), stop=(kc == KC - 1))
                if 1 in halves:
                    last.then_inc(Z.full[b], 1)

            def mem_scores(part, t, blk, qT, c0):
                b = S.wait_free(pe, part, t, f"m{blk}")
                for c in range(2):
                    for par in range(2):
                        rows = slice(par * HD, (par + 1) * HD)
                        last = mm(ps_s[:, b, par, c * NMEM:(c + 1) * NMEM],
                                  qT[rows, c0 + c, blk * P:(blk + 1) * P], kTm[rows, c, :], start=True, stop=True)
                last.then_inc(S.full[b], 1)

            def mem_transposes(part, t, blk, mc):
                pe.wait_ge(pm_norm.sem, pm_norm.after(part, t, blk))
                T.wait_free(pe, part, t, f"ptm{blk}{mc}")
                for e in range(4):
                    last = tr(ps_t[:, e * P:(e + 1) * P], pm[:, blk, e, mc * P:(mc + 1) * P], ident)
                last.then_inc(T.full[0], 1)

            def mem_values(part, t):
                T.wait_read(pe, part, t, "ptm11")
                V.wait_free(pe, part, t, "pvm")
                for c in range(2):
                    for mc in range(MC):
                        for par in range(2):
                            h = 2 * c + par
                            last = mm(ps_p[par * HD:(par + 1) * HD, c * NT:(c + 1) * NT],
                                      vm[:, mc, h * HD:(h + 1) * HD], big[:, mc * 4 + par * 2 + c, :],
                                      start=(mc == 0), stop=(mc == MC - 1), skip_group_check=True)
                last.then_inc(V.full[0], 1)

            def mix(part, t, n):
                pe.wait_ge(wx_in[0], 16)
                pe.wait_ge(d_in.sem, d_in.after(part, t))
                blocks = [(o, i) for o in range(POOLC) for i in range(POOLC)
                          if o // 3 == i // 3 and abs(o - i) < 2]
                for pair in range(3):
                    b = Z.wait_free(pe, part, t, f"mix{pair}")
                    for o in (2 * pair, 2 * pair + 1):
                        ins = [i for (oo, i) in blocks if oo == o]
                        for i in ins:
                            src = pooled(i)[:, 16:UW] if n == NT else \
                                pooled(i)[:, 0:DB * US].rearrange("p (b t) -> p b t", b=DB)[:, :, 16:US]
                            out = ps_z[:, b, (o % 2) * NT:(o % 2) * NT + n]
                            if n != NT:
                                out = out.rearrange("p (b t) -> p b t", b=DB)
                            last = mm(out, mix_w[:, blocks.index((o, i)), :], src,
                                      start=(i == ins[0]), stop=(i == ins[-1]))
                    last.then_inc(Z.full[b], 1)

            def project_out(part, t, groups, n=NT):
                for g in groups:
                    by_feature(part, t, f"out{g}", gate, w_out, g, n)

            pe.wait_ge(consts, 2)
            pe.wait_ge(small_in, 16)
            square_sums(T, "pre", 0, "ss_mem", 0)
            rstd_rows("pre", 0, "rb_mem", 0)
            Z.wait_read(pe, "pre", 0, "rb_mem")
            for l in range(2):
                for g in (2 * l, 2 * l + 1):
                    pe.wait_ge(wout_in[g], 16)
                for blk in range(MC):
                    by_token("pre", 0, f"mem{l}{blk}", (xn, x_buf[:, 1])[l], blk * P, w_out, 2 * l)
            for l in range(2):
                pe.wait_ge(heads_norm.sem, heads_norm.after("pre", 0, l))
                T.wait_free(pe, "pre", 0, f"kt{l}")
                for c in range(2):
                    for mc in range(MC):
                        last = tr(ps_t[:, (c * MC + mc) * P:(c * MC + mc + 1) * P],
                                  k_mem[l][:, mc, c * P:(c + 1) * P], ident)
                last.then_inc(T.full[0], 1)
            square_sums(T, "pre", 0, "ss", 1)
            rstd_rows("pre", 0, "rb", 1)
            Z.wait_read(pe, "pre", 0, "rb")
            T.wait_read(pe, "pre", 0, "kt0")

            def q_transposes_a(part, t, n=P, blocks=NBLK):
                pe.wait_ge(heads_norm.sem, heads_norm.after(part, t))
                T.wait_free(pe, part, t, "qT")
                for c in range(2):
                    for blk in range(blocks):
                        last = tr(ps_t[:, (c * blocks + blk) * n:(c * blocks + blk + 1) * n],
                                  q_of(0)[0:n, blk * 4 + 2 * c:blk * 4 + 2 * c + 2, :].rearrange("p h d -> p (h d)"),
                                  ident[0:n, 0:n])
                last.then_inc(T.full[0], 1)

            with pe.Fori(0, TILES // 2) as it:
                for p in range(2):
                    t = it * 2 + p
                    pe.wait_ge(win_in[0], 16)
                    b = Z.wait_free(pe, "A", t, "qm")
                    for blk in range(NBLK):
                        for kc in range(KC):
                            last = mm(ps_z[:, b, blk * 256:(blk + 1) * 256], xn[:, kc, blk * P:(blk + 1) * P],
                                      w_in[:, 0, kc, :], start=(kc == 0), stop=(kc == KC - 1))
                    last.then_inc(Z.full[b], 1)
                    for i in range(3):
                        pe.wait_ge(win_in[1 + i], 16)
                        by_feature("A", t, f"u{i}", xn, w_in, 1 + i)
                    q_transposes_a("A", t)
                    T.wait_read(pe, "A", t, "qT")
                    mem_scores("A", t, 0, qT_a, 0)
                    mem_scores("A", t, 1, qT_a, 0)
                    for g in range(4, 8):
                        pe.wait_ge(win_in[g], 16)
                    by_feature("A", t, "g0", xn, w_in, 4)
                    mem_transposes("A", t, 0, 0)
                    by_feature("A", t, "g1", xn, w_in, 5, halves=(0,))
                    mem_transposes("A", t, 0, 1)
                    by_feature("A", t, "g1", xn, w_in, 5, halves=(1,))
                    mem_transposes("A", t, 1, 0)
                    by_feature("A", t, "g2", xn, w_in, 6, halves=(0,))
                    mem_transposes("A", t, 1, 1)
                    by_feature("A", t, "g2", xn, w_in, 6, halves=(1,))
                    mem_values("A", t)
                    by_feature("A", t, "gm", xn, w_in, 7)
                    mix("A", t, NT)
                    for g in range(4):
                        pe.wait_ge(wout_in[g], 32)
                    V.wait_read(pe, "A", t, "pvm")
                    Z.wait_read(pe, "A", t, "mix2")
                    project_out("A", t, (0,))
                    square_sums(T, "A", t, "ss", 0)
                    project_out("A", t, (1,))
                    rstd_rows("A", t, "rb", 0)
                    project_out("A", t, (2, 3))

            def sample_mem_scores(part, qbd, x_slot):
                b = S.wait_free(pe, part, 0, "m")
                base = 0 if part == "SA" else 1
                for n in range(DB):
                    wait_slot(pe, part, n)
                    for c in range(2):
                        last = mm(ps_s[(n % 4) * 32:(n % 4) * 32 + 32, b, 0, (n // 4) * NMEM:(n // 4 + 1) * NMEM],
                                  qbd[:, c, n, :], slot(x_slot, n)[:, c, :], start=(c == 0), stop=(c == 1),
                                  skip_group_check=True)
                    if n < DB - 1:
                        last.then_inc(slot_used.sem, 1)
                last.then_inc(S.full[b], 1)

            def sample_mem_transposes(part):
                pe.wait_ge(pm_norm.sem, pm_norm.after(part, 0))
                for mc in range(MC):
                    T.wait_free(pe, part, 0, f"pt{mc}")
                    for half in range(2):
                        last = tr(ps_t[:, half * P:(half + 1) * P], pm[:, 0, half, mc * P:(mc + 1) * P], ident)
                    last.then_inc(T.full[0], 1)

            def sample_mem_values(part, x_slot):
                T.wait_read(pe, part, 0, "pt1")
                V.wait_free(pe, part, 0, "pvm")
                for n in range(DB):
                    wait_slot(pe, part, DB + n)
                    for c in range(2):
                        cols = slice(n * 32 + c * 16, n * 32 + c * 16 + 16)
                        for mc in range(MC):
                            last = mm(ps_p[:, cols], slot(x_slot, DB + n)[:, mc, c * P:(c + 1) * P], pt_s[:, mc, cols],
                                      start=(mc == 0), stop=(mc == MC - 1), skip_group_check=True)
                    if n < DB - 1:
                        last.then_inc(slot_used.sem, 1)
                last.then_inc(V.full[0], 1)

            b = Z.wait_free(pe, "SA", 0, "qm")
            for kc in range(KC):
                last = mm(ps_z[0:NS, b, 0:256], xn[:, kc, 0:NS], w_in[:, 0, kc, :], start=(kc == 0), stop=(kc == KC - 1))
            last.then_inc(Z.full[b], 1)
            for i in range(3):
                by_feature("SA", 0, f"u{i}", xn, w_in, 1 + i, NS)
            q_transposes_a("SA", 0, NS, 1)
            T.wait_read(pe, "SA", 0, "qT")
            sample_mem_scores("SA", qbd_a, 1)
            for i in range(3):
                by_feature("SA", 0, f"g{i}", xn, w_in, 4 + i, NS)
            by_feature("SA", 0, "gm", xn, w_in, 7, NS)
            sample_mem_transposes("SA")
            sample_mem_values("SA", 1)
            mix("SA", 0, NS)
            V.wait_read(pe, "SA", 0, "pvm")
            Z.wait_read(pe, "SA", 0, "mix2")
            project_out("SA", 0, range(4), NS)
            square_sums(T, "SA", 0, "ss", 0)
            rstd_rows("SA", 0, "rb", 0)
            Z.wait_read(pe, "SA", 0, "rb")

            pe.wait_ge(mem_reload, 32)

            def folded(group):
                if group in FOLD_V:
                    pe.wait_ge(in_folded[0], FOLD_V.index(group) + 1)
                else:
                    pe.wait_ge(in_folded[1], FOLD_P.index(group) + 1)

            def q_transposes_b(part, t, blk, half, n=P):
                pe.wait_ge(heads_norm.sem, heads_norm.after(part, t, 1 + blk))
                T.wait_free(pe, part, t, f"qT{blk}{half}")
                for c in range(4):
                    h = (half * 4 + c) * 2
                    last = tr(ps_t[:, c * n:(c + 1) * n], q_of(blk)[0:n, h:h + 2, :].rearrange("p h d -> p (h d)"),
                              ident[0:n, 0:n])
                last.then_inc(T.full[0], 1)

            def window_scores(t, p, i):
                blk, gi = W6[i]
                b = S.wait_free(pe, "B", t, f"w{i}")
                own = 2 * p + blk
                for c in range(2):
                    for par in range(2):
                        rows = slice(par * HD, (par + 1) * HD)
                        ch = 2 * gi + c
                        for j, s in enumerate(((own - 1) % 4, own)):
                            at = c * 256 + j * P
                            last = mm(ps_s[:, b, par, at:at + P], qT_b[rows, ch, blk * P:(blk + 1) * P],
                                      kT[rows, ch // 3, s, :], start=True, stop=True)
                last.then_inc(S.full[b], 1)

            def window_transposes(t, i):
                pe.wait_ge(pw_norm.sem, pw_norm.after("B", t, i))
                T.wait_free(pe, "B", t, f"ptw{i}")
                for e in range(4):
                    last = tr(ps_t[:, e * P:(e + 1) * P], sw[:, i % 2, e, :], ident)
                last.then_inc(T.full[0], 1)

            def window_values(t, p, i):
                blk, gi = W6[i]
                T.wait_read(pe, "B", t, f"ptw{i}")
                V.wait_free(pe, "B", t, f"pvw{i}")
                own = 2 * p + blk
                for c in range(2):
                    for j, (s, w) in enumerate((((own - 1) % 4, ptp), (own, ptc))):
                        for par in range(2):
                            kv = 2 * ((2 * gi + c) // 3) + par
                            last = mm(ps_p[par * HD:(par + 1) * HD, c * P:(c + 1) * P],
                                      v[:, s, kv * HD:(kv + 1) * HD], w[:, par * 2 + c, :],
                                      start=(j == 0), stop=(j == 1), skip_group_check=True)
                last.then_inc(V.full[0], 1)

            with pe.Fori(0, TILES // 2) as it:
                for p in range(2):
                    t = it * 2 + p
                    pe.wait_ge(kv_folded, 2)
                    by_token("B", t, "kv0", xn, 0, w_kv, 0)
                    by_token("B", t, "kv1", xn, P, w_kv, 0)
                    for g in range(4):
                        folded(g)
                    by_token("B", t, "qa0", xn, 0, w_in, 0)
                    by_token("B", t, "qb0", xn, 0, w_in, 2)
                    pe.wait_ge(heads_norm.sem, heads_norm.after("B", t, 0))
                    T.wait_free(pe, "B", t, "kT")
                    for kp in range(2):
                        for blk in range(NBLK):
                            last = tr(ps_t[:, (kp * 2 + blk) * P:(kp * 2 + blk + 1) * P],
                                      k_tok[:, blk, 2 * kp:2 * kp + 2, :].rearrange("p h d -> p (h d)"), ident)
                    last.then_inc(T.full[0], 1)
                    by_token("B", t, "qa1", xn, P, w_in, 0)
                    q_transposes_b("B", t, 0, 0)
                    by_token("B", t, "qb1", xn, P, w_in, 2)
                    q_transposes_b("B", t, 0, 1)
                    for g in range(4, 8):
                        folded(g)
                    by_feature("B", t, "gm", xn, w_in, 7, halves=(0,))
                    T.wait_read(pe, "B", t, "qT01")
                    mem_scores("B", t, 0, qT_b, 6)
                    window_scores(t, p, 0)
                    q_transposes_b("B", t, 1, 0)
                    by_feature("B", t, "gm", xn, w_in, 7, halves=(1,))
                    T.wait_read(pe, "B", t, "qT10")
                    q_transposes_b("B", t, 1, 1)
                    window_scores(t, p, 1)
                    by_feature("B", t, "g0", xn, w_in, 4, halves=(0,))
                    T.wait_read(pe, "B", t, "qT11")
                    mem_scores("B", t, 1, qT_b, 6)
                    by_feature("B", t, "g0", xn, w_in, 4, halves=(1,))
                    window_scores(t, p, 2)
                    window_transposes(t, 0)
                    by_feature("B", t, "g1", xn, w_in, 5, halves=(0,))
                    mem_transposes("B", t, 0, 0)
                    window_values(t, p, 0)
                    window_scores(t, p, 3)
                    mem_transposes("B", t, 0, 1)
                    by_feature("B", t, "g1", xn, w_in, 5, halves=(1,))
                    window_transposes(t, 1)
                    window_scores(t, p, 4)
                    mem_transposes("B", t, 1, 0)
                    window_values(t, p, 1)
                    by_feature("B", t, "g2", xn, w_in, 6, halves=(0,))
                    mem_transposes("B", t, 1, 1)
                    window_transposes(t, 2)
                    mem_values("B", t)
                    window_values(t, p, 2)
                    window_scores(t, p, 5)
                    window_transposes(t, 3)
                    by_feature("B", t, "g2", xn, w_in, 6, halves=(1,))
                    window_values(t, p, 3)
                    window_transposes(t, 4)
                    window_values(t, p, 4)
                    window_transposes(t, 5)
                    window_values(t, p, 5)
                    for g in range(4):
                        pe.wait_ge(wout_in[g], 48)
                    V.wait_read(pe, "B", t, "pvw5")
                    project_out("B", t, (0,))
                    square_sums(Z, "B", t, "ss", 0)
                    project_out("B", t, (1,))
                    rstd_rows("B", t, "rb", 0)
                    project_out("B", t, (2, 3))

            by_token("SB", 0, "kv0", xn, 0, w_kv, 0, NS)
            by_token("SB", 0, "qa0", xn, 0, w_in, 0, NS)
            by_token("SB", 0, "qb0", xn, 0, w_in, 2, NS)
            by_feature("SB", 0, "gm", xn, w_in, 7, NS)
            for i in range(3):
                by_feature("SB", 0, f"g{i}", xn, w_in, 4 + i, NS)
            pe.wait_ge(heads_norm.sem, heads_norm.after("SB", 0, 0))
            T.wait_free(pe, "SB", 0, "kT")
            for kp in range(2):
                last = tr(ps_t[:, kp * NS:(kp + 1) * NS],
                          k_tok[0:NS, 0, 2 * kp:2 * kp + 2, :].rearrange("p h d -> p (h d)"), ident[0:NS, 0:NS])
            last.then_inc(T.full[0], 1)
            q_transposes_b("SB", 0, 0, 0, NS)
            q_transposes_b("SB", 0, 0, 1, NS)
            T.wait_read(pe, "SB", 0, "qT01")
            sample_mem_scores("SB", qbd_b, 0)
            b = S.wait_free(pe, "SB", 0, "wn")
            for n in range(DB):
                for kp in range(2):
                    last = mm(ps_s[0:96, b, 0, n * DS:(n + 1) * DS], qbd_w[:, kp, n, :],
                              kT_new[:, kp, n * DS:(n + 1) * DS], start=(kp == 0), stop=(kp == 1))
            last.then_inc(S.full[b], 1)
            b = S.wait_free(pe, "SB", 0, "wc")
            pe.wait_ge(wx_in[0], 48)
            for n in range(DB):
                for kp in range(2):
                    last = mm(ps_s[0:96, b, n // 4, (n % 4) * P:(n % 4 + 1) * P], qbd_w[:, kp, n, :],
                              kT_old[:, kp, n, :], start=(kp == 0), stop=(kp == 1))
            last.then_inc(S.full[b], 1)
            sample_mem_transposes("SB")
            sample_mem_values("SB", 0)
            pe.wait_ge(pw_norm.sem, pw_norm.after("SB", 0))
            for half in range(2):
                T.wait_free(pe, "SB", 0, f"ptw{half}")
                for n in range(4):
                    last = tr(ps_t[:, n * 96:(n + 1) * 96], sw_s[:, half * 4 + n, :], ident[0:96, 0:96])
                last.then_inc(T.full[0], 1)
            T.wait_read(pe, "SB", 0, "ptw1")
            pe.wait_ge(wx_in[1], 32)
            pe.wait_ge(vnew_in, 16 * DB)
            for kp in range(2):
                V.wait_free(pe, "SB", 0, f"pvw{kp}")
                cols = slice(kp * 48, (kp + 1) * 48)
                for n in range(DB):
                    out = ps_p[:, n * 48:(n + 1) * 48]
                    mm(out, v_old[:, n, kp * P:(kp + 1) * P], pt_old[:, n, cols], start=True, stop=False)
                    last = mm(out, v_new[:, n, kp * P:(kp + 1) * P], pt_new[:, n, cols], start=False, stop=True)
                last.then_inc(V.full[0], 1)
            V.wait_read(pe, "SB", 0, "pvw1")
            project_out("SB", 0, range(4), NS)

        @block.scalar
        def _(act):
            f = nc.scalar.activation

            def squares_x(part, t, k, xb, arrived):
                act.wait_ge(x_in[xb], arrived)
                f(big[:, :, :], x_buf[:, xb], ACT.Square).then_inc(sq_x.sem, 1)

            def squares_heads(part, t, name, n=P, cols=512):
                b = Z.wait_full(act, part, t, name)
                return f(scr[0:n, b, 0:cols], ps_z[0:n, b, 0:cols], ACT.Square)

            def squares_kv(part, t, name, v_out, n=P):
                squares_heads(part, t, name, n, 256)
                b = Z.bank(part, name)
                f(v_out, ps_z[0:n, b, 256:512], ACT.Copy).then_inc(scr_in.sem, 1)

            def tanh(part, t, name, n=NT):
                b = Z.wait_full(act, part, t, name)
                pair = [x[:, b].rearrange("p (c n) -> p c n", c=2)[:, :, 0:n] for x in (scr, ps_z)]
                f(pair[0], pair[1], ACT.Tanh, scale=0.5).then_inc(scr_in.sem, 1)

            def from_t(part, t, name, out, src=None):
                T.wait_full(act, part, t, name)
                f(out, ps_t[:, :] if src is None else src, ACT.Copy).then_inc(T.free[0], 1)

            def mem_exps(part, t, blk):
                b = S.wait_full(act, part, t, f"m{blk}")
                act.wait_ge(m_neg_in.sem, m_neg_in.after(part, t, blk))
                for e in range(4):
                    last = f(pm[:, blk, e, :], ps_s[:, b, e // 2, (e % 2) * NMEM:(e % 2 + 1) * NMEM], ACT.Exp,
                             bias=m_neg[:, blk, e:e + 1], scale=SCALE, accum_out=m_sum[:, blk, e:e + 1])
                last.then_inc(S.free[b], 1)

            def mem_weights(part, t, blk, mc):
                from_t(part, t, f"ptm{blk}{mc}", big[:, mc * 4:mc * 4 + 4, blk * P:(blk + 1) * P],
                       ps_t[:, :].rearrange("p (e n) -> p e n", e=4))

            def sample_mem(part):
                b = S.wait_full(act, part, 0, "m")
                act.wait_ge(m_neg_in.sem, m_neg_in.after(part, 0))
                for half in range(2):
                    last = f(pm[:, 0, half, :], ps_s[:, b, 0, half * NMEM:(half + 1) * NMEM], ACT.Exp,
                             bias=m_neg[:, 0, half:half + 1], scale=SCALE, accum_out=m_sum[:, 0, half:half + 1])
                last.then_inc(S.free[b], 1)

            def sample_weights(part):
                for mc in range(MC):
                    from_t(part, 0, f"pt{mc}", pt_s[:, mc, :], ps_t[:, 0:NMEM])

            def to_blocks(out, c, par, src):
                rows = slice(par * HD, (par + 1) * HD)
                h = 2 * c + par
                return f(out[rows, c, :, h * DS:(h + 1) * DS], src[rows, :].rearrange("p (b t) -> p b t", b=DB),
                         ACT.Copy)

            squares_x("pre", 0, 0, 1, 16)
            for l in range(2):
                for blk in range(MC):
                    squares_kv("pre", 0, f"mem{l}{blk}", v_mem[l][:, blk, :])
            for l in range(2):
                from_t("pre", 0, f"kt{l}", kT_mem[l], ps_t[:, :].rearrange("p (c n) -> p c n", c=2))
                if l == 0:
                    squares_x("pre", 0, 1, 0, 16)

            with act.Fori(0, TILES // 2) as it:
                for p in range(2):
                    t = it * 2 + p
                    squares_heads("A", t, "qm").then_inc(scr_in.sem, 1)
                    act.wait_ge(u_free.sem, u_free.after("A", t, -1))
                    for i in range(3):
                        b = Z.wait_full(act, "A", t, f"u{i}")
                        f(u[:, 2 * i:2 * i + 2, 16:UW], ps_z[:, b].rearrange("p (c n) -> p c n", c=2), ACT.Copy)\
                            .then_inc(Z.free[b], 1)
                    from_t("A", t, "qT", qT_a[:, :, :], ps_t[:, :].rearrange("p (c n) -> p c n", c=2))
                    mem_exps("A", t, 0)
                    mem_exps("A", t, 1)
                    tanh("A", t, "g0")
                    mem_weights("A", t, 0, 0)
                    mem_weights("A", t, 0, 1)
                    tanh("A", t, "g1")
                    mem_weights("A", t, 1, 0)
                    mem_weights("A", t, 1, 1)
                    tanh("A", t, "g2")
                    V.wait_full(act, "A", t, "pvm")
                    squares_x("A", t, 0, 1 - p, it * 16 + 32)
                    tanh("A", t, "gm")

            squares_heads("SA", 0, "qm", NS, 256).then_inc(scr_in.sem, 1)
            act.wait_ge(state_set, 1)
            for i in range(3):
                b = Z.wait_full(act, "SA", 0, f"u{i}")
                for c in range(2):
                    last = f(by_batch(u[:, 2 * i + c])[:, :, 16:US],
                             ps_z[:, b, c * NT:c * NT + NS].rearrange("p (b t) -> p b t", b=DB), ACT.Copy)
                last.then_inc(Z.free[b], 1)
            act.wait_ge(qbd_zero.sem, qbd_zero.after("SA", 0))
            T.wait_full(act, "SA", 0, "qT")
            for c in range(2):
                for par in range(2):
                    last = to_blocks(qbd_a, c, par, ps_t[:, c * NS:(c + 1) * NS])
            last.then_inc(T.free[0], 1)
            sample_mem("SA")
            for g in (*G3, "gm"):
                tanh("SA", 0, g, NS)
            sample_weights("SA")
            V.wait_full(act, "SA", 0, "pvm")
            squares_x("SA", 0, 0, 1, 16 * 6)

            def window_exps(t, n):
                act.wait_ge(w_neg_in.sem, w_neg_in.after("B", t, n))
                for e in range(4):
                    f(sw[:, n % 2, e, :], sw[:, n % 2, e, :], ACT.Exp, bias=w_neg[:, n % 2, e:e + 1], scale=SCALE,
                      accum_out=w_sum[:, n % 2, e:e + 1])
                f(w_se[:, n % 2, :], w_sd[:, n % 2, :], ACT.Exp).then_inc(w_exp.sem, 1)

            with act.Fori(0, TILES // 2) as it:
                for p in range(2):
                    t = it * 2 + p
                    for blk in range(NBLK):
                        squares_kv("B", t, f"kv{blk}", v[:, 2 * p + blk, :])
                    squares_heads("B", t, "qa0").then_inc(scr_in.sem, 1)
                    squares_heads("B", t, "qb0").then_inc(scr_in.sem, 1)
                    from_t("B", t, "kT", kT[:, :, 2 * p:2 * p + 2, :],
                           ps_t[:, :].rearrange("p (k b n) -> p k b n", k=2, b=NBLK))

                    def queries(blk, half):
                        from_t("B", t, f"qT{blk}{half}", qT_b[:, half * 4:half * 4 + 4, blk * P:(blk + 1) * P],
                               ps_t[:, :].rearrange("p (c n) -> p c n", c=4))
                    squares_heads("B", t, "qa1").then_inc(scr_in.sem, 1)
                    queries(0, 0)
                    squares_heads("B", t, "qb1").then_inc(scr_in.sem, 1)
                    queries(0, 1)
                    mem_exps("B", t, 0)
                    queries(1, 0)
                    window_exps(t, 0)
                    queries(1, 1)
                    tanh("B", t, "gm")
                    window_exps(t, 1)
                    mem_exps("B", t, 1)
                    tanh("B", t, "g0")
                    mem_weights("B", t, 0, 0)
                    window_exps(t, 2)
                    mem_weights("B", t, 0, 1)
                    tanh("B", t, "g1")
                    mem_weights("B", t, 1, 0)
                    window_exps(t, 3)
                    mem_weights("B", t, 1, 1)
                    window_exps(t, 4)
                    window_exps(t, 5)
                    tanh("B", t, "g2")
                    squares_x("B", t, 0, p, (it + 6 + p) * 16)

            squares_kv("SB", 0, "kv0", v[0:NS, 0, :], NS)
            squares_heads("SB", 0, "qa0", NS).then_inc(scr_in.sem, 1)
            squares_heads("SB", 0, "qb0", NS).then_inc(scr_in.sem, 1)
            for g in ("gm", *G3):
                tanh("SB", 0, g, NS)
            from_t("SB", 0, "kT", kT_new, ps_t[:, 0:2 * NS].rearrange("p (k t) -> p k t", k=2))
            act.wait_ge(qbd_zero.sem, qbd_zero.after("SB", 0))
            for half in range(2):
                T.wait_full(act, "SB", 0, f"qT0{half}")
                for j in range(4):
                    for par in range(2):
                        c = half * 4 + j
                        src = ps_t[:, j * NS:(j + 1) * NS]
                        if c < POOLC:
                            rows = slice(par * HD, (par + 1) * HD)
                            at = (c // 3) * 48 + par * 24 + (c % 3) * DS
                            last = f(qbd_w[rows, c // 3, :, at:at + DS],
                                     src[rows, :].rearrange("p (b t) -> p b t", b=DB), ACT.Copy)
                        else:
                            last = to_blocks(qbd_b, c - POOLC, par, src)
                last.then_inc(T.free[0], 1)
            sample_mem("SB")
            act.wait_ge(w_neg_in.sem, w_neg_in.after("SB", 0))
            for n in range(DB):
                f(sw_s[:, n, :], sw_s[:, n, :], ACT.Exp, bias=s_neg[:, n:n + 1], scale=SCALE,
                  accum_out=s_sum[:, n:n + 1])
            f(s_se, s_sd, ACT.Exp).then_inc(w_exp.sem, 1)
            sample_weights("SB")

        @block.vector
        def _(dve):
            ve = nc.vector
            own = Steps(dve, dves)

            def x_variance(ring, part, t, name):
                b = ring.wait_full(dve, part, t, name)
                src = ps_t[:, 0:2] if ring is T else ps_z[:, b, 0:2]
                ve.tensor_scalar(x_var, src, 1.0 / D, EPS, ALU.mult, ALU.add).then_inc(ring.free[b], 1)

            def diagonals(part, t, k):
                dve.wait_ge(rstd_x.sem, rstd_x.after(part, t, k))
                for blk in range(NBLK):
                    last = ve.tensor_scalar(diag[:, blk, :], ident, x_rstd[:, blk:blk + 1], None, ALU.mult)
                last.then_inc(diag_x.sem, 1)

            def normalise(part, t, name, xb, gains):
                b = Z.wait_full(dve, part, t, name)
                if gains is None:
                    row_ = ps_z[:, b, 0:NT].rearrange("p (k n) -> p k n", k=1).to_broadcast([P, KC, NT])
                    last = ve.tensor_tensor(xn[:, :, :], x_buf[:, xb], row_, ALU.mult)
                else:
                    for g, dst in gains:
                        for kc in range(KC):
                            last = ve.scalar_tensor_tensor(dst[:, kc, :], x_buf[:, xb, kc, :],
                                                           gain[:, g, kc:kc + 1], ps_z[:, b, 0:NT],
                                                           ALU.mult, ALU.mult)
                last.then_inc(Z.free[b], 1)

            def head_group(part, t, name, k, ss, parts, n=P):
                dve.wait_ge(scr_in.sem, scr_in.after(part, t, k))
                b = Z.bank(part, name)
                heads = ss.shape[1]
                own(ve.tensor_reduce(ss, scr[0:n, b, 0:heads * HD].rearrange("p (h d) -> p h d", h=heads),
                                     AX.X, ALU.add))
                for dst, at, h, r in parts:
                    last = ve.tensor_tensor(dst, ps_z[0:n, b, at:at + h * HD].rearrange("p (h d) -> p h d", h=h),
                                            row(r, h, n), ALU.mult)
                last.then_inc(Z.free[b], 1)

            def variance(ss, rstd):
                own.wait()
                return ve.tensor_scalar(rstd, ss, 1.0 / HD, EPS, ALU.mult, ALU.add)

            def rotate(x, heads, cos, sin, n=P):
                def along(a):
                    w = a.shape[1]
                    return a.rearrange("p (h d) -> p h d", h=1).to_broadcast([n, heads, w])
                half = 8
                own.wait()
                ve.tensor_tensor(rot[0:n, 0:heads, 0:half], x[:, :, half:16], along(sin[:, 0:half]), ALU.mult)
                own(ve.tensor_tensor(rot[0:n, 0:heads, half:16], x[:, :, 0:half], along(sin[:, half:16]), ALU.mult))
                own.wait()
                own(ve.tensor_tensor(x[:, :, 0:16], x[:, :, 0:16], along(cos), ALU.mult))
                own.wait()
                return ve.tensor_tensor(x[:, :, 0:16], x[:, :, 0:16], rot[0:n, 0:heads, :], ALU.add)

            def mem_max(part, t, blk):
                b = S.wait_full(dve, part, t, f"m{blk}")
                own(ve.tensor_reduce(m_max[:, blk, :].rearrange("p (r c) -> p r c", r=2),
                                     ps_s[:, b].rearrange("p r (c m) -> p r c m", c=2), AX.X, ALU.max))
                own.wait()
                ve.tensor_scalar(m_neg[:, blk, :], m_max[:, blk, :], -SCALE, None, ALU.mult)\
                    .then_inc(m_neg_in.sem, 1)

            def mem_inverse(part, t, blk):
                S.wait_read(dve, part, t, f"m{blk}")
                ve.reciprocal(m_inv[:, blk, :], m_sum[:, blk, :]).then_inc(m_inv_in.sem, 1)

            def silu(part, t, name, k, c, n=NT):
                dve.wait_ge(scr_in.sem, scr_in.after(part, t, k))
                b = Z.bank(part, name)
                pair = [x[:, b].rearrange("p (c n) -> p c n", c=2)[:, :, 0:n] for x in (scr, ps_z)]
                ve.scalar_tensor_tensor(gate[:, c:c + 2, 0:n], pair[0], 1.0, pair[1], ALU.add, ALU.mult)\
                    .then_inc(Z.free[b], 1)

            def mem_gated(part, t):
                V.wait_full(dve, part, t, "pvm")
                Z.wait_read(dve, part, t, "gm")
                ve.scalar_tensor_tensor(gate[:, 6:8, :], ps_p[:, :].rearrange("p (c n) -> p c n", c=2), 0.5,
                                        gate[:, 6:8, :], ALU.mult, ALU.mult).then_inc(V.free[0], 1)

            def mix_gated(part, t, n=NT):
                Z.wait_read(dve, part, t, "g1")
                Z.wait_read(dve, part, t, "g2")
                for i in range(3):
                    b = Z.wait_full(dve, part, t, f"mix{i}")
                    for c in (2 * i, 2 * i + 1):
                        src = ps_z[:, b, (c % 2) * NT:(c % 2) * NT + n]
                        last = ve.scalar_tensor_tensor(gate[:, c, 0:n], src, half_scale[:, c:c + 1],
                                                       gate[:, c, 0:n], ALU.mult, ALU.mult)
                    last.then_inc(Z.free[b], 1)

            def add_outputs(part, t, xb, groups, n=NT):
                for g in groups:
                    b = Z.wait_full(dve, part, t, f"out{g}")
                    x = x_buf[:, xb, 2 * g:2 * g + 2, 0:n]
                    ve.tensor_tensor(x, x, ps_z[:, b].rearrange("p (c n) -> p c n", c=2)[:, :, 0:n], ALU.add)\
                        .then_inc(Z.free[b], 1)

            ve.memset(tiny[:, 56:57], 0.0).then_inc(S.free[0], 1)
            ve.memset(tiny[:, 57:58], 0.0).then_inc(S.free[1], 1)
            ve.memset(tiny[:, 58:59], 0.0).then_inc(V.free[0], 1)
            ve.memset(u[:, :, :], 0.0).then_inc(u_free.sem, 1)
            dve.wait_ge(small_in, 16)
            own(ve.tensor_scalar(half_scale, pscale, 0.5, None, ALU.mult))

            x_variance(T, "pre", 0, "ss_mem")
            diagonals("pre", 0, 0)
            normalise("pre", 0, "rb_mem", 1, ((3, xn), (4, x_buf[:, 1])))
            for l in range(2):
                if l:
                    dve.wait_ge(heads_var.sem, heads_var.after("pre", 0, 0))
                for blk in range(MC):
                    head_group("pre", 0, f"mem{l}{blk}", 2 * l + blk, k_ss[:, blk * 4:(blk + 1) * 4],
                               [(k_mem[l][:, blk, :].rearrange("p (h d) -> p h d", h=4), 0, 4, ROW_MEMK + l)])
                variance(k_ss, k_rstds[l]).then_inc(heads_var.sem, 1)
            x_variance(T, "pre", 0, "ss")
            diagonals("pre", 0, 1)
            normalise("pre", 0, "rb", 0, ((0, xn),))
            dve.wait_ge(outputs, 4 * 16)
            dve.wait_ge(x_stored.sem, x_stored.after("pre", 0))

            def window_differences(t):
                dve.wait_ge(win_sums.sem, win_sums.after("A", t))
                own(ve.tensor_tensor(win_a[:, 0:4:3, 16:32], win_a[:, 0:4:3, 16:32], corr[:, 0:4:3, :], ALU.mult))
                own(ve.tensor_tensor(win_b[:, 1:6, 16:32], win_b[:, 1:6, 16:32], corr[:, 1:6, :], ALU.mult))
                own.wait()
                own(ve.memset(corr, 1.0))
                for c in range(POOLC):
                    last = ve.scalar_tensor_tensor(pooled(c)[:, 16:UW], pooled(c)[:, 16:UW], invw[:, c:c + 1],
                                                   u[:, c, 16:UW], ALU.mult, ALU.subtract)
                last.then_inc(d_in.sem, 1)
                dve.wait_ge(d_in.sem, d_in.after("A", t))
                ve.tensor_copy(u[:, :, 0:16], u[:, :, NT:UW]).then_inc(u_free.sem, 1)

            own.loop(6)
            with dve.Fori(0, TILES // 2) as it:
                for p in range(2):
                    t = it * 2 + p
                    own.tile(t)
                    head_group("A", t, "qm", 0, q_ss[:, 0:8], [(q_of(0)[:, 0:8, :], 0, 8, ROW_MEMQ)])
                    variance(q_ss[:, 0:8], q_rstds[0][:, 0:8]).then_inc(heads_var.sem, 1)
                    for blk in range(NBLK):
                        mem_max("A", t, blk)
                    for blk in range(NBLK):
                        mem_inverse("A", t, blk)
                    silu("A", t, "g0", 1, 0)
                    silu("A", t, "g1", 2, 2)
                    window_differences(t)
                    silu("A", t, "g2", 3, 4)
                    silu("A", t, "gm", 4, 6)
                    mem_gated("A", t)
                    mix_gated("A", t)
                    add_outputs("A", t, p, (0,))
                    x_variance(T, "A", t, "ss")
                    diagonals("A", t, 0)
                    add_outputs("A", t, p, (1,))
                    normalise("A", t, "rb", 1 - p, ((0, xn),))
                    add_outputs("A", t, p, (2, 3))
            own.end_loop(TILES)

            def sample_mem_max(part):
                b = S.wait_full(dve, part, 0, "m")
                own(ve.tensor_reduce(m_max[:, 0, 0:2], ps_s[:, b, 0].rearrange("p (c m) -> p c m", c=2),
                                     AX.X, ALU.max))
                own.wait()
                ve.tensor_scalar(m_neg[:, 0, 0:2], m_max[:, 0, 0:2], -SCALE, None, ALU.mult)\
                    .then_inc(m_neg_in.sem, 1)

            def sample_mem_inverse(part):
                S.wait_read(dve, part, 0, "m")
                ve.reciprocal(m_inv[:, 0, 0:2], m_sum[:, 0, 0:2]).then_inc(m_inv_in.sem, 1)

            def sample_mem_gated(part):
                V.wait_full(dve, part, 0, "pvm")
                Z.wait_read(dve, part, 0, "gm")
                values = ps_p[:, 0:NMEM].rearrange("p (b c r t) -> p b c r t", b=DB, c=2, r=2)
                for par in range(2):
                    rows = slice(par * HD, (par + 1) * HD)
                    for c in range(2):
                        g = gate[rows, 6 + c, 0:NS].rearrange("p (b t) -> p b t", b=DB)
                        last = ve.scalar_tensor_tensor(g, values[rows, :, c, par, :], 0.5, g, ALU.mult, ALU.mult)
                last.then_inc(V.free[0], 1)

            dve.wait_ge(state_in, 16)
            dve.wait_ge(state_out, 16)
            for c in range(POOLC):
                last = ve.tensor_copy(by_batch(u[:, c])[:, :, 1:16], state_tmp[:, c])
            last.then_inc(state_set, 1)
            head_group("SA", 0, "qm", 0, q_ss[0:NS, 0:4], [(q_of(0)[0:NS, 0:4, :], 0, 4, ROW_MEMQ)], NS)
            variance(q_ss[0:NS, 0:4], q_rstds[0][0:NS, 0:4]).then_inc(heads_var.sem, 1)
            ve.memset(qbd_a, 0.0).then_inc(qbd_zero.sem, 1)
            Z.wait_read(dve, "SA", 0, "u2")
            Z.wait_read(dve, "SA", 0, "u1")
            for c in range(POOLC):
                last = ve.tensor_copy(state_tmp[:, c], by_batch(u[:, c])[:, :, US - PAD:US])
            last.then_inc(pool_out, 1)
            sample_mem_max("SA")
            sample_mem_inverse("SA")
            silu("SA", 0, "g0", 1, 0, NS)
            silu("SA", 0, "g1", 2, 2, NS)
            dve.wait_ge(win_sums.sem, win_sums.after("SA", 0))
            for c in range(POOLC):
                w_, u_ = (by_batch(x)[:, :, 16:US] for x in (pooled(c), u[:, c]))
                last = ve.scalar_tensor_tensor(w_, w_, invw[:, c:c + 1], u_, ALU.mult, ALU.subtract)
            last.then_inc(d_in.sem, 1)
            silu("SA", 0, "g2", 3, 4, NS)
            silu("SA", 0, "gm", 4, 6, NS)
            sample_mem_gated("SA")
            mix_gated("SA", 0, NS)
            add_outputs("SA", 0, 0, range(4), NS)
            dve.wait_ge(wx_in[0], 32)
            dve.wait_ge(wx_in[1], 16)

            def fold(w, g):
                return ve.tensor_tensor(w, w, gain[:, g, :].rearrange("p (k n) -> p k n", n=1)
                                        .to_broadcast([P, KC, 256]), ALU.mult)

            x_variance(T, "SA", 0, "ss")
            for g in range(2):
                fold(w_kv[:, g], 2).then_inc(kv_folded, 1)
            diagonals("SA", 0, 0)
            normalise("SA", 0, "rb", 1, None)
            for g in FOLD_V:
                dve.wait_ge(win_in[g], 32)
                fold(w_in[:, g], 1).then_inc(in_folded[0], 1)
            own(ve.memset(kT[:, :, 3, :], 0.0))
            own(ve.memset(v[:, 3, :], 0.0))
            own.wait()
            dve.wait_ge(state_out, 32)

            def k_heads(part, t, blk, at, n=P):
                head_group(part, t, f"kv{blk}", blk, k_ss[0:n, blk * 4:(blk + 1) * 4],
                           [(k_tok[0:n, blk], 0, 4, ROW_K)], n)

            def q_heads(part, t, blk, cos, sin, n=P):
                k = (2 if part == "B" else 1) + 2 * blk
                q = q_of(blk)[0:n]
                dve.wait_ge(heads_var.sem, heads_var.after(part, t, blk))
                head_group(part, t, f"qa{blk}", k, q_ss[0:n, 0:8], [(q[:, 0:8], 0, 8, ROW_Q)], n)
                head_group(part, t, f"qb{blk}", k + 1, q_ss[0:n, 8:16],
                           [(q[:, 8:12], 0, 4, ROW_Q), (q[:, 12:16], 4 * HD, 4, ROW_MEMQ + 1)], n)
                own(variance(q_ss[0:n], q_rstds[blk][0:n]))
                Z.wait_read(dve, part, t, f"qb{blk}")
                Z.wait_read(dve, part, t, f"qa{blk}")
                rotate(q[:, 0:12], 12, cos, sin, n).then_inc(heads_var.sem, 1)

            def window_front(t, i):
                blk, gi = W6[i]
                b = S.wait_full(dve, "B", t, f"w{i}")
                prev, n = ("prev_now", "prev_hi")[blk], i % 2
                scores = ps_s[:, b].rearrange("p r (c j n) -> p r c j n", c=2, j=2)

                def across(a):
                    return a.rearrange("p (r c n) -> p r c n", r=1, c=1).to_broadcast([P, 2, 2, BLK])

                def heads(a):
                    return a.rearrange("p (r c) n -> p r c n", r=2)
                own(ve.tensor_tensor(heads(lo[:, :, :]), scores[:, :, :, 1, :], across(sm("cur_hi")), ALU.min))
                ve.tensor_tensor(heads(sw[:, n]), scores[:, :, :, 0, :], across(sm(prev)), ALU.min)\
                    .then_inc(S.free[b], 1)
                S.wait_read(dve, "B", t, f"w{i}")
                own(ve.tensor_tensor(sw[:, n], sw[:, n], lo[:, :, :], ALU.max))
                own.wait()
                own(ve.tensor_reduce(w_max[:, n, :], sw[:, n], AX.X, ALU.max))
                own.wait()
                sinks = sm("sink")[:, gi * 4:gi * 4 + 4]
                own(ve.scalar_tensor_tensor(w_max[:, n, :], w_max[:, n, :], SCALE, sinks, ALU.mult, ALU.max))
                own.wait()
                ve.tensor_tensor(w_sd[:, n, :], sinks, w_max[:, n, :], ALU.subtract)
                ve.tensor_scalar(w_neg[:, n, :], w_max[:, n, :], -1.0, None, ALU.mult).then_inc(w_neg_in.sem, 1)
                if i == 4:
                    own(ve.tensor_copy(sm("prev_now"), sm("prev_hi")))
                    own.wait()

            def window_back(t, n):
                i = n % 2
                dve.wait_ge(w_exp.sem, w_exp.after("B", t, n))
                own(ve.tensor_tensor(w_sum[:, i, :], w_sum[:, i, :], w_se[:, i, :], ALU.add))
                own.wait()
                ve.reciprocal(w_inv[:, i, :], w_sum[:, i, :]).then_inc(w_inv_in.sem, 1)

            def window_weights(t, n):
                T.wait_full(dve, "B", t, f"ptw{n}")
                src = ps_t[:, :].rearrange("p (e n) -> p e n", e=4)
                for dst, mask in ((ptc, "curT"), (ptp, "prevT")):
                    m = sm(mask).rearrange("p (e n) -> p e n", e=1).to_broadcast([P, 4, BLK])
                    last = ve.tensor_tensor(dst, src, m, ALU.mult)
                last.then_inc(T.free[0], 1)

            def window_gated(t, n):
                blk, gi = W6[n]
                V.wait_full(dve, "B", t, f"pvw{n}")
                if blk == 0:
                    Z.wait_read(dve, "B", t, f"g{gi}")
                g = gate[:, 2 * gi:2 * gi + 2, blk * P:(blk + 1) * P]
                ve.scalar_tensor_tensor(g, ps_p[:, 0:2 * P].rearrange("p (c n) -> p c n", c=2), 0.5, g,
                                        ALU.mult, ALU.mult).then_inc(V.free[0], 1)

            own.loop(NBLK * (4 + 5) + 2 + 6 * 5 + 1)
            with dve.Fori(0, TILES // 2) as it:
                for p in range(2):
                    t = it * 2 + p
                    own.tile(t)

                    def angles(name, blk):
                        return sm(name)[:, bass.ds((t * NBLK + blk) * 16, 16)]
                    for blk in range(NBLK):
                        k_heads("B", t, blk, None)
                        Z.wait_read(dve, "B", t, f"kv{blk}")
                        own(rotate(k_tok[:, blk], 4, angles("cos", blk), angles("sin", blk)))
                    variance(k_ss, k_rstds[0]).then_inc(heads_var.sem, 1)
                    for blk in range(NBLK):
                        q_heads("B", t, blk, angles("cos", blk), angles("sin", blk))
                    mem_max("B", t, 0)
                    window_front(t, 0)
                    mem_inverse("B", t, 0)
                    silu("B", t, "gm", 6, 6)
                    window_back(t, 0)
                    window_front(t, 1)
                    mem_max("B", t, 1)
                    window_back(t, 1)
                    silu("B", t, "g0", 7, 0)
                    mem_inverse("B", t, 1)
                    window_weights(t, 0)
                    window_front(t, 2)
                    window_gated(t, 0)
                    window_back(t, 2)
                    window_weights(t, 1)
                    silu("B", t, "g1", 8, 2)
                    window_front(t, 3)
                    window_gated(t, 1)
                    window_back(t, 3)
                    window_weights(t, 2)
                    window_front(t, 4)
                    mem_gated("B", t)
                    window_gated(t, 2)
                    window_weights(t, 3)
                    window_back(t, 4)
                    window_front(t, 5)
                    silu("B", t, "g2", 9, 4)
                    window_gated(t, 3)
                    window_weights(t, 4)
                    window_back(t, 5)
                    window_gated(t, 4)
                    window_weights(t, 5)
                    window_gated(t, 5)
                    add_outputs("B", t, 1 - p, (0,))
                    x_variance(Z, "B", t, "ss")
                    diagonals("B", t, 0)
                    add_outputs("B", t, 1 - p, (1,))
                    normalise("B", t, "rb", p, None)
                    add_outputs("B", t, 1 - p, (2, 3))
            own.end_loop(TILES)

            k_heads("SB", 0, 0, None, NS)
            Z.wait_read(dve, "SB", 0, "kv0")
            own(rotate(k_tok[0:NS, 0], 4, sm("cos_s")[0:NS], sm("sin_s")[0:NS], NS))
            variance(k_ss[0:NS, 0:4], k_rstds[0][0:NS, 0:4]).then_inc(heads_var.sem, 1)
            q_heads("SB", 0, 0, sm("cos_s")[0:NS], sm("sin_s")[0:NS], NS)
            ve.memset(w_flat[:, 0:2048], 0.0).then_inc(qbd_zero.sem, 1)
            silu("SB", 0, "gm", 3, 6, NS)
            for i in range(3):
                silu("SB", 0, f"g{i}", 4 + i, 2 * i, NS)
            sample_mem_max("SB")
            sample_mem_inverse("SB")
            b = S.wait_full(dve, "SB", 0, "wn")
            new_hi, old_hi = (sm(x)[0:96].rearrange("p (b t) -> p b t", b=1).to_broadcast([96, DB, DS])
                              for x in ("new_hi", "old_hi"))
            ve.tensor_tensor(lo_s, ps_s[0:96, b, 0, 0:NS].rearrange("p (b t) -> p b t", b=DB), new_hi, ALU.min)\
                .then_inc(S.free[b], 1)
            b = S.wait_full(dve, "SB", 0, "wc")
            ve.tensor_copy(sw_s.rearrange("p (r b) t -> p r (b t)", r=2), ps_s[0:96, b]).then_inc(S.free[b], 1)
            S.wait_read(dve, "SB", 0, "wc")
            S.wait_read(dve, "SB", 0, "wn")
            first = sw_s[:, :, 0:DS]
            own(ve.tensor_tensor(first, first, old_hi, ALU.min))
            own.wait()
            own(ve.tensor_tensor(first, first, lo_s, ALU.max))
            own.wait()
            own(ve.tensor_reduce(s_max, sw_s, AX.X, ALU.max))
            own.wait()
            sink = sm("sinkcol")[0:96]
            own(ve.tensor_scalar(s_max, s_max, SCALE, sink, ALU.mult, ALU.max))
            own.wait()
            ve.tensor_scalar(s_sd, s_max, -1.0, sink, ALU.mult, ALU.add)
            ve.tensor_scalar(s_neg, s_max, -1.0, None, ALU.mult).then_inc(w_neg_in.sem, 1)
            sample_mem_gated("SB")
            dve.wait_ge(w_exp.sem, w_exp.after("SB", 0))
            own(ve.tensor_tensor(s_sum, s_sum, s_se, ALU.add))
            own.wait()
            ve.reciprocal(s_inv, s_sum).then_inc(w_inv_in.sem, 1)
            for half in range(2):
                T.wait_full(dve, "SB", 0, f"ptw{half}")
                some = slice(half * 4, half * 4 + 4)
                for dst, name, rows in ((pt_old, "oldT", P), (pt_new, "newT", DS)):
                    m = sm(name)[0:rows].rearrange("p (b n) -> p b n", b=1).to_broadcast([rows, 4, 96])
                    last = ve.tensor_tensor(dst[:, some, :], ps_t[0:rows, 0:384].rearrange("p (b n) -> p b n", b=4),
                                            m, ALU.mult)
                last.then_inc(T.free[0], 1)
            for kp in range(2):
                V.wait_full(dve, "SB", 0, f"pvw{kp}")
                values = ps_p[:, 0:384].rearrange("p (b n) -> p b n", b=DB)
                for par in range(2):
                    rows = slice(par * HD, (par + 1) * HD)
                    for g in range(3):
                        at = par * 24 + g * DS
                        x = gate[rows, 3 * kp + g, 0:NS].rearrange("p (b t) -> p b t", b=DB)
                        last = ve.scalar_tensor_tensor(x, values[rows, :, at:at + DS], 0.5, x, ALU.mult, ALU.mult)
                last.then_inc(V.free[0], 1)
            add_outputs("SB", 0, 1, range(4), NS)

        @block.gpsimd
        def _(pool):
            tt = nc.gpsimd.tensor_tensor
            own = Steps(pool, pools)

            def rsqrt(out, x):
                n, w = x.shape
                return tt(out, x, power[0:n, 0:w], ALU.pow)

            def sums(part, t, k):
                pool.wait_ge(sq_x.sem, sq_x.after(part, t, k))
                own(tt(big[:, 0:4], big[:, 0:4], big[:, 4:8], ALU.add))
                own.wait()
                own(tt(big[:, 0:2], big[:, 0:2], big[:, 2:4], ALU.add))
                own.wait()
                tt(big[:, 0], big[:, 0], big[:, 1], ALU.add).then_inc(sums_x.sem, 1)

            def rstd(ring, part, t, name):
                ring.wait_read(pool, part, t, name)
                rsqrt(x_rstd, x_var).then_inc(rstd_x.sem, 1)

            def heads(part, t, k, r, x):
                pool.wait_ge(heads_var.sem, heads_var.after(part, t, k))
                own(rsqrt(r, r))
                own.wait()
                n, h, d = x.shape
                tt(x, x, r.rearrange("p (h d) -> p h d", d=1).to_broadcast([n, h, d]), ALU.mult)\
                    .then_inc(heads_norm.sem, 1)

            def mem_norm(part, t, blk):
                pool.wait_ge(m_inv_in.sem, m_inv_in.after(part, t, blk))
                r = m_inv[:, blk, :].rearrange("p (e n) -> p e n", n=1).to_broadcast([P, 4, NMEM])
                tt(pm[:, blk], pm[:, blk], r, ALU.mult).then_inc(pm_norm.sem, 1)

            def sample_mem_norm(part):
                pool.wait_ge(m_inv_in.sem, m_inv_in.after(part, 0))
                r = m_inv[:, 0, 0:2].rearrange("p (e n) -> p e n", n=1).to_broadcast([P, 2, NMEM])
                tt(pm[:, 0, 0:2], pm[:, 0, 0:2], r, ALU.mult).then_inc(pm_norm.sem, 1)

            def windows(u_, a, b_, n):
                own(tt(a(slice(0, 6))[..., 2:n], u_[..., 2:n], u_[..., 1:n - 1], ALU.add))
                own.wait()
                own(tt(b_(slice(1, 6))[..., 4:n], a(slice(1, 6))[..., 4:n], a(slice(1, 6))[..., 2:n - 2], ALU.add))
                own.wait()
                own(tt(a(slice(3, 6))[..., 8:n], b_(slice(3, 6))[..., 8:n], b_(slice(3, 6))[..., 4:n - 4], ALU.add))
                own.wait()
                own(tt(b_(slice(4, 6))[..., 16:n], a(slice(4, 6))[..., 16:n], a(slice(4, 6))[..., 8:n - 8], ALU.add))
                own.wait()

            nc.gpsimd.memset(ones[:, :], 1.0).then_inc(consts, 1)
            nc.gpsimd.memset(power, -0.5).then_inc(consts, 1)
            pool.wait_ge(consts, 2)
            sums("pre", 0, 0)
            rstd(T, "pre", 0, "ss_mem")
            for l in range(2):
                heads("pre", 0, l, k_rstds[l], quarters[l].rearrange("p b (h d) -> p (b h) d", d=HD))
            sums("pre", 0, 1)
            rstd(T, "pre", 0, "ss")

            own.loop(8)
            with pool.Fori(0, TILES // 2) as it:
                for p in range(2):
                    t = it * 2 + p
                    own.tile(t)
                    heads("A", t, 0, q_rstds[0][:, 0:8], q_of(0)[:, 0:8, :])
                    Z.wait_read(pool, "A", t, "u2")
                    Z.wait_read(pool, "A", t, "u1")
                    own(tt(win_a[:, 0:6, 2:UW], u[:, :, 2:UW], u[:, :, 1:UW - 1], ALU.add))
                    own.wait()
                    own(tt(win_b[:, 1:6, 4:UW], win_a[:, 1:6, 4:UW], win_a[:, 1:6, 2:UW - 2], ALU.add))
                    mem_norm("A", t, 0)
                    mem_norm("A", t, 1)
                    own.wait()
                    own(tt(win_a[:, 3:6, 8:UW], win_b[:, 3:6, 8:UW], win_b[:, 3:6, 4:UW - 4], ALU.add))
                    own(tt(win_b[0:HD, 1, 16:UW], win_a[0:HD, 1, 16:UW], ones[0:HD, 0:1].to_broadcast([HD, NT]), ALU.mult))
                    own.wait()
                    own(tt(win_b[:, 4:6, 16:UW], win_a[:, 4:6, 16:UW], win_a[:, 4:6, 8:UW - 8], ALU.add))
                    own.wait()
                    tt(win_b[0:HD, 4, 16:UW], win_a[0:HD, 4, 16:UW], ones[0:HD, 0:1].to_broadcast([HD, NT]), ALU.mult).then_inc(win_sums.sem, 1)
                    sums("A", t, 0)
                    rstd(T, "A", t, "ss")
            own.end_loop(TILES)

            heads("SA", 0, 0, q_rstds[0][0:NS, 0:4], q_of(0)[0:NS, 0:4, :])
            Z.wait_read(pool, "SA", 0, "u2")
            Z.wait_read(pool, "SA", 0, "u1")
            pool.wait_ge(state_set, 1)

            def b4(x, c):
                return by_batch(x[:, c])
            for dst, src, chunks, w in ((win_a, u, range(0, 6), 2), (win_b, win_a, range(1, 6), 4),
                                        (win_a, win_b, range(3, 6), 8), (win_b, win_a, range(4, 6), 16)):
                for c in chunks:
                    s_ = b4(src, c)
                    own(tt(b4(dst, c)[:, :, w:US], s_[:, :, w:US], s_[:, :, w - w // 2:US - w // 2], ALU.add))
                own.wait()
            for c in (1, 4):
                last = nc.gpsimd.tensor_copy(b4(win_b, c)[0:HD, :, 16:US], b4(win_a, c)[0:HD, :, 16:US])
            last.then_inc(win_sums.sem, 1)
            sample_mem_norm("SA")
            sums("SA", 0, 0)
            rstd(T, "SA", 0, "ss")
            for g in FOLD_P:
                pool.wait_ge(win_in[g], 32)
                tt(w_in[:, g], w_in[:, g], gain[:, 1, :].rearrange("p (k n) -> p k n", n=1)
                   .to_broadcast([P, KC, 256]), ALU.mult).then_inc(in_folded[1], 1)

            def window_norm(t, n):
                i = n % 2
                pool.wait_ge(w_inv_in.sem, w_inv_in.after("B", t, n))
                r = w_inv[:, i, :].rearrange("p (e n) -> p e n", n=1).to_broadcast([P, 4, BLK])
                tt(sw[:, i], sw[:, i], r, ALU.mult).then_inc(pw_norm.sem, 1)

            own.loop(5)
            with pool.Fori(0, TILES // 2) as it:
                for p in range(2):
                    t = it * 2 + p
                    own.tile(t)
                    heads("B", t, 0, k_rstds[0], k_tok[:, :, :, :].rearrange("p b h d -> p (b h) d"))
                    heads("B", t, 1, q_rstds[0], q_of(0))
                    heads("B", t, 2, q_rstds[1], q_of(1))
                    mem_norm("B", t, 0)
                    window_norm(t, 0)
                    window_norm(t, 1)
                    mem_norm("B", t, 1)
                    for i in range(2, 6):
                        window_norm(t, i)
                    sums("B", t, 0)
                    rstd(Z, "B", t, "ss")
            own.end_loop(TILES)

            heads("SB", 0, 0, k_rstds[0][0:NS, 0:4], k_tok[0:NS, 0])
            heads("SB", 0, 1, q_rstds[0][0:NS, :], q_of(0)[0:NS])
            sample_mem_norm("SB")
            pool.wait_ge(w_inv_in.sem, w_inv_in.after("SB", 0))
            tt(sw_s, sw_s, s_inv.rearrange("p (b n) -> p b n", n=1).to_broadcast([96, DB, P]), ALU.mult)\
                .then_inc(pw_norm.sem, 1)


def _feature_major(w):
    k, n = w.shape
    return w.reshape(k // P, P, n).transpose(1, 0, 2)


def _column_groups(w):
    return np.stack([_feature_major(w[:, g * 256:(g + 1) * 256]) for g in range(w.shape[1] // 256)])


def _tables():
    c = {}
    i = np.arange(P)
    c["ident"] = np.eye(P)
    c["cur_hi"] = np.where(i[None, :] <= i[:, None], BIG, -BIG)
    c["prev_hi"] = -c["cur_hi"]
    c["prev_now"] = np.full((P, P), -BIG)
    c["curT"] = (i[:, None] <= i[None, :]) * 1.0
    c["prevT"] = 1.0 - c["curT"]
    t = np.arange(P) % DS
    j = np.arange(DS)
    c["new_hi"] = np.where(j[None, :] <= t[:, None], BIG, -BIG)
    c["old_hi"] = -c["new_hi"]
    tr = np.arange(96) % DS
    c["oldT"] = (i[:, None] > tr[None, :]) * 1.0
    c["newT"] = (i[:, None] <= tr[None, :]) * 1.0
    win = np.repeat(np.array(WINDOWS), 192)
    win = win.reshape(POOLC, P).T
    c["invw"] = 1.0 / win
    c["corr"] = win[:, :, None] / np.minimum(np.arange(16)[None, None, :] + 1, win[:, :, None])
    inv = np.float32(500000.0) ** (-np.arange(8, dtype=np.float32) * np.float32(2.0) / np.float32(16))
    for suffix, pos in (("", np.arange(SEQ).reshape(16, P)), ("_s", (SEQ + np.arange(P) % DS).reshape(1, P))):
        ang = (pos.astype(np.float32)[..., None] * inv.astype(np.float32)).astype(np.float32)
        cos, sin = np.cos(ang), np.sin(ang)
        c["cos" + suffix] = np.concatenate([cos, cos], -1).transpose(1, 0, 2)
        c["sin" + suffix] = np.concatenate([-sin, sin], -1).transpose(1, 0, 2)
    return c


def kernel(x_prompt, x_sample, state_pool, cache_swa_k, cache_swa_v, cache_mem_k, cache_mem_v, mem_prompt,
           norm_a, w_in_a, pool_mix_w, pool_scale, w_out_a, kv_norm, w_kv, k_norm,
           norm_b, w_in_b, q_norm, sinks, w_out_b, mem_norm, w_mem_kv, mem_q_norm, mem_k_norm):
    import concourse.bacc as _bacc
    from concourse import mybir as _mybir
    from concourse.bass_utils import run_bass_kernel_spmd as _run

    f = np.float32
    (x_prompt, x_sample, state_pool, cache_swa_k, cache_swa_v, cache_mem_k, cache_mem_v, mem_prompt,
     norm_a, w_in_a, pool_mix_w, pool_scale, w_out_a, kv_norm, w_kv, k_norm,
     norm_b, w_in_b, q_norm, sinks, w_out_b, mem_norm, w_mem_kv, mem_q_norm, mem_k_norm) = (
        np.asarray(a) for a in (
            x_prompt, x_sample, state_pool, cache_swa_k, cache_swa_v, cache_mem_k, cache_mem_v, mem_prompt,
            norm_a, w_in_a, pool_mix_w, pool_scale, w_out_a, kv_norm, w_kv, k_norm,
            norm_b, w_in_b, q_norm, sinks, w_out_b, mem_norm, w_mem_kv, mem_q_norm, mem_k_norm))
    W = 768

    order = [(2 * (c // 3) + par) * 3 + c % 3 for c in range(POOLC) for par in range(2)]
    by_head = np.concatenate([np.arange(h * HD, (h + 1) * HD) for h in order])

    arrays = {}
    x = np.zeros((TILES + 1, P, KC, NT), f)
    x[:TILES] = x_prompt[0].reshape(TILES, NT, KC, P).transpose(0, 3, 2, 1)
    x[TILES, :, :, :NS] = x_sample.reshape(NS, KC, P).transpose(2, 1, 0)
    arrays["x"] = x
    arrays["memx"] = _feature_major(mem_prompt[0].T)
    arrays["w_mem"] = np.concatenate([_column_groups(w_mem_kv[l]) for l in range(2)])

    a = w_in_a[0]
    arrays["w_in_a"] = _column_groups(np.concatenate([a[:, 2 * W:2 * W + 256], a[:, :2 * W], a[:, 2 * W + 256:]], 1))
    b = w_in_b[0]
    arrays["w_in_b"] = _column_groups(np.concatenate(
        [b[:, :W][:, by_head], b[:, 2 * W:2 * W + 256], b[:, W:2 * W][:, by_head], b[:, 2 * W + 256:]], 1))
    arrays["w_kv"] = _column_groups(w_kv)
    arrays["w_out_a"] = _column_groups(w_out_a[0])
    wo = w_out_b[0]
    arrays["w_out_b"] = _column_groups(np.concatenate([wo[:W][by_head], wo[W:]], 0))

    full = np.zeros((W, W), f)
    for g in range(4):
        full[g * 192:(g + 1) * 192, g * 192:(g + 1) * 192] = pool_mix_w[0, g]
    blocks = [full[i * P:(i + 1) * P, o * P:(o + 1) * P] for o in range(POOLC) for i in range(POOLC)
              if o // 3 == i // 3 and abs(o - i) < 2]
    arrays["mix"] = np.concatenate(blocks, 1)

    small = np.zeros((P, NSMALL), f)

    def put(name, value):
        at, n = SMALL[name]
        small[:, at:at + n] = np.asarray(value).reshape(P, n)

    for name, value in _tables().items():
        put(name, value)
    put("gain", np.stack([g.reshape(KC, P).T for g in (norm_a[0], norm_b[0], kv_norm, mem_norm[0], mem_norm[1])], 1))
    put("pscale", pool_scale[0].reshape(POOLC, P).T)
    rows = np.concatenate([mem_q_norm[0], mem_q_norm[1], mem_k_norm[0], mem_k_norm[1], k_norm, q_norm[0]])
    put("row", np.broadcast_to(rows, (P, 6 * HD)))
    s = sinks[0]
    put("sink", np.broadcast_to([s[order[2 * (2 * gi + c) + par]] for gi in range(3) for par in range(2)
                                 for c in range(2)], (P, QH)))
    col = np.zeros((P,), f)
    col[:96] = np.repeat(s, DS)
    put("sinkcol", col)
    arrays["small"] = small

    arrays["state"] = state_pool[0].transpose(2, 0, 1).reshape(POOLC, P, DB, PAD).transpose(1, 0, 2, 3)
    arrays["kc_tok"] = cache_swa_k.reshape(DB, BLK, 256)
    arrays["vc_tok"] = cache_swa_v.reshape(DB, BLK, 256)
    arrays["kc"] = cache_swa_k.reshape(DB, BLK, 2, P).transpose(3, 2, 0, 1)
    arrays["vc"] = cache_swa_v.reshape(DB, BLK, 256).transpose(1, 0, 2)
    arrays["mem_ks"] = cache_mem_k.reshape(2, DB, NMEM, 2, P).transpose(0, 1, 4, 3, 2)
    arrays["mem_vs"] = cache_mem_v.reshape(2, DB, MC, P, 256).transpose(0, 1, 3, 2, 4)

    outs = {"y": (TILES + 1, P, KC, NT), "pool_p": (P, POOLC, PAD), "pool_s": (P, POOLC, DB, PAD),
            "swa_k_p": (BLK, 256), "swa_v_p": (BLK, 256), "swa_k_s": (DB, BLK, 256), "swa_v_s": (DB, BLK, 256),
            "mem_k": (2, P, MC, 256), "mem_v": (2, P, MC, 256)}
    nc = _bacc.Bacc("TRN2", target_bir_lowering=False, num_devices=1)
    F = _mybir.dt.float32
    io = {}
    for name in arrays:
        arrays[name] = np.ascontiguousarray(arrays[name], dtype=f)
        io[name] = nc.dram_tensor(name, arrays[name].shape, F, kind="ExternalInput").ap()
    for name, shape in outs.items():
        io[name] = nc.dram_tensor(name, shape, F, kind="ExternalOutput").ap()
    io["x1"] = nc.dram_tensor("x1", (TILES + 1, P, KC, NT), F, kind="Internal").ap()
    io["kt1"] = nc.dram_tensor("kt1", (P, 2, NMEM), F, kind="Internal").ap()
    build(nc, io)
    r = _run(nc, [arrays], core_ids=[0]).results[0]

    y = r["y"]
    y_prompt = y[:TILES].transpose(0, 3, 2, 1).reshape(1, SEQ, D)
    y_sample = y[TILES, :, :, :NS].transpose(2, 1, 0).reshape(DB, DS, D)
    pool_p = r["pool_p"].transpose(2, 1, 0).reshape(1, 1, PAD, W)
    pool_s = r["pool_s"].transpose(2, 3, 1, 0).reshape(1, DB, PAD, W)
    mem = [r[n].transpose(0, 2, 1, 3).reshape(2, 1, NMEM, 4, HD) for n in ("mem_k", "mem_v")]
    return (y_prompt, y_sample, pool_p, pool_s,
            r["swa_k_p"].reshape(1, BLK, 4, HD), r["swa_v_p"].reshape(1, BLK, 4, HD),
            r["swa_k_s"].reshape(DB, BLK, 4, HD), r["swa_v_s"].reshape(DB, BLK, 4, HD), *mem)
```

```python
from contextlib import ExitStack

import numpy as np
import concourse.bass as bass
from concourse import mybir

F32 = mybir.dt.float32
F16 = mybir.dt.float16
BF16 = mybir.dt.bfloat16
I32 = mybir.dt.int32
ALU = mybir.AluOpType
ACT = mybir.ActivationFunctionType
AX = mybir.AxisListType

P = 128
D = 1024
KC = D // P
NT = 256
SEQ = 2048
TILES = SEQ // NT
BLK = 128
NBLK = NT // BLK
HD = 64
DB, DS = 8, 8
NS = DB * DS
NMEM = 256
MC = NMEM // P
POOLC = 6
PAD = 15
UW = 16 + NT
US = 16 + DS
QH = 12
EPS = 1e-6
BIG = 1e30
SCALE = HD ** -0.5
WINDOWS = (2, 4, 8, 16)
X_UNIT = 2.0 ** 10

SMALL = {}


def _small_layout():
    at = 0
    for name, n in (
        ("gain", 5 * KC),
        ("pscale", POOLC),
        ("row", 6 * HD),
        ("sink", QH),
        ("sinkcol", 1),
        ("invw", POOLC),
        ("corr", POOLC * 16),
        ("cos", 16 * 16),
        ("sin", 16 * 16),
        ("cos_s", 16),
        ("sin_s", 16),
        ("ident", P),
        ("cur_hi", P),
        ("prev_hi", P),
        ("prev_now", P),
        ("curT", P),
        ("prevT", P),
        ("new_hi", DS),
        ("old_hi", DS),
        ("oldT", 96),
        ("newT", 96),
    ):
        SMALL[name] = (at, n)
        at += n
    return at


NSMALL = _small_layout()

ROW_MEMQ, ROW_MEMK, ROW_K, ROW_Q = 0, 2, 4, 5


class Signal:

    TRIPS = {"pre": 1, "A": TILES, "SA": 1, "B": TILES, "SB": 1}

    def __init__(self, sem, per_tile, step=1, primed=0):
        self.sem, self.n, self.step = sem, per_tile, step
        self.base, at = {}, primed
        for part, trips in self.TRIPS.items():
            self.base[part] = at
            at += per_tile.get(part, 0) * trips
        self.total = at * step

    def after(self, part, tile, k=0):
        return (tile * self.n.get(part, 0) + (self.base[part] + k + 1)) * self.step


class Ring:

    def __init__(self, full, free, groups, primed=0):
        self.full, self.free, self.groups, self.primed = full, free, groups, primed
        self.nb = len(full)
        self.base, at = {}, 0
        for part, trips in Signal.TRIPS.items():
            self.base[part] = at
            n = len(groups.get(part, ()))
            assert trips == 1 or n % self.nb == 0, (part, n)
            at += n * trips

    def bank(self, part, name):
        return (self.base[part] + self.groups[part].index(name)) % self.nb

    def before(self, part, tile, name):
        at = self.base[part] + self.groups[part].index(name)
        return tile * (len(self.groups[part]) // self.nb) + at // self.nb

    def wait_free(self, eng, part, tile, name):
        n = self.before(part, tile, name)
        if not (isinstance(n, int) and n + self.primed == 0):
            eng.wait_ge(self.free[self.bank(part, name)], n + self.primed)
        return self.bank(part, name)

    def wait_full(self, eng, part, tile, name):
        eng.wait_ge(self.full[self.bank(part, name)], self.before(part, tile, name) + 1)
        return self.bank(part, name)

    def wait_read(self, eng, part, tile, name):
        eng.wait_ge(self.free[self.bank(part, name)], self.before(part, tile, name) + 1 + self.primed)


class Steps:

    def __init__(self, eng, sem):
        self.eng, self.sem = eng, sem
        self.before_loop = self.k = self.per = 0
        self.tile_ = 0

    def loop(self, per):
        self.before_loop, self.k, self.per = self.before_loop + self.k, per, per

    def tile(self, t):
        assert self.k == self.per, ("steps of a tile", self.k)
        self.k, self.tile_ = 0, t

    def end_loop(self, tiles):
        assert self.k == self.per, ("steps of a tile", self.k)
        self.before_loop, self.k, self.per, self.tile_ = self.before_loop + tiles * self.per, 0, 0, 0

    def __call__(self, ins):
        ins.then_inc(self.sem, 1)
        self.k += 1

    def wait(self):
        self.eng.wait_ge(self.sem, self.tile_ * self.per + (self.before_loop + self.k))


def build(nc, io):
    with ExitStack() as ctx:
        def sb(name, shape):
            return ctx.enter_context(nc.sbuf_tensor(name + "_sb", [P, *shape], F32))

        def sem(name):
            return ctx.enter_context(nc.semaphore(name))

        w_in = sb("w_in", [8, KC * 256])
        w_out = sb("w_out", [4, KC, 256])
        w_x = sb("w_x", [4096])
        x_buf = sb("x_buf", [2, KC, NT])
        xn = sb("xn", [KC, NT])
        big = sb("big", [8, NT])
        pm = sb("pm", [NBLK, 4, NMEM])
        gate = sb("gate", [KC, NT])
        scr = sb("scr", [2, 512])
        kTm = sb("kTm", [2, NMEM])
        vm = sb("vm", [MC, 256])
        ph = sb("ph", [6656])
        small = sb("small", [NSMALL])
        ones = sb("ones", [P])
        diag = sb("diag", [NBLK, P])
        tiny = sb("tiny", [320])

        def sm(name):
            a, n = SMALL[name]
            return small[:, a:a + n]

        gain = sm("gain").rearrange("p (g k) -> p g k", g=5)
        ident = sm("ident")
        invw, pscale = sm("invw"), sm("pscale")
        corr = sm("corr").rearrange("p (c t) -> p c t", c=POOLC)

        def row(n, heads, parts=P):
            a = SMALL["row"][0] + n * HD
            return small[0:parts, a:a + HD].rearrange("p (h d) -> p h d", h=1).to_broadcast([parts, heads, HD])

        x_var, x_rstd = tiny[:, 0:2], tiny[:, 2:4]
        q_ss = tiny[:, 4:20]
        q_rstds = [tiny[:, 20:36], tiny[:, 212:228]]
        k_ss = tiny[:, 36:44]
        k_rstds = [tiny[:, 44:52], q_rstds[1][:, 0:8]]
        m_max = tiny[:, 52:60].rearrange("p (b e) -> p b e", b=2)
        m_neg = tiny[:, 60:68].rearrange("p (b e) -> p b e", b=2)
        m_sum = tiny[:, 68:76].rearrange("p (b e) -> p b e", b=2)
        m_inv = tiny[:, 76:84].rearrange("p (b e) -> p b e", b=2)
        w_max = tiny[:, 84:92].rearrange("p (b e) -> p b e", b=2)
        w_neg = tiny[:, 92:100].rearrange("p (b e) -> p b e", b=2)
        w_sum = tiny[:, 100:108].rearrange("p (b e) -> p b e", b=2)
        w_inv = tiny[:, 108:116].rearrange("p (b e) -> p b e", b=2)
        w_sd = tiny[:, 116:124].rearrange("p (b e) -> p b e", b=2)
        w_se = tiny[:, 124:132].rearrange("p (b e) -> p b e", b=2)
        power = tiny[:, 192:208]
        s_max, s_neg, s_sum, s_inv = (tiny[0:96, 144 + 8 * i:152 + 8 * i] for i in range(4))
        s_sd, s_se = tiny[0:96, 176:184], tiny[0:96, 184:192]
        unit_a, unit_b = tiny[:, 232:240], tiny[:, 240:250]
        halfunit_a, halfunit_b = tiny[:, 250:258], tiny[:, 258:266]
        unit_heads = tiny[:, 266:282]
        k_unit = tiny[:, 294:302]
        w_top, w_scale, w_power = tiny[:, 282:284], tiny[:, 284:286], tiny[:, 302:304]
        mix_scale = tiny[:, 286:286 + POOLC]
        rot = sb("rot", [QH, 16])

        def flat(a):
            return a.rearrange("p e n -> p (e n)")

        def q_of(blk):
            return flat(pm[:, blk]).rearrange("p (h d) -> p h d", h=16)

        quarters = [flat(pm[:, i // 2])[:, (i % 2) * 512:(i % 2 + 1) * 512].rearrange("p (c n) -> p c n", c=2)
                    for i in range(4)]
        k_mem = quarters[0:2]
        kT_mem, v_mem = [kTm[:, :, :], quarters[2]], [vm[:, :, :], quarters[3]]

        qT_a = ph[:, 0:512].rearrange("p (c t) -> p c t", c=2)
        u = ph[:, 512:512 + POOLC * UW].rearrange("p (c t) -> p c t", c=POOLC)
        win_a = ph[:, 2144:2144 + POOLC * UW].rearrange("p (c t) -> p c t", c=POOLC)
        win_b = ph[:, 3776:3776 + POOLC * UW].rearrange("p (c t) -> p c t", c=POOLC)
        mix_w = w_x[:, 0:14 * P].rearrange("p (n m) -> p n m", n=14)
        qT_b = ph[:, 0:2048].rearrange("p (c t) -> p c t", c=8)
        ptc = ph[:, 2048:2560].rearrange("p (e t) -> p e t", e=4)
        ptp = ph[:, 2560:3072].rearrange("p (e t) -> p e t", e=4)
        kT = ph[:, 3072:4096].rearrange("p (k s t) -> p k s t", k=2, s=4)
        v = ph[:, 4096:5120].rearrange("p (s n) -> p s n", s=4)
        sw = ph[:, 5120:6144].rearrange("p (b e t) -> p b e t", b=2, e=4)
        k_tok = ph[:, 6144:6656].rearrange("p (b h d) -> p b h d", b=2, h=4)
        w_kv = w_x[:, :].bitcast(F16).rearrange("p (g s k n) -> p g s k n", g=2, s=2, k=KC)
        w_split = w_in[:, :, :].bitcast(F16).rearrange("p g (s k n) -> p g s k n", s=2, k=KC)
        xs = xn[:, :, :].rearrange("p k n -> p (k n)").bitcast(F16).rearrange("p (s k n) -> p s k n", s=2, k=KC)
        stage_a = [ph[:, i * 2048:(i + 1) * 2048].rearrange("p (k n) -> p k n", k=KC) for i in range(3)]
        raw = [w_in[:, g, :].rearrange("p (k n) -> p k n", k=KC) for g in range(8)] + [w_out[:, 0], w_out[:, 1]]
        stage_b = w_x[:, 14 * P:14 * P + 2048].rearrange("p (k n) -> p k n", k=KC)
        scratch_b = ph[:, 5408:6432].bitcast(BF16).rearrange("p (k n) -> p k n", k=KC)
        parts_b = [x.bitcast(F16).rearrange("p (s k n) -> p s k n", s=2, k=4)
                   for x in (ph[:, 5408:6432], w_x[:, 14 * P:14 * P + 1024])]
        lo = sb("lo", [4, BLK])
        top_diag = lo[:, 0:2, :]

        ps_z = ctx.enter_context(nc.psum_tensor("ps_z", [P, 2, 512], F32))
        ps_s = ctx.enter_context(nc.psum_tensor("ps_s", [P, 2, 2, 512], F32))
        ps_t = ctx.enter_context(nc.psum_tensor("ps_t", [P, 512], F32))
        ps_p = ctx.enter_context(nc.psum_tensor("ps_p", [P, 512], F32))

        first_parts = [w_split[:, g] for g in range(8)] + [
            x.bitcast(F16).rearrange("p (s k n) -> p s k n", s=2, k=KC)
            for x in (w_x[:, 14 * P:14 * P + 2048], gate[:, :, :].rearrange("p k n -> p (k n)"))]

        qbd_a = ph[:, 0:512].rearrange("p (c b n) -> p c b n", c=2, b=DB)
        state_tmp = pm[:, 1, :, :].rearrange("p e n -> p (e n)")[:, 0:POOLC * DB * PAD]\
            .rearrange("p (c b t) -> p c b t", c=POOLC, b=DB)
        pt_s = big[:, 0:2, :]
        w_flat = w_in[:, :, :].rearrange("p g n -> p (g n)")
        qbd_w = w_flat[:, 0:1536].rearrange("p (k b n) -> p k b n", k=2, b=DB)
        qbd_b = w_flat[:, 1536:2048].rearrange("p (c b n) -> p c b n", c=2, b=DB)
        v_new = w_flat[0:DS, 2048:4096].rearrange("p (b n) -> p b n", b=DB)
        sw_s = w_flat[0:96, 4096:5120].rearrange("p (b t) -> p b t", b=DB)
        pt_old = w_flat[:, 5120:5888].rearrange("p (b n) -> p b n", b=DB)
        pt_new = w_flat[0:DS, 5888:6656].rearrange("p (b n) -> p b n", b=DB)
        lo_s = w_flat[0:96, 6656:6720].rearrange("p (b t) -> p b t", b=DB)
        kT_new = ph[:, 3072:3200].rearrange("p (k t) -> p k t", k=2)
        kT_old = w_x[:, 0:2048].rearrange("p (k b t) -> p k b t", k=2, b=DB)
        v_old = w_x[:, 2048:4096].rearrange("p (b n) -> p b n", b=DB)

        def pooled(c):
            return win_a[:, c] if c in (0, 3) else win_b[:, c]

        def by_batch(x):
            return x[:, 0:DB * US].rearrange("p (b t) -> p b t", b=DB)

        def slot(xb, n):
            return x_buf[:, xb].rearrange("p k n -> p (k n)")[:, (n % 4) * 512:(n % 4 + 1) * 512]\
                .rearrange("p (c n) -> p c n", c=2)

        def tile_of(d, t):
            return d[t] if isinstance(t, int) else d[bass.ds(t, 1)].rearrange("a p k n -> (a p) k n")

        U3, G3 = ["u0", "u1", "u2"], ["g0", "g1", "g2"]
        OUT = ["out0", "out1", "out2", "out3"]
        PTM = ["ptm00", "ptm01", "ptm10", "ptm11"]
        OUTS = ["out0", "out1", "rb", "out2", "out3"]
        W6 = [(0, 0), (1, 0), (0, 1), (1, 1), (0, 2), (1, 2)]
        Z = Ring([sem("z_full0"), sem("z_full1")], [sem("z_free0"), sem("z_free1")], {
            "pre": ["rb_mem", "mem00", "mem01", "mem10", "mem11", "rb"],
            "A": ["qm", *U3, *G3, "gm", "mix0", "mix1", "mix2", *OUTS],
            "SA": ["qm", *U3, *G3, "gm", "mix0", "mix1", "mix2", "out0", "rb", "out1"],
            "B": ["kv0", "kv1", "qa0", "qb0", "qa1", "qb1", "gm", "g0", "g1", "g2", *OUT],
            "SB": ["kv0", "qa0", "qb0", "gm", *G3, "out0", "out1"],
        })
        T = Ring([sem("t_full")], [sem("t_free")], {
            "pre": ["ss_mem", "top0", "top1", "kt0", "top2", "kt1", "top3", "ss", *(f"top{g}" for g in range(4, 10))],
            "A": ["qT", *PTM, "top0", "ss"],
            "SA": ["qT", "pt0", "pt1", "ss", "ot0", "ot1"],
            "B": ["kT", "qT00", "qT01", "qT10", "qT11", "ptw0", "ptm00", "ptm01", "ptw1", "ptm10", "ptm11",
                  "ptw2", "ptw3", "ptw4", "ptw5"],
            "SB": ["kT", "qT00", "qT01", "ptw0", "ptw1", "pt0", "pt1", "ot0", "ot1"],
        })
        S = Ring([sem("s_full0"), sem("s_full1")], [sem("s_free0"), sem("s_free1")], {
            "A": ["m0", "m1"],
            "SA": ["m"],
            "B": ["m0", "w0", "w1", "m1", "w2", "w3", "w4", "w5"],
            "SB": ["wn", "wc", "m"],
        }, primed=1)
        V = Ring([sem("p_full")], [sem("p_free")], {
            "A": ["pvm"], "SA": ["pvm"],
            "B": ["pvw0", "pvw1", "pvm", "pvw2", "pvw3", "pvw4", "pvw5", "ss", "rb"],
            "SB": ["pvw0", "pvw1", "pvm"],
        }, primed=1)

        one = {"pre": 2, "A": 1, "SA": 1, "B": 1}
        small_in = sem("small_in")
        win_in = [sem(f"win_in{g}") for g in range(8)]
        raw_in = [sem(f"raw_in{g}") for g in range(10)]
        mix_in = sem("mix_in")
        prep = {"pre": 10, "A": 1}
        stageb_in = Signal(sem("stageb_in"), {"A": 1}, 16)
        w_gained = Signal(sem("w_gained"), prep)
        top_sum = Signal(sem("top_sum"), prep)
        top_in = Signal(sem("top_in"), prep)
        scale_in = Signal(sem("scale_in"), prep)
        high_in = Signal(sem("high_in"), {"pre": 10, "A": 2})
        low_in = Signal(sem("low_in"), {"pre": 10, "A": 2})
        parts_out = Signal(sem("parts_out"), {"pre": 2, "A": 2}, 16)
        xhigh_in = Signal(sem("xhigh_in"), {"pre": 1, "A": 1, "SA": 1, "B": 1})
        xlow_in = Signal(sem("xlow_in"), {"pre": 1, "A": 1, "SA": 1, "B": 1})
        wout_in = [sem(f"wout_in{g}") for g in range(4)]
        wx_in = [sem("wx_in0"), sem("wx_in1")]
        x_in = [sem("x_in0"), sem("x_in1")]
        x_stored = Signal(sem("x_stored"), {"pre": 1, "A": 1, "SA": 1, "B": 1, "SB": 1}, 16)
        outputs = sem("outputs")
        state_in = sem("state_in")
        state_out = sem("state_out")
        mem_reload = sem("mem_reload")
        vnew_in = sem("vnew_in")
        slot_in = [sem(f"slot_in{i}") for i in range(4)]
        slot_used = Signal(sem("slot_used"), {"SA": 14, "SB": 14})
        sq_x = Signal(sem("sq_x"), one)
        sums_x = Signal(sem("sums_x"), {"A": 1, "SA": 1, "B": 1})
        rstd_x = Signal(sem("rstd_x"), one)
        diag_x = Signal(sem("diag_x"), one)
        scr_in = Signal(sem("scr_in"), {"pre": 4, "A": 5, "SA": 5, "B": 10, "SB": 7})
        heads_var = Signal(sem("heads_var"), {"pre": 2, "A": 1, "SA": 1, "B": 3, "SB": 2})
        heads_norm = Signal(sem("heads_norm"), {"pre": 2, "A": 1, "SA": 1, "B": 3, "SB": 2})
        m_neg_in = Signal(sem("m_neg_in"), {"A": 2, "SA": 1, "B": 2, "SB": 1})
        m_inv_in = Signal(sem("m_inv_in"), {"A": 2, "SA": 1, "B": 2, "SB": 1})
        pm_norm = Signal(sem("pm_norm"), {"A": 2, "SA": 1, "B": 2, "SB": 1})
        w_neg_in = Signal(sem("w_neg_in"), {"B": 6, "SB": 1})
        w_exp = Signal(sem("w_exp"), {"B": 6, "SB": 1})
        w_inv_in = Signal(sem("w_inv_in"), {"B": 6, "SB": 1})
        pw_norm = Signal(sem("pw_norm"), {"B": 6, "SB": 1})
        u_free = Signal(sem("u_free"), {"pre": 1, "A": 1, "SA": 1})
        win_sums = Signal(sem("win_sums"), {"A": 1, "SA": 1})
        d_in = Signal(sem("d_in"), {"A": 1, "SA": 1})
        pool_out = sem("pool_out")
        state_set = sem("state_set")
        qbd_zero = Signal(sem("qbd_zero"), {"SA": 1, "SB": 1})
        consts = sem("consts")
        acts, dves, pools = sem("act_steps"), sem("dve_steps"), sem("pool_steps")

        def load_slot(sp, part, n, layer, xb):
            if n >= 4:
                m = n - 4
                if m == 7:
                    S.wait_full(sp, part, 0, "m")
                else:
                    sp.wait_ge(slot_used.sem, slot_used.after(part, 0, m if m < 7 else m - 1))
            src = io["mem_ks"][layer, n] if n < DB else io["mem_vs"][layer, n - DB]
            nc.sync.dma_start(slot(xb, n), src).then_inc(slot_in[n % 4], 16)

        def wait_slot(pe, part, n):
            pe.wait_ge(slot_in[n % 4], 16 * ((4 if part == "SB" else 0) + n // 4 + 1))

        block = ctx.enter_context(nc.Block())
        xd, x1d, yd = io["x"], io["x1"], io["y"]

        @block.sync
        def _(sp):
            dma = nc.sync.dma_start
            dma(x_buf[:, 1], io["memx"]).then_inc(x_in[1], 16)
            dma(small[:, :], io["small"]).then_inc(small_in, 16)
            for g in range(4):
                dma(w_out[:, g], io["w_mem"][g]).then_inc(wout_in[g], 16)
            for g in range(8):
                dma(raw[g], io["w_in_a"][g]).then_inc(raw_in[g], 16)
                if g == 2:
                    dma(x_buf[:, 0], xd[0]).then_inc(x_in[0], 16)
            Z.wait_full(sp, "pre", 0, "mem01")
            for g in (8, 9):
                dma(raw[g], io["w_in_b"][g]).then_inc(raw_in[g], 16)
            dma(w_x[:, 0:14 * P], io["mix"]).then_inc(mix_in, 16)

            for l in range(2):
                sp.wait_ge(heads_norm.sem, heads_norm.after("pre", 0, l))
                dma(io["mem_k"][l], k_mem[l]).then_inc(outputs, 16)
                T.wait_read(sp, "pre", 0, f"kt{l}")
                dma(io["mem_v"][l], v_mem[l]).then_inc(outputs, 16)
            dma(io["kt1"], kT_mem[1]).then_inc(x_stored.sem, 16)
            for g in (2, 3, 0, 1):
                if g < 2:
                    sp.wait_ge(w_gained.sem, w_gained.after("pre", 0, 8 + g))
                dma(w_out[:, g], io["w_out_a"][g]).then_inc(wout_in[g], 16)
            for g in (8, 9):
                sp.wait_ge(low_in.sem, low_in.after("pre", 0, g))
                dma(io["parts"][g], first_parts[g]).then_inc(parts_out.sem, 16)

            def prepare(t, src, dst):
                sp.wait_ge(parts_out.sem, parts_out.after("A", t, -1))
                dma(stage_b, src).then_inc(stageb_in.sem, 16)
                for half in range(2):
                    sp.wait_ge(low_in.sem, low_in.after("A", t, half))
                    dma(dst[:, :, half * 4:half * 4 + 4, :], parts_b[half]).then_inc(parts_out.sem, 16)

            with sp.Fori(0, TILES // 2) as it:
                for p in range(2):
                    t = it * 2 + p
                    sp.wait_ge(x_stored.sem, x_stored.after("A", t, -1))
                    dma(x_buf[:, 1 - p], tile_of(xd, t + 1)).then_inc(x_in[1 - p], 16)
                    prepare(t, io["w_in_b"][bass.ds(t, 1)].rearrange("a p k n -> (a p) k n"),
                            io["parts"][bass.ds(t, 1)].rearrange("a p s k n -> (a p) s k n"))
                    Z.wait_read(sp, "A", t, "out3")
                    dma(tile_of(x1d, t), x_buf[:, p]).then_inc(x_stored.sem, 16)

            sp.wait_ge(outputs, 4 * 16)
            dma(kTm[:, :, :], io["kt1"]).then_inc(mem_reload, 16)
            dma(vm[:, :, :], io["mem_v"][1]).then_inc(mem_reload, 16)
            sp.wait_ge(x_stored.sem, x_stored.after("A", TILES - 1))
            for n in range(16):
                load_slot(sp, "SA", n, 0, 1)
            sp.wait_ge(pool_out, 1)
            dma(io["pool_s"], state_tmp).then_inc(state_out, 16)
            V.wait_full(sp, "SA", 0, "pvm")
            dma(x_buf[:, 1], x1d[0]).then_inc(x_in[1], 16)
            Z.wait_full(sp, "SA", 0, "mix2")
            sp.wait_ge(parts_out.sem, parts_out.total)
            for g in range(2):
                dma(w_kv[:, g], io["parts"][8 + g]).then_inc(wx_in[g], 16)
            Z.wait_full(sp, "SA", 0, "out1")
            for g in range(4):
                dma(w_out[:, g], io["w_out_b"][g]).then_inc(wout_in[g], 16)
            T.wait_read(sp, "SA", 0, "ot1")
            dma(x1d[TILES], x_buf[:, 0]).then_inc(x_stored.sem, 16)
            dma(io["swa_k_s"][:, 0:BLK - DS], io["kc_tok"][:, DS:BLK]).then_inc(outputs, 16)
            dma(io["swa_v_s"][:, 0:BLK - DS], io["vc_tok"][:, DS:BLK]).then_inc(outputs, 16)

            with sp.Fori(0, TILES // 2) as it:
                for p in range(2):
                    t = it * 2 + p
                    sp.wait_ge(x_stored.sem, x_stored.after("B", t, -1))
                    dma(x_buf[:, p], tile_of(x1d, t + 1)).then_inc(x_in[p], 16)
                    Z.wait_read(sp, "B", t, "out3")
                    dma(tile_of(yd, t), x_buf[:, 1 - p]).then_inc(x_stored.sem, 16)

            dma(io["swa_k_p"], k_tok[:, 1].rearrange("p h d -> p (h d)")).then_inc(outputs, 16)
            dma(io["swa_v_p"], v[:, 3]).then_inc(outputs, 16)
            sp.wait_ge(x_stored.sem, x_stored.after("B", TILES - 1))
            Z.wait_full(sp, "SB", 0, "kv0")
            dma(kT_old, io["kc"]).then_inc(wx_in[0], 16)
            for n in range(4):
                load_slot(sp, "SB", n, 1, 0)
            dma(v_old, io["vc"]).then_inc(wx_in[1], 16)
            Z.wait_full(sp, "SB", 0, "qb0")
            sp.wait_ge(scr_in.sem, scr_in.after("SB", 0, 0))
            for b in range(DB):
                dma(v_new[:, b], v[b * DS:(b + 1) * DS, 0]).then_inc(vnew_in, 16)
            sp.wait_ge(heads_norm.sem, heads_norm.after("SB", 0, 0))
            for b in range(DB):
                rows = slice(b * DS, (b + 1) * DS)
                dma(io["swa_k_s"][b, BLK - DS:BLK], k_tok[rows, 0].rearrange("p h d -> p (h d)")).then_inc(outputs, 16)
                dma(io["swa_v_s"][b, BLK - DS:BLK], v[rows, 0]).then_inc(outputs, 16)
            for n in range(4, 16):
                load_slot(sp, "SB", n, 1, 0)
            T.wait_read(sp, "SB", 0, "ot1")
            dma(yd[TILES], x_buf[:, 1]).then_inc(x_stored.sem, 16)
            sp.wait_ge(x_stored.sem, x_stored.total)
            sp.wait_ge(state_out, 32)
            sp.wait_ge(outputs, 16 * (4 + 2 + 2 + 2 * DB))

        @block.tensor
        def _(pe):
            mm, tr = nc.tensor.matmul, nc.tensor.transpose

            def square_sums(ring, part, t, name, k):
                if part == "pre":
                    pe.wait_ge(sq_x.sem, sq_x.after(part, t, k))
                else:
                    pe.wait_ge(sums_x.sem, sums_x.after(part, t, k))
                b = ring.wait_free(pe, part, t, name)
                out = ps_t if ring is T else ps_p
                chunks = KC if part == "pre" else 1
                for blk in range(NBLK):
                    for kc in range(chunks):
                        last = mm(out[:, blk:blk + 1], big[:, kc, blk * P:(blk + 1) * P], ones[:, 0:1],
                                  start=(kc == 0), stop=(kc == chunks - 1))
                last.then_inc(ring.full[b], 1)

            def rstd_rows(part, t, name, k):
                pe.wait_ge(diag_x.sem, diag_x.after(part, t, k))
                ring = V if part == "B" else Z
                b = ring.wait_free(pe, part, t, name)
                out = ps_p[:, :] if part == "B" else ps_z[:, b]
                for blk in range(NBLK):
                    last = mm(out[:, blk * P:(blk + 1) * P], ones[:, :], diag[:, blk, :], start=True, stop=True)
                last.then_inc(ring.full[b], 1)

            PARTS = ((0, 0), (0, 1), (1, 0))

            def split_tokens(part, t, name, tok, w, gs, n=P):
                b = Z.wait_free(pe, part, t, name)
                out = ps_z[0:n, b, 0:256 * len(gs)].rearrange("p (g n) -> p g n", g=len(gs))
                for kc in range(KC):
                    for ws, x in PARTS:
                        last = mm(out, xs[:, x, kc, tok:tok + n], w[:, gs[0]:gs[-1] + 1, ws, kc, :],
                                  start=(kc == 0 and ws + x == 0), stop=(kc == KC - 1 and ws == 1))
                last.then_inc(Z.full[b], 1)

            def split_features(part, t, name, g, n=NT, halves=(0, 1), kcs=range(KC)):
                first, whole = 0 in halves and 0 in kcs, 1 in halves and KC - 1 in kcs
                b = Z.wait_free(pe, part, t, name) if first else Z.bank(part, name)
                for half in halves:
                    for kc in kcs:
                        for ws, x in PARTS:
                            last = mm(ps_z[:, b, half * NT:half * NT + n],
                                      w_split[:, g, ws, kc, half * P:(half + 1) * P], xs[:, x, kc, 0:n],
                                      start=(kc == 0 and ws + x == 0), stop=(kc == KC - 1 and ws == 1))
                if whole:
                    last.then_inc(Z.full[b], 1)

            def magnitude_rows(part, t, k, name):
                pe.wait_ge(top_in.sem, top_in.after(part, t, k))
                T.wait_free(pe, part, t, name)
                mm(ps_t[:, 0:P], ones[:, :], top_diag[:, k % 2], start=True, stop=True).then_inc(T.full[0], 1)

            def by_token(part, t, name, src, tok, w, g, n=P):
                b = Z.wait_free(pe, part, t, name)
                for kc in range(KC):
                    last = mm(ps_z[0:n, b, :].rearrange("p (g n) -> p g n", g=2), src[:, kc, tok:tok + n],
                              w[:, g:g + 2, kc, :], start=(kc == 0), stop=(kc == KC - 1))
                last.then_inc(Z.full[b], 1)

            def by_feature(part, t, name, src, w, g, n=NT, halves=(0, 1)):
                b = Z.wait_free(pe, part, t, name) if 0 in halves else Z.bank(part, name)
                for half in halves:
                    for kc in range(KC):
                        last = mm(ps_z[:, b, half * NT:half * NT + n], w[:, g, kc, half * P:(half + 1) * P],
                                  src[:, kc, 0:n], start=(kc == 0), stop=(kc == KC - 1))
                if 1 in halves:
                    last.then_inc(Z.full[b], 1)

            def mem_scores(part, t, blk, qT, c0):
                b = S.wait_free(pe, part, t, f"m{blk}")
                for c in range(2):
                    for par in range(2):
                        rows = slice(par * HD, (par + 1) * HD)
                        last = mm(ps_s[:, b, par, c * NMEM:(c + 1) * NMEM],
                                  qT[rows, c0 + c, blk * P:(blk + 1) * P], kTm[rows, c, :], start=True, stop=True)
                last.then_inc(S.full[b], 1)

            def mem_transposes(part, t, blk, mc):
                pe.wait_ge(pm_norm.sem, pm_norm.after(part, t, blk))
                T.wait_free(pe, part, t, f"ptm{blk}{mc}")
                for e in range(4):
                    last = tr(ps_t[:, e * P:(e + 1) * P], pm[:, blk, e, mc * P:(mc + 1) * P], ident)
                last.then_inc(T.full[0], 1)

            def mem_values(part, t):
                T.wait_read(pe, part, t, "ptm11")
                V.wait_free(pe, part, t, "pvm")
                for c in range(2):
                    for mc in range(MC):
                        for par in range(2):
                            h = 2 * c + par
                            last = mm(ps_p[par * HD:(par + 1) * HD, c * NT:(c + 1) * NT],
                                      vm[:, mc, h * HD:(h + 1) * HD], big[:, mc * 4 + par * 2 + c, :],
                                      start=(mc == 0), stop=(mc == MC - 1), skip_group_check=True)
                last.then_inc(V.full[0], 1)

            def mix(part, t, n):
                pe.wait_ge(mix_in, 16)
                pe.wait_ge(d_in.sem, d_in.after(part, t))
                blocks = [(o, i) for o in range(POOLC) for i in range(POOLC)
                          if o // 3 == i // 3 and abs(o - i) < 2]
                for pair in range(3):
                    b = Z.wait_free(pe, part, t, f"mix{pair}")
                    for o in (2 * pair, 2 * pair + 1):
                        ins = [i for (oo, i) in blocks if oo == o]
                        for i in ins:
                            src = pooled(i)[:, 16:UW] if n == NT else \
                                pooled(i)[:, 0:DB * US].rearrange("p (b t) -> p b t", b=DB)[:, :, 16:US]
                            out = ps_z[:, b, (o % 2) * NT:(o % 2) * NT + n]
                            if n != NT:
                                out = out.rearrange("p (b t) -> p b t", b=DB)
                            last = mm(out, mix_w[:, blocks.index((o, i)), :], src,
                                      start=(i == ins[0]), stop=(i == ins[-1]))
                    last.then_inc(Z.full[b], 1)

            def project_out(part, t, groups, n=NT):
                for g in groups:
                    by_feature(part, t, f"out{g}", gate, w_out, g, n)

            def memory_keys(l):
                pe.wait_ge(heads_norm.sem, heads_norm.after("pre", 0, l))
                T.wait_free(pe, "pre", 0, f"kt{l}")
                for c in range(2):
                    for mc in range(MC):
                        last = tr(ps_t[:, (c * MC + mc) * P:(c * MC + mc + 1) * P],
                                  k_mem[l][:, mc, c * P:(c + 1) * P], ident)
                last.then_inc(T.full[0], 1)

            pe.wait_ge(consts, 2)
            pe.wait_ge(small_in, 16)
            square_sums(T, "pre", 0, "ss_mem", 0)
            rstd_rows("pre", 0, "rb_mem", 0)
            Z.wait_read(pe, "pre", 0, "rb_mem")
            pe.wait_ge(wout_in[0], 16)
            pe.wait_ge(wout_in[1], 16)
            by_token("pre", 0, "mem00", xn, 0, w_out, 0)
            by_token("pre", 0, "mem01", xn, P, w_out, 0)
            pe.wait_ge(wout_in[2], 16)
            pe.wait_ge(wout_in[3], 16)
            by_token("pre", 0, "mem10", x_buf[:, 1], 0, w_out, 2)
            magnitude_rows("pre", 0, 0, "top0")
            by_token("pre", 0, "mem11", x_buf[:, 1], P, w_out, 2)
            magnitude_rows("pre", 0, 1, "top1")
            memory_keys(0)
            magnitude_rows("pre", 0, 2, "top2")
            memory_keys(1)
            magnitude_rows("pre", 0, 3, "top3")
            square_sums(T, "pre", 0, "ss", 1)
            magnitude_rows("pre", 0, 4, "top4")
            rstd_rows("pre", 0, "rb", 1)
            for g in range(5, 10):
                magnitude_rows("pre", 0, g, f"top{g}")

            def q_transposes_a(part, t, n=P, blocks=NBLK):
                pe.wait_ge(heads_norm.sem, heads_norm.after(part, t))
                T.wait_free(pe, part, t, "qT")
                for c in range(2):
                    for blk in range(blocks):
                        last = tr(ps_t[:, (c * blocks + blk) * n:(c * blocks + blk + 1) * n],
                                  q_of(0)[0:n, blk * 4 + 2 * c:blk * 4 + 2 * c + 2, :].rearrange("p h d -> p (h d)"),
                                  ident[0:n, 0:n])
                last.then_inc(T.full[0], 1)

            with pe.Fori(0, TILES // 2) as it:
                for p in range(2):
                    t = it * 2 + p
                    pe.wait_ge(low_in.sem, low_in.after("pre", 0, 7))
                    pe.wait_ge(xlow_in.sem, xlow_in.after("A", t, -1))
                    b = Z.wait_free(pe, "A", t, "qm")
                    for blk in range(NBLK):
                        for kc in range(KC):
                            for ws, x in PARTS:
                                last = mm(ps_z[:, b, blk * 256:(blk + 1) * 256], xs[:, x, kc, blk * P:(blk + 1) * P],
                                          w_split[:, 0, ws, kc, :],
                                          start=(kc == 0 and ws + x == 0), stop=(kc == KC - 1 and ws == 1))
                    last.then_inc(Z.full[b], 1)
                    for i in range(3):
                        split_features("A", t, f"u{i}", 1 + i)
                    q_transposes_a("A", t)
                    T.wait_read(pe, "A", t, "qT")
                    mem_scores("A", t, 0, qT_a, 0)
                    mem_scores("A", t, 1, qT_a, 0)
                    split_features("A", t, "g0", 4)
                    mem_transposes("A", t, 0, 0)
                    split_features("A", t, "g1", 5, halves=(0,))
                    mem_transposes("A", t, 0, 1)
                    split_features("A", t, "g1", 5, halves=(1,))
                    mem_transposes("A", t, 1, 0)
                    split_features("A", t, "g2", 6, halves=(0,))
                    mem_transposes("A", t, 1, 1)
                    split_features("A", t, "g2", 6, halves=(1,))
                    mem_values("A", t)
                    split_features("A", t, "gm", 7)
                    mix("A", t, NT)
                    magnitude_rows("A", t, 0, "top0")
                    for g in range(4):
                        pe.wait_ge(wout_in[g], 32)
                    V.wait_read(pe, "A", t, "pvm")
                    Z.wait_read(pe, "A", t, "mix2")
                    project_out("A", t, (0,))
                    square_sums(T, "A", t, "ss", 0)
                    project_out("A", t, (1,))
                    rstd_rows("A", t, "rb", 0)
                    project_out("A", t, (2, 3))

            def sample_mem_scores(part, qbd, x_slot):
                b = S.wait_free(pe, part, 0, "m")
                base = 0 if part == "SA" else 1
                for n in range(DB):
                    wait_slot(pe, part, n)
                    for c in range(2):
                        last = mm(ps_s[(n % 4) * 32:(n % 4) * 32 + 32, b, 0, (n // 4) * NMEM:(n // 4 + 1) * NMEM],
                                  qbd[:, c, n, :], slot(x_slot, n)[:, c, :], start=(c == 0), stop=(c == 1),
                                  skip_group_check=True)
                    if n < DB - 1:
                        last.then_inc(slot_used.sem, 1)
                last.then_inc(S.full[b], 1)

            def sample_mem_transposes(part):
                pe.wait_ge(pm_norm.sem, pm_norm.after(part, 0))
                for mc in range(MC):
                    T.wait_free(pe, part, 0, f"pt{mc}")
                    for half in range(2):
                        last = tr(ps_t[:, half * P:(half + 1) * P], pm[:, 0, half, mc * P:(mc + 1) * P], ident)
                    last.then_inc(T.full[0], 1)

            def sample_mem_values(part, x_slot):
                T.wait_read(pe, part, 0, "pt1")
                V.wait_free(pe, part, 0, "pvm")
                for n in range(DB):
                    wait_slot(pe, part, DB + n)
                    for c in range(2):
                        cols = slice(n * 32 + c * 16, n * 32 + c * 16 + 16)
                        for mc in range(MC):
                            last = mm(ps_p[:, cols], slot(x_slot, DB + n)[:, mc, c * P:(c + 1) * P], pt_s[:, mc, cols],
                                      start=(mc == 0), stop=(mc == MC - 1), skip_group_check=True)
                    if n < DB - 1:
                        last.then_inc(slot_used.sem, 1)
                last.then_inc(V.full[0], 1)

            def sample_out(part, half):
                by_token(part, 0, f"out{half}", gate, 0, w_out, 2 * half, NS)

            def sample_out_transposes(part, half):
                b = Z.bank(part, f"out{half}")
                Z.wait_read(pe, part, 0, f"out{half}")
                T.wait_free(pe, part, 0, f"ot{half}")
                for c in range(4):
                    last = tr(ps_t[:, c * NS:(c + 1) * NS], scr[0:NS, b, c * P:(c + 1) * P], ident[0:NS, 0:NS])
                last.then_inc(T.full[0], 1)

            pe.wait_ge(xlow_in.sem, xlow_in.after("SA", 0, -1))
            split_tokens("SA", 0, "qm", 0, w_split, (0,), NS)
            for i in range(3):
                split_features("SA", 0, f"u{i}", 1 + i, NS)
            q_transposes_a("SA", 0, NS, 1)
            T.wait_read(pe, "SA", 0, "qT")
            sample_mem_scores("SA", qbd_a, 1)
            for i in range(3):
                split_features("SA", 0, f"g{i}", 4 + i, NS)
            split_features("SA", 0, "gm", 7, NS)
            sample_mem_transposes("SA")
            sample_mem_values("SA", 1)
            mix("SA", 0, NS)
            V.wait_read(pe, "SA", 0, "pvm")
            Z.wait_read(pe, "SA", 0, "mix2")
            sample_out("SA", 0)
            square_sums(T, "SA", 0, "ss", 0)
            sample_out_transposes("SA", 0)
            rstd_rows("SA", 0, "rb", 0)
            sample_out("SA", 1)
            sample_out_transposes("SA", 1)
            pe.wait_ge(mem_reload, 32)

            def q_transposes_b(part, t, blk, half, n=P):
                pe.wait_ge(heads_norm.sem, heads_norm.after(part, t, 1 + blk))
                T.wait_free(pe, part, t, f"qT{blk}{half}")
                for c in range(4):
                    h = (half * 4 + c) * 2
                    last = tr(ps_t[:, c * n:(c + 1) * n], q_of(blk)[0:n, h:h + 2, :].rearrange("p h d -> p (h d)"),
                              ident[0:n, 0:n])
                last.then_inc(T.full[0], 1)

            def window_scores(t, p, i):
                blk, gi = W6[i]
                b = S.wait_free(pe, "B", t, f"w{i}")
                own = 2 * p + blk
                for c in range(2):
                    for par in range(2):
                        rows = slice(par * HD, (par + 1) * HD)
                        ch = 2 * gi + c
                        for j, s in enumerate(((own - 1) % 4, own)):
                            at = c * 256 + j * P
                            last = mm(ps_s[:, b, par, at:at + P], qT_b[rows, ch, blk * P:(blk + 1) * P],
                                      kT[rows, ch // 3, s, :], start=True, stop=True)
                last.then_inc(S.full[b], 1)

            def window_transposes(t, i):
                pe.wait_ge(pw_norm.sem, pw_norm.after("B", t, i))
                T.wait_free(pe, "B", t, f"ptw{i}")
                for e in range(4):
                    last = tr(ps_t[:, e * P:(e + 1) * P], sw[:, i % 2, e, :], ident)
                last.then_inc(T.full[0], 1)

            def window_values(t, p, i):
                blk, gi = W6[i]
                T.wait_read(pe, "B", t, f"ptw{i}")
                V.wait_free(pe, "B", t, f"pvw{i}")
                own = 2 * p + blk
                for c in range(2):
                    for j, (s, w) in enumerate((((own - 1) % 4, ptp), (own, ptc))):
                        for par in range(2):
                            kv = 2 * ((2 * gi + c) // 3) + par
                            last = mm(ps_p[par * HD:(par + 1) * HD, c * P:(c + 1) * P],
                                      v[:, s, kv * HD:(kv + 1) * HD], w[:, par * 2 + c, :],
                                      start=(j == 0), stop=(j == 1), skip_group_check=True)
                last.then_inc(V.full[0], 1)

            with pe.Fori(0, TILES // 2) as it:
                for p in range(2):
                    t = it * 2 + p
                    pe.wait_ge(xlow_in.sem, xlow_in.after("B", t, -1))
                    for g in range(2):
                        pe.wait_ge(wx_in[g], 16)
                    split_tokens("B", t, "kv0", 0, w_kv, (0, 1))
                    split_tokens("B", t, "kv1", P, w_kv, (0, 1))
                    for g in range(4):
                        pe.wait_ge(win_in[g], 16)
                    split_tokens("B", t, "qa0", 0, w_split, (0, 1))
                    split_tokens("B", t, "qb0", 0, w_split, (2, 3))
                    pe.wait_ge(heads_norm.sem, heads_norm.after("B", t, 0))
                    T.wait_free(pe, "B", t, "kT")
                    for kp in range(2):
                        for blk in range(NBLK):
                            last = tr(ps_t[:, (kp * 2 + blk) * P:(kp * 2 + blk + 1) * P],
                                      k_tok[:, blk, 2 * kp:2 * kp + 2, :].rearrange("p h d -> p (h d)"), ident)
                    last.then_inc(T.full[0], 1)
                    split_tokens("B", t, "qa1", P, w_split, (0, 1))
                    split_tokens("B", t, "qb1", P, w_split, (2, 3))
                    q_transposes_b("B", t, 0, 0)
                    for g in range(4, 8):
                        pe.wait_ge(win_in[g], 16)
                    split_features("B", t, "gm", 7, halves=(0,))
                    q_transposes_b("B", t, 0, 1)
                    split_features("B", t, "gm", 7, halves=(1,))
                    T.wait_read(pe, "B", t, "qT01")
                    mem_scores("B", t, 0, qT_b, 6)
                    window_scores(t, p, 0)
                    q_transposes_b("B", t, 1, 0)
                    split_features("B", t, "g0", 4, halves=(0,))
                    T.wait_read(pe, "B", t, "qT10")
                    q_transposes_b("B", t, 1, 1)
                    window_scores(t, p, 1)
                    split_features("B", t, "g0", 4, halves=(1,))
                    T.wait_read(pe, "B", t, "qT11")
                    mem_scores("B", t, 1, qT_b, 6)
                    window_transposes(t, 0)
                    window_scores(t, p, 2)
                    split_features("B", t, "g1", 5, halves=(0,))
                    mem_transposes("B", t, 0, 0)
                    window_values(t, p, 0)
                    mem_transposes("B", t, 0, 1)
                    split_features("B", t, "g1", 5, halves=(1,))
                    window_transposes(t, 1)
                    window_scores(t, p, 3)
                    split_features("B", t, "g2", 6, halves=(0,), kcs=range(0, 4))
                    mem_transposes("B", t, 1, 0)
                    window_values(t, p, 1)
                    mem_transposes("B", t, 1, 1)
                    split_features("B", t, "g2", 6, halves=(0,), kcs=range(4, 8))
                    window_transposes(t, 2)
                    mem_values("B", t)
                    window_scores(t, p, 4)
                    window_values(t, p, 2)
                    window_transposes(t, 3)
                    window_scores(t, p, 5)
                    split_features("B", t, "g2", 6, halves=(1,))
                    window_values(t, p, 3)
                    for g in range(4):
                        pe.wait_ge(wout_in[g], 48)
                    b = Z.wait_free(pe, "B", t, "out0")

                    def first_output(chunks):
                        for kc in chunks:
                            mm(ps_z[:, b, 0:NT], w_out[:, 0, kc, 0:P], gate[:, kc, :],
                               start=(kc == 0), stop=(kc == 5))
                    window_transposes(t, 4)
                    V.wait_read(pe, "B", t, "pvw2")
                    first_output((0, 1, 6))
                    window_values(t, p, 4)
                    window_transposes(t, 5)
                    V.wait_read(pe, "B", t, "pvw3")
                    first_output((7, 2, 3))
                    window_values(t, p, 5)
                    V.wait_read(pe, "B", t, "pvw5")
                    first_output((4, 5))
                    by_feature("B", t, "out0", gate, w_out, 0, halves=(1,))
                    square_sums(V, "B", t, "ss", 0)
                    project_out("B", t, (1,))
                    rstd_rows("B", t, "rb", 0)
                    project_out("B", t, (2, 3))

            pe.wait_ge(xlow_in.sem, xlow_in.after("SB", 0, -1))
            split_tokens("SB", 0, "kv0", 0, w_kv, (0, 1), NS)
            split_tokens("SB", 0, "qa0", 0, w_split, (0, 1), NS)
            split_tokens("SB", 0, "qb0", 0, w_split, (2, 3), NS)
            split_features("SB", 0, "gm", 7, NS)
            for i in range(3):
                split_features("SB", 0, f"g{i}", 4 + i, NS)
            pe.wait_ge(heads_norm.sem, heads_norm.after("SB", 0, 0))
            T.wait_free(pe, "SB", 0, "kT")
            for kp in range(2):
                last = tr(ps_t[:, kp * NS:(kp + 1) * NS],
                          k_tok[0:NS, 0, 2 * kp:2 * kp + 2, :].rearrange("p h d -> p (h d)"), ident[0:NS, 0:NS])
            last.then_inc(T.full[0], 1)
            q_transposes_b("SB", 0, 0, 0, NS)
            q_transposes_b("SB", 0, 0, 1, NS)
            T.wait_read(pe, "SB", 0, "qT01")
            b = S.wait_free(pe, "SB", 0, "wn")
            for n in range(DB):
                for kp in range(2):
                    last = mm(ps_s[0:96, b, 0, n * DS:(n + 1) * DS], qbd_w[:, kp, n, :],
                              kT_new[:, kp, n * DS:(n + 1) * DS], start=(kp == 0), stop=(kp == 1))
            last.then_inc(S.full[b], 1)
            b = S.wait_free(pe, "SB", 0, "wc")
            pe.wait_ge(wx_in[0], 32)
            for n in range(DB):
                for kp in range(2):
                    last = mm(ps_s[0:96, b, n // 4, (n % 4) * P:(n % 4 + 1) * P], qbd_w[:, kp, n, :],
                              kT_old[:, kp, n, :], start=(kp == 0), stop=(kp == 1))
            last.then_inc(S.full[b], 1)
            sample_mem_scores("SB", qbd_b, 0)
            pe.wait_ge(pw_norm.sem, pw_norm.after("SB", 0))
            for half in range(2):
                T.wait_free(pe, "SB", 0, f"ptw{half}")
                for n in range(4):
                    last = tr(ps_t[:, n * 96:(n + 1) * 96], sw_s[:, half * 4 + n, :], ident[0:96, 0:96])
                last.then_inc(T.full[0], 1)
            T.wait_read(pe, "SB", 0, "ptw1")
            pe.wait_ge(wx_in[1], 32)
            pe.wait_ge(vnew_in, 16 * DB)
            for kp in range(2):
                V.wait_free(pe, "SB", 0, f"pvw{kp}")
                cols = slice(kp * 48, (kp + 1) * 48)
                for n in range(DB):
                    out = ps_p[:, n * 48:(n + 1) * 48]
                    mm(out, v_old[:, n, kp * P:(kp + 1) * P], pt_old[:, n, cols], start=True, stop=False)
                    last = mm(out, v_new[:, n, kp * P:(kp + 1) * P], pt_new[:, n, cols], start=False, stop=True)
                last.then_inc(V.full[0], 1)
            sample_mem_transposes("SB")
            sample_mem_values("SB", 0)
            V.wait_read(pe, "SB", 0, "pvm")
            sample_out("SB", 0)
            sample_out("SB", 1)
            sample_out_transposes("SB", 0)
            sample_out_transposes("SB", 1)

        @block.scalar
        def _(act):
            f = nc.scalar.activation

            def squares_x(part, t, k, xb, arrived):
                act.wait_ge(x_in[xb], arrived)
                f(big[:, :, :], x_buf[:, xb], ACT.Square).then_inc(sq_x.sem, 1)

            def squares_heads(part, t, name, units, n=P, cols=512):
                b = Z.wait_full(act, part, t, name)
                w = cols // len(units)
                for i, unit in enumerate(units):
                    last = f(scr[0:n, b, i * w:(i + 1) * w], ps_z[0:n, b, i * w:(i + 1) * w], ACT.Square,
                             scale=unit if isinstance(unit, float) else unit[0:n])
                return last

            def squares_kv(part, t, name, v_out, units=(1.0, 1.0), n=P):
                squares_heads(part, t, name, units[0:1], n, 256)
                b = Z.bank(part, name)
                f(v_out, ps_z[0:n, b, 256:512], ACT.Copy, scale=units[1] if isinstance(units[1], float) else units[1][0:n])\
                    .then_inc(scr_in.sem, 1)

            def x_high(part, t):
                (V if part == "B" else Z).wait_read(act, part, t, "rb")
                f(xs[:, 0], big[:, :, :], ACT.Copy).then_inc(xhigh_in.sem, 1)

            def high(part, t, k, dst, src):
                act.wait_ge(scale_in.sem, scale_in.after(part, t, k))
                f(dst, src, ACT.Copy, scale=w_scale[:, k % 2:k % 2 + 1]).then_inc(high_in.sem, 1)

            def high_b(part, t, k):
                for half in range(2):
                    if half:
                        act.wait_ge(low_in.sem, low_in.after(part, t, 2 * k))
                    high(part, t, k, parts_b[half][:, 0], stage_b[:, half * 4:half * 4 + 4, :])

            def tanh(part, t, name, halfunit, n=NT):
                b = Z.wait_full(act, part, t, name)
                pair = [x[:, b].rearrange("p (c n) -> p c n", c=2)[:, :, 0:n] for x in (scr, ps_z)]
                f(pair[0], pair[1], ACT.Tanh, scale=halfunit).then_inc(scr_in.sem, 1)

            def from_t(part, t, name, out, src=None):
                T.wait_full(act, part, t, name)
                f(out, ps_t[:, :] if src is None else src, ACT.Copy).then_inc(T.free[0], 1)

            def mem_exps(part, t, blk):
                b = S.wait_full(act, part, t, f"m{blk}")
                act.wait_ge(m_neg_in.sem, m_neg_in.after(part, t, blk))
                for e in range(4):
                    last = f(pm[:, blk, e, :], ps_s[:, b, e // 2, (e % 2) * NMEM:(e % 2 + 1) * NMEM], ACT.Exp,
                             bias=m_neg[:, blk, e:e + 1], scale=SCALE, accum_out=m_sum[:, blk, e:e + 1])
                last.then_inc(S.free[b], 1)

            def mem_weights(part, t, blk, mc):
                from_t(part, t, f"ptm{blk}{mc}", big[:, mc * 4:mc * 4 + 4, blk * P:(blk + 1) * P],
                       ps_t[:, :].rearrange("p (e n) -> p e n", e=4))

            def sample_mem(part):
                b = S.wait_full(act, part, 0, "m")
                act.wait_ge(m_neg_in.sem, m_neg_in.after(part, 0))
                for half in range(2):
                    last = f(pm[:, 0, half, :], ps_s[:, b, 0, half * NMEM:(half + 1) * NMEM], ACT.Exp,
                             bias=m_neg[:, 0, half:half + 1], scale=SCALE, accum_out=m_sum[:, 0, half:half + 1])
                last.then_inc(S.free[b], 1)

            def sample_weights(part):
                for mc in range(MC):
                    from_t(part, 0, f"pt{mc}", pt_s[:, mc, :], ps_t[:, 0:NMEM])

            def sample_out(part, half):
                b = Z.wait_full(act, part, 0, f"out{half}")
                f(scr[0:NS, b, :], ps_z[0:NS, b, :], ACT.Copy).then_inc(Z.free[b], 1)

            def to_blocks(out, c, par, src):
                rows = slice(par * HD, (par + 1) * HD)
                h = 2 * c + par
                return f(out[rows, c, :, h * DS:(h + 1) * DS], src[rows, :].rearrange("p (b t) -> p b t", b=DB),
                         ACT.Copy)

            def magnitudes(part, t, k, src, beside):
                act.wait_ge(w_gained.sem, w_gained.after(part, t, k))
                if beside.dtype != BF16:
                    beside = beside.bitcast(BF16)
                f(beside, src, ACT.Abs, accum_out=w_top[:, k % 2:k % 2 + 1]).then_inc(top_sum.sem, 1)

            def memory_keys(l):
                from_t("pre", 0, f"kt{l}", kT_mem[l], ps_t[:, :].rearrange("p (c n) -> p c n", c=2))

            def start(g):
                magnitudes("pre", 0, g, stage_a[g % 3], first_parts[g][:, 0])

            def end(g):
                high("pre", 0, g, first_parts[g][:, 0], stage_a[g % 3])

            squares_x("pre", 0, 0, 1, 16)
            squares_kv("pre", 0, "mem00", v_mem[0][:, 0, :])
            squares_kv("pre", 0, "mem01", v_mem[0][:, 1, :])
            start(0)
            squares_kv("pre", 0, "mem10", v_mem[1][:, 0, :])
            start(1)
            end(0)
            squares_kv("pre", 0, "mem11", v_mem[1][:, 1, :])
            memory_keys(0)
            start(2)
            end(1)
            memory_keys(1)
            start(3)
            squares_x("pre", 0, 1, 0, 16)
            end(2)
            for g in range(4, 10):
                start(g)
                end(g - 1)
                if g == 5:
                    x_high("pre", 0)
            end(9)

            def ua(g):
                return unit_a[:, g:g + 1]

            def ub(g):
                return unit_b[:, g:g + 1]

            with act.Fori(0, TILES // 2) as it:
                for p in range(2):
                    t = it * 2 + p
                    squares_heads("A", t, "qm", (ua(0),)).then_inc(scr_in.sem, 1)
                    act.wait_ge(u_free.sem, u_free.after("A", t, -1))
                    for i in range(3):
                        b = Z.wait_full(act, "A", t, f"u{i}")
                        f(u[:, 2 * i:2 * i + 2, 16:UW], ps_z[:, b].rearrange("p (c n) -> p c n", c=2), ACT.Copy,
                          scale=ua(1 + i))\
                            .then_inc(Z.free[b], 1)
                    from_t("A", t, "qT", qT_a[:, :, :], ps_t[:, :].rearrange("p (c n) -> p c n", c=2))
                    mem_exps("A", t, 0)
                    mem_exps("A", t, 1)
                    tanh("A", t, "g0", halfunit_a[:, 4:5])
                    mem_weights("A", t, 0, 0)
                    mem_weights("A", t, 0, 1)
                    tanh("A", t, "g1", halfunit_a[:, 5:6])
                    mem_weights("A", t, 1, 0)
                    mem_weights("A", t, 1, 1)
                    tanh("A", t, "g2", halfunit_a[:, 6:7])
                    magnitudes("A", t, 0, stage_b, scratch_b)
                    V.wait_full(act, "A", t, "pvm")
                    squares_x("A", t, 0, 1 - p, it * 16 + 32)
                    tanh("A", t, "gm", halfunit_a[:, 7:8])
                    high_b("A", t, 0)
                    x_high("A", t)

            act.wait_ge(u_free.sem, u_free.after("A", TILES - 1))
            nc.scalar.dma_start(io["pool_p"], u[:, :, 1:16]).then_inc(state_out, 16)
            nc.scalar.dma_start(state_tmp, io["state"]).then_inc(state_in, 16)
            squares_heads("SA", 0, "qm", (ua(0),), NS, 256).then_inc(scr_in.sem, 1)
            act.wait_ge(state_set, 1)
            for i in range(3):
                b = Z.wait_full(act, "SA", 0, f"u{i}")
                for c in range(2):
                    last = f(by_batch(u[:, 2 * i + c])[:, :, 16:US],
                             ps_z[:, b, c * NT:c * NT + NS].rearrange("p (b t) -> p b t", b=DB), ACT.Copy,
                             scale=ua(1 + i))
                last.then_inc(Z.free[b], 1)
            act.wait_ge(qbd_zero.sem, qbd_zero.after("SA", 0))
            T.wait_full(act, "SA", 0, "qT")
            for c in range(2):
                for par in range(2):
                    last = to_blocks(qbd_a, c, par, ps_t[:, c * NS:(c + 1) * NS])
            last.then_inc(T.free[0], 1)
            sample_mem("SA")
            act.wait_ge(parts_out.sem, parts_out.total)
            for g in range(4):
                nc.scalar.dma_start(w_split[:, g], io["parts"][g]).then_inc(win_in[g], 16)
            for i, g in enumerate((*G3, "gm")):
                tanh("SA", 0, g, halfunit_a[:, 4 + i:5 + i], NS)
            sample_weights("SA")
            V.wait_full(act, "SA", 0, "pvm")
            squares_x("SA", 0, 0, 1, 16 * 6)
            Z.wait_full(act, "SA", 0, "mix2")
            for g in (7, 4, 5, 6):
                nc.scalar.dma_start(w_split[:, g], io["parts"][g]).then_inc(win_in[g], 16)
            sample_out("SA", 0)
            x_high("SA", 0)
            sample_out("SA", 1)

            def window_exps(t, n):
                act.wait_ge(w_neg_in.sem, w_neg_in.after("B", t, n))
                for e in range(4):
                    f(sw[:, n % 2, e, :], sw[:, n % 2, e, :], ACT.Exp, bias=w_neg[:, n % 2, e:e + 1], scale=SCALE,
                      accum_out=w_sum[:, n % 2, e:e + 1])
                f(w_se[:, n % 2, :], w_sd[:, n % 2, :], ACT.Exp).then_inc(w_exp.sem, 1)

            with act.Fori(0, TILES // 2) as it:
                for p in range(2):
                    t = it * 2 + p
                    for blk in range(NBLK):
                        squares_kv("B", t, f"kv{blk}", v[:, 2 * p + blk, :], (ub(8), ub(9)))
                    squares_heads("B", t, "qa0", (ub(0), ub(1))).then_inc(scr_in.sem, 1)
                    squares_heads("B", t, "qb0", (ub(2), ub(3))).then_inc(scr_in.sem, 1)
                    from_t("B", t, "kT", kT[:, :, 2 * p:2 * p + 2, :],
                           ps_t[:, :].rearrange("p (k b n) -> p k b n", k=2, b=NBLK))

                    def queries(blk, half):
                        from_t("B", t, f"qT{blk}{half}", qT_b[:, half * 4:half * 4 + 4, blk * P:(blk + 1) * P],
                               ps_t[:, :].rearrange("p (c n) -> p c n", c=4))
                    squares_heads("B", t, "qa1", (ub(0), ub(1))).then_inc(scr_in.sem, 1)
                    squares_heads("B", t, "qb1", (ub(2), ub(3))).then_inc(scr_in.sem, 1)
                    queries(0, 0)
                    queries(0, 1)
                    tanh("B", t, "gm", halfunit_b[:, 7:8])
                    mem_exps("B", t, 0)
                    queries(1, 0)
                    window_exps(t, 0)
                    queries(1, 1)
                    window_exps(t, 1)
                    tanh("B", t, "g0", halfunit_b[:, 4:5])
                    mem_exps("B", t, 1)
                    mem_weights("B", t, 0, 0)
                    window_exps(t, 2)
                    mem_weights("B", t, 0, 1)
                    tanh("B", t, "g1", halfunit_b[:, 5:6])
                    mem_weights("B", t, 1, 0)
                    window_exps(t, 3)
                    mem_weights("B", t, 1, 1)
                    window_exps(t, 4)
                    window_exps(t, 5)
                    tanh("B", t, "g2", halfunit_b[:, 6:7])
                    squares_x("B", t, 0, p, (it + 6 + p) * 16)
                    x_high("B", t)

            squares_kv("SB", 0, "kv0", v[0:NS, 0, :], (ub(8), ub(9)), NS)
            squares_heads("SB", 0, "qa0", (ub(0), ub(1)), NS).then_inc(scr_in.sem, 1)
            squares_heads("SB", 0, "qb0", (ub(2), ub(3)), NS).then_inc(scr_in.sem, 1)
            for g, k in (("gm", 7), ("g0", 4), ("g1", 5), ("g2", 6)):
                tanh("SB", 0, g, halfunit_b[:, k:k + 1], NS)
            from_t("SB", 0, "kT", kT_new, ps_t[:, 0:2 * NS].rearrange("p (k t) -> p k t", k=2))
            act.wait_ge(qbd_zero.sem, qbd_zero.after("SB", 0))
            for half in range(2):
                T.wait_full(act, "SB", 0, f"qT0{half}")
                for j in range(4):
                    for par in range(2):
                        c = half * 4 + j
                        src = ps_t[:, j * NS:(j + 1) * NS]
                        if c < POOLC:
                            rows = slice(par * HD, (par + 1) * HD)
                            at = (c // 3) * 48 + par * 24 + (c % 3) * DS
                            last = f(qbd_w[rows, c // 3, :, at:at + DS],
                                     src[rows, :].rearrange("p (b t) -> p b t", b=DB), ACT.Copy)
                        else:
                            last = to_blocks(qbd_b, c - POOLC, par, src)
                last.then_inc(T.free[0], 1)
            act.wait_ge(w_neg_in.sem, w_neg_in.after("SB", 0))
            for n in range(DB):
                f(sw_s[:, n, :], sw_s[:, n, :], ACT.Exp, bias=s_neg[:, n:n + 1], scale=SCALE,
                  accum_out=s_sum[:, n:n + 1])
            f(s_se, s_sd, ACT.Exp).then_inc(w_exp.sem, 1)
            sample_mem("SB")
            sample_weights("SB")
            sample_out("SB", 0)
            sample_out("SB", 1)

        @block.vector
        def _(dve):
            ve = nc.vector
            own = Steps(dve, dves)

            def x_variance(ring, part, t, name):
                b = ring.wait_full(dve, part, t, name)
                src = (ps_t if ring is T else ps_p)[:, 0:2]
                ve.tensor_scalar(x_var, src, 1.0 / D, EPS, ALU.mult, ALU.add).then_inc(ring.free[b], 1)

            def diagonals(part, t, k, scale=X_UNIT):
                dve.wait_ge(rstd_x.sem, rstd_x.after(part, t, k))
                for blk in range(NBLK):
                    last = ve.tensor_scalar(diag[:, blk, :], ident, x_rstd[:, blk:blk + 1], scale, ALU.mult, ALU.mult)
                last.then_inc(diag_x.sem, 1)

            def normalise_memory(xb):
                b = Z.wait_full(dve, "pre", 0, "rb_mem")
                for g, dst in ((3, xn), (4, x_buf[:, xb])):
                    for kc in range(KC):
                        last = ve.scalar_tensor_tensor(dst[:, kc, :], x_buf[:, xb, kc, :],
                                                       gain[:, g, kc:kc + 1], ps_z[:, b, 0:NT],
                                                       ALU.mult, ALU.mult)
                last.then_inc(Z.free[b], 1)

            def normalise(part, t, xb):
                ring = V if part == "B" else Z
                b = ring.wait_full(dve, part, t, "rb")
                row_ = (ps_p[:, 0:NT] if part == "B" else ps_z[:, b, 0:NT])\
                    .rearrange("p (k n) -> p k n", k=1).to_broadcast([P, KC, NT])
                ve.tensor_tensor(big[:, :, :], x_buf[:, xb], row_, ALU.mult).then_inc(ring.free[b], 1)

            def x_low(part, t):
                dve.wait_ge(xhigh_in.sem, xhigh_in.after(part, t))
                ve.tensor_tensor(xs[:, 1], big[:, :, :], xs[:, 0], ALU.subtract).then_inc(xlow_in.sem, 1)

            def weight_top(part, t, k):
                dve.wait_ge(top_sum.sem, top_sum.after(part, t, k))
                ve.tensor_scalar(top_diag[:, k % 2], ident, w_top[:, k % 2:k % 2 + 1], None, ALU.mult).then_inc(top_in.sem, 1)

            def weight_scale(part, t, k, name, unit):
                T.wait_full(dve, part, t, name)
                power2 = w_power[:, k % 2:k % 2 + 1]
                own(ve.tensor_reduce(power2, ps_t[:, 0:P], AX.X, ALU.max))
                own.wait()
                ve.tensor_scalar(power2, power2, 2.0 ** -100, None, ALU.max).then_inc(T.free[0], 1)
                T.wait_read(dve, part, t, name)
                bits = power2.bitcast(I32)
                own(ve.tensor_scalar(bits, bits, 0x7F800000, None, ALU.bitwise_and))
                own.wait()
                own(ve.tensor_scalar(unit, power2, 2.0 ** -14 / X_UNIT, None, ALU.mult))
                own(ve.reciprocal(power2, power2))
                own.wait()
                ve.tensor_scalar(w_scale[:, k % 2:k % 2 + 1], power2, 2.0 ** 14, None, ALU.mult)\
                    .then_inc(scale_in.sem, 1)

            def low(part, t, k, n, dst, high_, src):
                dve.wait_ge(high_in.sem, high_in.after(part, t, n))
                ve.scalar_tensor_tensor(dst, src, w_scale[:, k % 2:k % 2 + 1], high_, ALU.mult, ALU.subtract)\
                    .then_inc(low_in.sem, 1)

            def low_b(part, t, k, half):
                low(part, t, k, 2 * k + half, parts_b[half][:, 1], parts_b[half][:, 0],
                    stage_b[:, half * 4:half * 4 + 4, :])

            def head_group(part, t, name, k, ss, parts, n=P):
                dve.wait_ge(scr_in.sem, scr_in.after(part, t, k))
                b = Z.bank(part, name)
                heads = ss.shape[1]
                own(ve.tensor_reduce(ss, scr[0:n, b, 0:heads * HD].rearrange("p (h d) -> p h d", h=heads),
                                     AX.X, ALU.add))
                for dst, at, h, r in parts:
                    last = ve.tensor_tensor(dst, ps_z[0:n, b, at:at + h * HD].rearrange("p (h d) -> p h d", h=h),
                                            row(r, h, n), ALU.mult)
                last.then_inc(Z.free[b], 1)

            def variance(ss, rstd):
                own.wait()
                return ve.tensor_scalar(rstd, ss, 1.0 / HD, EPS, ALU.mult, ALU.add)

            def rotate(x, heads, cos, sin, n=P):
                def along(a):
                    w = a.shape[1]
                    return a.rearrange("p (h d) -> p h d", h=1).to_broadcast([n, heads, w])
                half = 8
                own.wait()
                ve.tensor_tensor(rot[0:n, 0:heads, 0:half], x[:, :, half:16], along(sin[:, 0:half]), ALU.mult)
                own(ve.tensor_tensor(rot[0:n, 0:heads, half:16], x[:, :, 0:half], along(sin[:, half:16]), ALU.mult))
                own.wait()
                own(ve.tensor_tensor(x[:, :, 0:16], x[:, :, 0:16], along(cos), ALU.mult))
                own.wait()
                return ve.tensor_tensor(x[:, :, 0:16], x[:, :, 0:16], rot[0:n, 0:heads, :], ALU.add)

            def mem_max(part, t, blk):
                b = S.wait_full(dve, part, t, f"m{blk}")
                own(ve.tensor_reduce(m_max[:, blk, :].rearrange("p (r c) -> p r c", r=2),
                                     ps_s[:, b].rearrange("p r (c m) -> p r c m", c=2), AX.X, ALU.max))
                own.wait()
                ve.tensor_scalar(m_neg[:, blk, :], m_max[:, blk, :], -SCALE, None, ALU.mult)\
                    .then_inc(m_neg_in.sem, 1)

            def mem_inverse(part, t, blk):
                S.wait_read(dve, part, t, f"m{blk}")
                ve.reciprocal(m_inv[:, blk, :], m_sum[:, blk, :]).then_inc(m_inv_in.sem, 1)

            def silu(part, t, name, k, c, n=NT):
                dve.wait_ge(scr_in.sem, scr_in.after(part, t, k))
                b = Z.bank(part, name)
                pair = [x[:, b].rearrange("p (c n) -> p c n", c=2)[:, :, 0:n] for x in (scr, ps_z)]
                ve.scalar_tensor_tensor(gate[:, c:c + 2, 0:n], pair[0], 1.0, pair[1], ALU.add, ALU.mult)\
                    .then_inc(Z.free[b], 1)

            def mem_gated(part, t):
                V.wait_full(dve, part, t, "pvm")
                Z.wait_read(dve, part, t, "gm")
                ve.scalar_tensor_tensor(gate[:, 6:8, :], ps_p[:, :].rearrange("p (c n) -> p c n", c=2),
                                        (halfunit_a if part == "A" else halfunit_b)[:, 7:8], gate[:, 6:8, :], ALU.mult, ALU.mult).then_inc(V.free[0], 1)

            def mix_gated(part, t, n=NT):
                Z.wait_read(dve, part, t, "g1")
                Z.wait_read(dve, part, t, "g2")
                for i in range(3):
                    b = Z.wait_full(dve, part, t, f"mix{i}")
                    for c in (2 * i, 2 * i + 1):
                        src = ps_z[:, b, (c % 2) * NT:(c % 2) * NT + n]
                        last = ve.scalar_tensor_tensor(gate[:, c, 0:n], src, mix_scale[:, c:c + 1],
                                                       gate[:, c, 0:n], ALU.mult, ALU.mult)
                    last.then_inc(Z.free[b], 1)

            def add_sample_outputs(part, xb, half):
                T.wait_full(dve, part, 0, f"ot{half}")
                x = x_buf[:, xb, 4 * half:4 * half + 4, 0:NS]
                ve.tensor_tensor(x, x, ps_t[:, 0:4 * NS].rearrange("p (c n) -> p c n", c=4), ALU.add)\
                    .then_inc(T.free[0], 1)

            def add_outputs(part, t, xb, groups, n=NT):
                for g in groups:
                    b = Z.wait_full(dve, part, t, f"out{g}")
                    x = x_buf[:, xb, 2 * g:2 * g + 2, 0:n]
                    ve.tensor_tensor(x, x, ps_z[:, b].rearrange("p (c n) -> p c n", c=2)[:, :, 0:n], ALU.add)\
                        .then_inc(Z.free[b], 1)

            ve.memset(tiny[:, 56:57], 0.0).then_inc(S.free[0], 1)
            ve.memset(tiny[:, 57:58], 0.0).then_inc(S.free[1], 1)
            ve.memset(tiny[:, 58:59], 0.0).then_inc(V.free[0], 1)
            dve.wait_ge(small_in, 16)

            def start(g):
                weight_top("pre", 0, g)

            def scale(g):
                weight_scale("pre", 0, g, f"top{g}", unit_a[:, g:g + 1] if g < 8 else unit_b[:, g:g + 1])

            def end(g):
                low("pre", 0, g, g, first_parts[g][:, 1], first_parts[g][:, 0], stage_a[g % 3])

            def memory_heads(l, blk):
                head_group("pre", 0, f"mem{l}{blk}", 2 * l + blk, k_ss[:, blk * 4:(blk + 1) * 4],
                           [(k_mem[l][:, blk, :].rearrange("p (h d) -> p h d", h=4), 0, 4, ROW_MEMK + l)])
                if blk:
                    variance(k_ss, k_rstds[l]).then_inc(heads_var.sem, 1)

            x_variance(T, "pre", 0, "ss_mem")
            diagonals("pre", 0, 0, 1.0)
            normalise_memory(1)
            memory_heads(0, 0)
            memory_heads(0, 1)
            start(0)
            dve.wait_ge(heads_var.sem, heads_var.after("pre", 0, 0))
            memory_heads(1, 0)
            scale(0)
            start(1)
            end(0)
            memory_heads(1, 1)
            scale(1)
            start(2)
            end(1)
            scale(2)
            start(3)
            end(2)
            scale(3)
            x_variance(T, "pre", 0, "ss")
            for g in range(4, 10):
                start(g)
                if g == 9:
                    own(ve.tensor_scalar(halfunit_a, unit_a, 0.5, None, ALU.mult))
                    own.wait()
                    for c in range(POOLC):
                        own(ve.tensor_scalar(mix_scale[:, c:c + 1], pscale[:, c:c + 1],
                                             halfunit_a[:, 4 + c // 2:5 + c // 2], None, ALU.mult))
                scale(g)
                end(g - 1)
                if g == 4:
                    diagonals("pre", 0, 1)
                if g == 5:
                    normalise("pre", 0, 0)
                if g == 7:
                    x_low("pre", 0)
            end(9)
            dve.wait_ge(low_in.sem, low_in.after("pre", 0, 9))
            ve.memset(u[:, :, 0:16], 0.0).then_inc(u_free.sem, 1)
            dve.wait_ge(outputs, 4 * 16)
            dve.wait_ge(x_stored.sem, x_stored.after("pre", 0))

            def window_differences(t):
                dve.wait_ge(win_sums.sem, win_sums.after("A", t))
                own(ve.tensor_tensor(win_a[:, 0:4:3, 16:32], win_a[:, 0:4:3, 16:32], corr[:, 0:4:3, :], ALU.mult))
                own(ve.tensor_tensor(win_b[:, 1:6, 16:32], win_b[:, 1:6, 16:32], corr[:, 1:6, :], ALU.mult))
                own.wait()
                own(ve.memset(corr, 1.0))
                for c in range(POOLC):
                    last = ve.scalar_tensor_tensor(pooled(c)[:, 16:UW], pooled(c)[:, 16:UW], invw[:, c:c + 1],
                                                   u[:, c, 16:UW], ALU.mult, ALU.subtract)
                last.then_inc(d_in.sem, 1)
                dve.wait_ge(d_in.sem, d_in.after("A", t))
                ve.tensor_copy(u[:, :, 0:16], u[:, :, NT:UW]).then_inc(u_free.sem, 1)

            own.loop(1 + 2 + 3 + 4)
            with dve.Fori(0, TILES // 2) as it:
                for p in range(2):
                    t = it * 2 + p
                    own.tile(t)
                    head_group("A", t, "qm", 0, q_ss[:, 0:8], [(q_of(0)[:, 0:8, :], 0, 8, ROW_MEMQ)])
                    variance(q_ss[:, 0:8], q_rstds[0][:, 0:8]).then_inc(heads_var.sem, 1)
                    for blk in range(NBLK):
                        mem_max("A", t, blk)
                    for blk in range(NBLK):
                        mem_inverse("A", t, blk)
                    dve.wait_ge(parts_out.sem, parts_out.after("pre", 0, 1))
                    silu("A", t, "g0", 1, 0)
                    silu("A", t, "g1", 2, 2)
                    window_differences(t)
                    silu("A", t, "g2", 3, 4)
                    silu("A", t, "gm", 4, 6)
                    weight_top("A", t, 0)
                    mem_gated("A", t)
                    mix_gated("A", t)
                    weight_scale("A", t, 0, "top0", unit_b[:, bass.ds(t, 1)])
                    add_outputs("A", t, p, (0,))
                    x_variance(T, "A", t, "ss")
                    diagonals("A", t, 0)
                    low_b("A", t, 0, 0)
                    add_outputs("A", t, p, (1,))
                    low_b("A", t, 0, 1)
                    normalise("A", t, 1 - p)
                    add_outputs("A", t, p, (2,))
                    x_low("A", t)
                    add_outputs("A", t, p, (3,))
            own.end_loop(TILES)

            def sample_mem_max(part):
                b = S.wait_full(dve, part, 0, "m")
                own(ve.tensor_reduce(m_max[:, 0, 0:2], ps_s[:, b, 0].rearrange("p (c m) -> p c m", c=2),
                                     AX.X, ALU.max))
                own.wait()
                ve.tensor_scalar(m_neg[:, 0, 0:2], m_max[:, 0, 0:2], -SCALE, None, ALU.mult)\
                    .then_inc(m_neg_in.sem, 1)

            def sample_mem_inverse(part):
                S.wait_read(dve, part, 0, "m")
                ve.reciprocal(m_inv[:, 0, 0:2], m_sum[:, 0, 0:2]).then_inc(m_inv_in.sem, 1)

            def sample_mem_gated(part):
                V.wait_full(dve, part, 0, "pvm")
                Z.wait_read(dve, part, 0, "gm")
                values = ps_p[:, 0:NMEM].rearrange("p (b c r t) -> p b c r t", b=DB, c=2, r=2)
                for par in range(2):
                    rows = slice(par * HD, (par + 1) * HD)
                    for c in range(2):
                        g = gate[rows, 6 + c, 0:NS].rearrange("p (b t) -> p b t", b=DB)
                        last = ve.scalar_tensor_tensor(g, values[rows, :, c, par, :],
                                                       (halfunit_a if part == "SA" else halfunit_b)[rows, 7:8], g,
                                                       ALU.mult, ALU.mult)
                last.then_inc(V.free[0], 1)

            dve.wait_ge(state_in, 16)
            dve.wait_ge(state_out, 16)
            for c in range(POOLC):
                last = ve.tensor_copy(by_batch(u[:, c])[:, :, 1:16], state_tmp[:, c])
            last.then_inc(state_set, 1)
            head_group("SA", 0, "qm", 0, q_ss[0:NS, 0:4], [(q_of(0)[0:NS, 0:4, :], 0, 4, ROW_MEMQ)], NS)
            variance(q_ss[0:NS, 0:4], q_rstds[0][0:NS, 0:4]).then_inc(heads_var.sem, 1)
            ve.memset(qbd_a, 0.0).then_inc(qbd_zero.sem, 1)
            Z.wait_read(dve, "SA", 0, "u2")
            Z.wait_read(dve, "SA", 0, "u1")
            for c in range(POOLC):
                last = ve.tensor_copy(state_tmp[:, c], by_batch(u[:, c])[:, :, US - PAD:US])
            last.then_inc(pool_out, 1)
            sample_mem_max("SA")
            sample_mem_inverse("SA")
            silu("SA", 0, "g0", 1, 0, NS)
            silu("SA", 0, "g1", 2, 2, NS)
            dve.wait_ge(win_sums.sem, win_sums.after("SA", 0))
            for c in range(POOLC):
                w_, u_ = (by_batch(x)[:, :, 16:US] for x in (pooled(c), u[:, c]))
                last = ve.scalar_tensor_tensor(w_, w_, invw[:, c:c + 1], u_, ALU.mult, ALU.subtract)
            last.then_inc(d_in.sem, 1)
            silu("SA", 0, "g2", 3, 4, NS)
            silu("SA", 0, "gm", 4, 6, NS)
            sample_mem_gated("SA")
            mix_gated("SA", 0, NS)
            x_variance(T, "SA", 0, "ss")
            diagonals("SA", 0, 0)
            add_sample_outputs("SA", 0, 0)
            normalise("SA", 0, 1)
            x_low("SA", 0)
            add_sample_outputs("SA", 0, 1)
            own(ve.tensor_scalar(halfunit_b, unit_b[:, 0:8], 0.5, None, ALU.mult))
            for g in range(4):
                own(ve.tensor_copy(unit_heads[:, 4 * g:4 * g + 4], unit_b[:, g:g + 1].to_broadcast([P, 4])))
            own(ve.tensor_copy(k_unit, unit_b[:, 8:9].to_broadcast([P, 8])))
            own(ve.memset(kT[:, :, 3, :], 0.0))
            own(ve.memset(v[:, 3, :], 0.0))
            own.wait()
            dve.wait_ge(state_out, 32)

            def k_heads(part, t, blk, at, n=P):
                head_group(part, t, f"kv{blk}", blk, k_ss[0:n, blk * 4:(blk + 1) * 4],
                           [(k_tok[0:n, blk], 0, 4, ROW_K)], n)

            def q_heads(part, t, blk, cos, sin, n=P):
                k = (2 if part == "B" else 1) + 2 * blk
                q = q_of(blk)[0:n]
                dve.wait_ge(heads_var.sem, heads_var.after(part, t, blk))
                head_group(part, t, f"qa{blk}", k, q_ss[0:n, 0:8], [(q[:, 0:8], 0, 8, ROW_Q)], n)
                head_group(part, t, f"qb{blk}", k + 1, q_ss[0:n, 8:16],
                           [(q[:, 8:12], 0, 4, ROW_Q), (q[:, 12:16], 4 * HD, 4, ROW_MEMQ + 1)], n)
                own(variance(q_ss[0:n], q_rstds[blk][0:n]))
                Z.wait_read(dve, part, t, f"qb{blk}")
                Z.wait_read(dve, part, t, f"qa{blk}")
                rotate(q[:, 0:12], 12, cos, sin, n).then_inc(heads_var.sem, 1)

            def window_front(t, i):
                blk, gi = W6[i]
                b = S.wait_full(dve, "B", t, f"w{i}")
                prev, n = ("prev_now", "prev_hi")[blk], i % 2
                scores = ps_s[:, b].rearrange("p r (c j n) -> p r c j n", c=2, j=2)

                def across(a):
                    return a.rearrange("p (r c n) -> p r c n", r=1, c=1).to_broadcast([P, 2, 2, BLK])

                def heads(a):
                    return a.rearrange("p (r c) n -> p r c n", r=2)
                own(ve.tensor_tensor(heads(lo[:, :, :]), scores[:, :, :, 1, :], across(sm("cur_hi")), ALU.min))
                ve.tensor_tensor(heads(sw[:, n]), scores[:, :, :, 0, :], across(sm(prev)), ALU.min)\
                    .then_inc(S.free[b], 1)
                S.wait_read(dve, "B", t, f"w{i}")
                own(ve.tensor_tensor(sw[:, n], sw[:, n], lo[:, :, :], ALU.max))
                own.wait()
                own(ve.tensor_reduce(w_max[:, n, :], sw[:, n], AX.X, ALU.max))
                own.wait()
                sinks = sm("sink")[:, gi * 4:gi * 4 + 4]
                own(ve.scalar_tensor_tensor(w_max[:, n, :], w_max[:, n, :], SCALE, sinks, ALU.mult, ALU.max))
                own.wait()
                ve.tensor_tensor(w_sd[:, n, :], sinks, w_max[:, n, :], ALU.subtract)
                ve.tensor_scalar(w_neg[:, n, :], w_max[:, n, :], -1.0, None, ALU.mult).then_inc(w_neg_in.sem, 1)
                if i == 4:
                    own(ve.tensor_copy(sm("prev_now"), sm("prev_hi")))
                    own.wait()

            def window_back(t, n):
                i = n % 2
                dve.wait_ge(w_exp.sem, w_exp.after("B", t, n))
                own(ve.tensor_tensor(w_sum[:, i, :], w_sum[:, i, :], w_se[:, i, :], ALU.add))
                own.wait()
                ve.reciprocal(w_inv[:, i, :], w_sum[:, i, :]).then_inc(w_inv_in.sem, 1)

            def window_weights(t, n):
                T.wait_full(dve, "B", t, f"ptw{n}")
                src = ps_t[:, :].rearrange("p (e n) -> p e n", e=4)
                for dst, mask in ((ptc, "curT"), (ptp, "prevT")):
                    m = sm(mask).rearrange("p (e n) -> p e n", e=1).to_broadcast([P, 4, BLK])
                    last = ve.tensor_tensor(dst, src, m, ALU.mult)
                last.then_inc(T.free[0], 1)

            def window_gated(t, n):
                blk, gi = W6[n]
                V.wait_full(dve, "B", t, f"pvw{n}")
                if blk == 0:
                    Z.wait_read(dve, "B", t, f"g{gi}")
                g = gate[:, 2 * gi:2 * gi + 2, blk * P:(blk + 1) * P]
                ve.scalar_tensor_tensor(g, ps_p[:, 0:2 * P].rearrange("p (c n) -> p c n", c=2),
                                        halfunit_b[:, 4 + gi:5 + gi], g, ALU.mult, ALU.mult).then_inc(V.free[0], 1)

            own.loop(NBLK * (4 + 5) + 2 + 6 * 5 + 1)
            with dve.Fori(0, TILES // 2) as it:
                for p in range(2):
                    t = it * 2 + p
                    own.tile(t)

                    def angles(name, blk):
                        return sm(name)[:, bass.ds((t * NBLK + blk) * 16, 16)]
                    for blk in range(NBLK):
                        k_heads("B", t, blk, None)
                        Z.wait_read(dve, "B", t, f"kv{blk}")
                        own(rotate(k_tok[:, blk], 4, angles("cos", blk), angles("sin", blk)))
                    variance(k_ss, k_rstds[0]).then_inc(heads_var.sem, 1)
                    for blk in range(NBLK):
                        q_heads("B", t, blk, angles("cos", blk), angles("sin", blk))
                    mem_max("B", t, 0)
                    window_front(t, 0)
                    silu("B", t, "gm", 6, 6)
                    mem_inverse("B", t, 0)
                    window_back(t, 0)
                    window_front(t, 1)
                    mem_max("B", t, 1)
                    window_weights(t, 0)
                    window_back(t, 1)
                    window_front(t, 2)
                    silu("B", t, "g0", 7, 0)
                    mem_inverse("B", t, 1)
                    window_gated(t, 0)
                    window_back(t, 2)
                    window_weights(t, 1)
                    silu("B", t, "g1", 8, 2)
                    window_front(t, 3)
                    window_gated(t, 1)
                    window_back(t, 3)
                    window_weights(t, 2)
                    mem_gated("B", t)
                    window_front(t, 4)
                    window_gated(t, 2)
                    window_weights(t, 3)
                    window_back(t, 4)
                    window_front(t, 5)
                    window_gated(t, 3)
                    window_weights(t, 4)
                    window_back(t, 5)
                    silu("B", t, "g2", 9, 4)
                    window_gated(t, 4)
                    window_weights(t, 5)
                    window_gated(t, 5)
                    add_outputs("B", t, 1 - p, (0,))
                    x_variance(V, "B", t, "ss")
                    diagonals("B", t, 0)
                    add_outputs("B", t, 1 - p, (1,))
                    normalise("B", t, p)
                    add_outputs("B", t, 1 - p, (2,))
                    x_low("B", t)
                    add_outputs("B", t, 1 - p, (3,))
            own.end_loop(TILES)

            k_heads("SB", 0, 0, None, NS)
            Z.wait_read(dve, "SB", 0, "kv0")
            own(rotate(k_tok[0:NS, 0], 4, sm("cos_s")[0:NS], sm("sin_s")[0:NS], NS))
            variance(k_ss[0:NS, 0:4], k_rstds[0][0:NS, 0:4]).then_inc(heads_var.sem, 1)
            q_heads("SB", 0, 0, sm("cos_s")[0:NS], sm("sin_s")[0:NS], NS)
            silu("SB", 0, "gm", 3, 6, NS)
            silu("SB", 0, "g0", 4, 0, NS)
            ve.memset(w_flat[:, 0:2048], 0.0).then_inc(qbd_zero.sem, 1)
            silu("SB", 0, "g1", 5, 2, NS)
            silu("SB", 0, "g2", 6, 4, NS)
            b = S.wait_full(dve, "SB", 0, "wn")
            new_hi, old_hi = (sm(x)[0:96].rearrange("p (b t) -> p b t", b=1).to_broadcast([96, DB, DS])
                              for x in ("new_hi", "old_hi"))
            ve.tensor_tensor(lo_s, ps_s[0:96, b, 0, 0:NS].rearrange("p (b t) -> p b t", b=DB), new_hi, ALU.min)\
                .then_inc(S.free[b], 1)
            b = S.wait_full(dve, "SB", 0, "wc")
            ve.tensor_copy(sw_s.rearrange("p (r b) t -> p r (b t)", r=2), ps_s[0:96, b]).then_inc(S.free[b], 1)
            S.wait_read(dve, "SB", 0, "wc")
            S.wait_read(dve, "SB", 0, "wn")
            first = sw_s[:, :, 0:DS]
            own(ve.tensor_tensor(first, first, old_hi, ALU.min))
            own.wait()
            own(ve.tensor_tensor(first, first, lo_s, ALU.max))
            own.wait()
            own(ve.tensor_reduce(s_max, sw_s, AX.X, ALU.max))
            own.wait()
            sink = sm("sinkcol")[0:96]
            own(ve.tensor_scalar(s_max, s_max, SCALE, sink, ALU.mult, ALU.max))
            own.wait()
            ve.tensor_scalar(s_sd, s_max, -1.0, sink, ALU.mult, ALU.add)
            ve.tensor_scalar(s_neg, s_max, -1.0, None, ALU.mult).then_inc(w_neg_in.sem, 1)
            dve.wait_ge(w_exp.sem, w_exp.after("SB", 0))
            own(ve.tensor_tensor(s_sum, s_sum, s_se, ALU.add))
            own.wait()
            ve.reciprocal(s_inv, s_sum).then_inc(w_inv_in.sem, 1)
            sample_mem_max("SB")
            sample_mem_inverse("SB")
            for half in range(2):
                T.wait_full(dve, "SB", 0, f"ptw{half}")
                some = slice(half * 4, half * 4 + 4)
                for dst, name, rows in ((pt_old, "oldT", P), (pt_new, "newT", DS)):
                    m = sm(name)[0:rows].rearrange("p (b n) -> p b n", b=1).to_broadcast([rows, 4, 96])
                    last = ve.tensor_tensor(dst[:, some, :], ps_t[0:rows, 0:384].rearrange("p (b n) -> p b n", b=4),
                                            m, ALU.mult)
                last.then_inc(T.free[0], 1)
            for kp in range(2):
                V.wait_full(dve, "SB", 0, f"pvw{kp}")
                values = ps_p[:, 0:384].rearrange("p (b n) -> p b n", b=DB)
                for par in range(2):
                    rows = slice(par * HD, (par + 1) * HD)
                    for g in range(3):
                        at = par * 24 + g * DS
                        x = gate[rows, 3 * kp + g, 0:NS].rearrange("p (b t) -> p b t", b=DB)
                        last = ve.scalar_tensor_tensor(x, values[rows, :, at:at + DS],
                                                       halfunit_b[rows, 4 + (3 * kp + g) // 2:5 + (3 * kp + g) // 2], x,
                                                       ALU.mult, ALU.mult)
                last.then_inc(V.free[0], 1)
            sample_mem_gated("SB")
            add_sample_outputs("SB", 1, 0)
            add_sample_outputs("SB", 1, 1)

        @block.gpsimd
        def _(pool):
            tt = nc.gpsimd.tensor_tensor
            own = Steps(pool, pools)

            def rsqrt(out, x):
                n, w = x.shape
                return tt(out, x, power[0:n, 0:w], ALU.pow)

            def sums(part, t, k):
                pool.wait_ge(sq_x.sem, sq_x.after(part, t, k))
                own(tt(big[:, 0:4], big[:, 0:4], big[:, 4:8], ALU.add))
                own.wait()
                own(tt(big[:, 0:2], big[:, 0:2], big[:, 2:4], ALU.add))
                own.wait()
                tt(big[:, 0], big[:, 0], big[:, 1], ALU.add).then_inc(sums_x.sem, 1)

            def rstd(ring, part, t, name):
                ring.wait_read(pool, part, t, name)
                rsqrt(x_rstd, x_var).then_inc(rstd_x.sem, 1)

            def heads(part, t, k, r, x, unit=None):
                pool.wait_ge(heads_var.sem, heads_var.after(part, t, k))
                own(rsqrt(r, r))
                own.wait()
                if unit is not None:
                    own(tt(r, r, unit, ALU.mult))
                    own.wait()
                n, h, d = x.shape
                tt(x, x, r.rearrange("p (h d) -> p h d", d=1).to_broadcast([n, h, d]), ALU.mult)\
                    .then_inc(heads_norm.sem, 1)

            def gained(out, w, g):
                tt(out, w, gain[:, g, :].rearrange("p (k n) -> p k n", n=1).to_broadcast([P, KC, 256]), ALU.mult)\
                    .then_inc(w_gained.sem, 1)

            def mem_norm(part, t, blk):
                pool.wait_ge(m_inv_in.sem, m_inv_in.after(part, t, blk))
                r = m_inv[:, blk, :].rearrange("p (e n) -> p e n", n=1).to_broadcast([P, 4, NMEM])
                tt(pm[:, blk], pm[:, blk], r, ALU.mult).then_inc(pm_norm.sem, 1)

            def sample_mem_norm(part):
                pool.wait_ge(m_inv_in.sem, m_inv_in.after(part, 0))
                r = m_inv[:, 0, 0:2].rearrange("p (e n) -> p e n", n=1).to_broadcast([P, 2, NMEM])
                tt(pm[:, 0, 0:2], pm[:, 0, 0:2], r, ALU.mult).then_inc(pm_norm.sem, 1)

            def windows(u_, a, b_, n):
                own(tt(a(slice(0, 6))[..., 2:n], u_[..., 2:n], u_[..., 1:n - 1], ALU.add))
                own.wait()
                own(tt(b_(slice(1, 6))[..., 4:n], a(slice(1, 6))[..., 4:n], a(slice(1, 6))[..., 2:n - 2], ALU.add))
                own.wait()
                own(tt(a(slice(3, 6))[..., 8:n], b_(slice(3, 6))[..., 8:n], b_(slice(3, 6))[..., 4:n - 4], ALU.add))
                own.wait()
                own(tt(b_(slice(4, 6))[..., 16:n], a(slice(4, 6))[..., 16:n], a(slice(4, 6))[..., 8:n - 8], ALU.add))
                own.wait()

            nc.gpsimd.memset(ones[:, :], 1.0).then_inc(consts, 1)
            nc.gpsimd.memset(power, -0.5).then_inc(consts, 1)
            pool.wait_ge(consts, 2)
            def first_gained(g):
                pool.wait_ge(raw_in[g], 16)
                if g >= 3:
                    pool.wait_ge(low_in.sem, low_in.after("pre", 0, g - 3))
                gained(stage_a[g % 3], raw[g], 0 if g < 8 else 2)

            def memory_heads(l):
                heads("pre", 0, l, k_rstds[l], quarters[l].rearrange("p b (h d) -> p (b h) d", d=HD))

            rstd(T, "pre", 0, "ss_mem")
            first_gained(0)
            memory_heads(0)
            first_gained(1)
            first_gained(2)
            memory_heads(1)
            first_gained(3)
            first_gained(4)
            rstd(T, "pre", 0, "ss")
            for g in range(5, 10):
                first_gained(g)

            own.loop(9)
            with pool.Fori(0, TILES // 2) as it:
                for p in range(2):
                    t = it * 2 + p
                    own.tile(t)
                    heads("A", t, 0, q_rstds[0][:, 0:8], q_of(0)[:, 0:8, :], unit_a[:, 0:1].to_broadcast([P, 8]))
                    Z.wait_read(pool, "A", t, "u2")
                    Z.wait_read(pool, "A", t, "u1")
                    own(tt(win_a[:, 0:6, 2:UW], u[:, :, 2:UW], u[:, :, 1:UW - 1], ALU.add))
                    own.wait()
                    own(tt(win_b[:, 1:6, 4:UW], win_a[:, 1:6, 4:UW], win_a[:, 1:6, 2:UW - 2], ALU.add))
                    mem_norm("A", t, 0)
                    mem_norm("A", t, 1)
                    own.wait()
                    own(tt(win_a[:, 3:6, 8:UW], win_b[:, 3:6, 8:UW], win_b[:, 3:6, 4:UW - 4], ALU.add))
                    own(tt(win_b[0:HD, 1, 16:UW], win_a[0:HD, 1, 16:UW], ones[0:HD, 0:1].to_broadcast([HD, NT]), ALU.mult))
                    own.wait()
                    own(tt(win_b[:, 4:6, 16:UW], win_a[:, 4:6, 16:UW], win_a[:, 4:6, 8:UW - 8], ALU.add))
                    own.wait()
                    tt(win_b[0:HD, 4, 16:UW], win_a[0:HD, 4, 16:UW], ones[0:HD, 0:1].to_broadcast([HD, NT]), ALU.mult).then_inc(win_sums.sem, 1)
                    pool.wait_ge(stageb_in.sem, stageb_in.after("A", t))
                    gained(stage_b, stage_b, 1)
                    sums("A", t, 0)
                    rstd(T, "A", t, "ss")
            own.end_loop(TILES)

            heads("SA", 0, 0, q_rstds[0][0:NS, 0:4], q_of(0)[0:NS, 0:4, :], unit_a[0:NS, 0:1].to_broadcast([NS, 4]))
            Z.wait_read(pool, "SA", 0, "u2")
            Z.wait_read(pool, "SA", 0, "u1")
            pool.wait_ge(state_set, 1)

            def b4(x, c):
                return by_batch(x[:, c])
            for dst, src, chunks, w in ((win_a, u, range(0, 6), 2), (win_b, win_a, range(1, 6), 4),
                                        (win_a, win_b, range(3, 6), 8), (win_b, win_a, range(4, 6), 16)):
                for c in chunks:
                    s_ = b4(src, c)
                    own(tt(b4(dst, c)[:, :, w:US], s_[:, :, w:US], s_[:, :, w - w // 2:US - w // 2], ALU.add))
                own.wait()
            for c in (1, 4):
                last = nc.gpsimd.tensor_copy(b4(win_b, c)[0:HD, :, 16:US], b4(win_a, c)[0:HD, :, 16:US])
            last.then_inc(win_sums.sem, 1)
            sample_mem_norm("SA")
            sums("SA", 0, 0)
            rstd(T, "SA", 0, "ss")
            def window_norm(t, n):
                i = n % 2
                pool.wait_ge(w_inv_in.sem, w_inv_in.after("B", t, n))
                r = w_inv[:, i, :].rearrange("p (e n) -> p e n", n=1).to_broadcast([P, 4, BLK])
                tt(sw[:, i], sw[:, i], r, ALU.mult).then_inc(pw_norm.sem, 1)

            own.loop(8)
            with pool.Fori(0, TILES // 2) as it:
                for p in range(2):
                    t = it * 2 + p
                    own.tile(t)
                    heads("B", t, 0, k_rstds[0], k_tok[:, :, :, :].rearrange("p b h d -> p (b h) d"), k_unit)
                    heads("B", t, 1, q_rstds[0], q_of(0), unit_heads)
                    heads("B", t, 2, q_rstds[1], q_of(1), unit_heads)
                    mem_norm("B", t, 0)
                    window_norm(t, 0)
                    window_norm(t, 1)
                    mem_norm("B", t, 1)
                    for i in range(2, 6):
                        window_norm(t, i)
                    sums("B", t, 0)
                    rstd(V, "B", t, "ss")
            own.end_loop(TILES)

            heads("SB", 0, 0, k_rstds[0][0:NS, 0:4], k_tok[0:NS, 0], k_unit[0:NS, 0:4])
            heads("SB", 0, 1, q_rstds[0][0:NS, :], q_of(0)[0:NS], unit_heads[0:NS])
            pool.wait_ge(w_inv_in.sem, w_inv_in.after("SB", 0))
            tt(sw_s, sw_s, s_inv.rearrange("p (b n) -> p b n", n=1).to_broadcast([96, DB, P]), ALU.mult)\
                .then_inc(pw_norm.sem, 1)
            sample_mem_norm("SB")


def _feature_major(w):
    k, n = w.shape
    return w.reshape(k // P, P, n).transpose(1, 0, 2)


def _column_groups(w):
    return np.stack([_feature_major(w[:, g * 256:(g + 1) * 256]) for g in range(w.shape[1] // 256)])


def _tables():
    c = {}
    i = np.arange(P)
    c["ident"] = np.eye(P)
    c["cur_hi"] = np.where(i[None, :] <= i[:, None], BIG, -BIG)
    c["prev_hi"] = -c["cur_hi"]
    c["prev_now"] = np.full((P, P), -BIG)
    c["curT"] = (i[:, None] <= i[None, :]) * 1.0
    c["prevT"] = 1.0 - c["curT"]
    t = np.arange(P) % DS
    j = np.arange(DS)
    c["new_hi"] = np.where(j[None, :] <= t[:, None], BIG, -BIG)
    c["old_hi"] = -c["new_hi"]
    tr = np.arange(96) % DS
    c["oldT"] = (i[:, None] > tr[None, :]) * 1.0
    c["newT"] = (i[:, None] <= tr[None, :]) * 1.0
    win = np.repeat(np.array(WINDOWS), 192)
    win = win.reshape(POOLC, P).T
    c["invw"] = 1.0 / win
    c["corr"] = win[:, :, None] / np.minimum(np.arange(16)[None, None, :] + 1, win[:, :, None])
    inv = np.float32(500000.0) ** (-np.arange(8, dtype=np.float32) * np.float32(2.0) / np.float32(16))
    for suffix, pos in (("", np.arange(SEQ).reshape(16, P)), ("_s", (SEQ + np.arange(P) % DS).reshape(1, P))):
        ang = (pos.astype(np.float32)[..., None] * inv.astype(np.float32)).astype(np.float32)
        cos, sin = np.cos(ang), np.sin(ang)
        c["cos" + suffix] = np.concatenate([cos, cos], -1).transpose(1, 0, 2)
        c["sin" + suffix] = np.concatenate([-sin, sin], -1).transpose(1, 0, 2)
    return c


def kernel(x_prompt, x_sample, state_pool, cache_swa_k, cache_swa_v, cache_mem_k, cache_mem_v, mem_prompt,
           norm_a, w_in_a, pool_mix_w, pool_scale, w_out_a, kv_norm, w_kv, k_norm,
           norm_b, w_in_b, q_norm, sinks, w_out_b, mem_norm, w_mem_kv, mem_q_norm, mem_k_norm):
    import concourse.bacc as _bacc
    from concourse import mybir as _mybir
    from concourse.bass_utils import run_bass_kernel_spmd as _run

    f = np.float32
    (x_prompt, x_sample, state_pool, cache_swa_k, cache_swa_v, cache_mem_k, cache_mem_v, mem_prompt,
     norm_a, w_in_a, pool_mix_w, pool_scale, w_out_a, kv_norm, w_kv, k_norm,
     norm_b, w_in_b, q_norm, sinks, w_out_b, mem_norm, w_mem_kv, mem_q_norm, mem_k_norm) = (
        np.asarray(a) for a in (
            x_prompt, x_sample, state_pool, cache_swa_k, cache_swa_v, cache_mem_k, cache_mem_v, mem_prompt,
            norm_a, w_in_a, pool_mix_w, pool_scale, w_out_a, kv_norm, w_kv, k_norm,
            norm_b, w_in_b, q_norm, sinks, w_out_b, mem_norm, w_mem_kv, mem_q_norm, mem_k_norm))
    W = 768

    order = [(2 * (c // 3) + par) * 3 + c % 3 for c in range(POOLC) for par in range(2)]
    by_head = np.concatenate([np.arange(h * HD, (h + 1) * HD) for h in order])

    arrays = {}
    x = np.zeros((TILES + 1, P, KC, NT), f)
    x[:TILES] = x_prompt[0].reshape(TILES, NT, KC, P).transpose(0, 3, 2, 1)
    x[TILES, :, :, :NS] = x_sample.reshape(NS, KC, P).transpose(2, 1, 0)
    arrays["x"] = x
    arrays["memx"] = _feature_major(mem_prompt[0].T)
    arrays["w_mem"] = np.concatenate([_column_groups(w_mem_kv[l]) for l in range(2)])

    a = w_in_a[0]
    arrays["w_in_a"] = _column_groups(np.concatenate([a[:, 2 * W:2 * W + 256], a[:, :2 * W], a[:, 2 * W + 256:]], 1))
    b = w_in_b[0]
    arrays["w_in_b"] = _column_groups(np.concatenate(
        [b[:, :W][:, by_head], b[:, 2 * W:2 * W + 256], b[:, W:2 * W][:, by_head], b[:, 2 * W + 256:], w_kv], 1))
    arrays["w_out_a"] = _column_groups(w_out_a[0])
    wo = w_out_b[0]
    arrays["w_out_b"] = _column_groups(np.concatenate([wo[:W][by_head], wo[W:]], 0))

    full = np.zeros((W, W), f)
    for g in range(4):
        full[g * 192:(g + 1) * 192, g * 192:(g + 1) * 192] = pool_mix_w[0, g]
    blocks = [full[i * P:(i + 1) * P, o * P:(o + 1) * P] for o in range(POOLC) for i in range(POOLC)
              if o // 3 == i // 3 and abs(o - i) < 2]
    arrays["mix"] = np.concatenate(blocks, 1)

    small = np.zeros((P, NSMALL), f)

    def put(name, value):
        at, n = SMALL[name]
        small[:, at:at + n] = np.asarray(value).reshape(P, n)

    for name, value in _tables().items():
        put(name, value)
    put("gain", np.stack([g.reshape(KC, P).T for g in (norm_a[0], norm_b[0], kv_norm, mem_norm[0], mem_norm[1])], 1))
    put("pscale", pool_scale[0].reshape(POOLC, P).T)
    rows = np.concatenate([mem_q_norm[0], mem_q_norm[1], mem_k_norm[0], mem_k_norm[1], k_norm, q_norm[0]])
    put("row", np.broadcast_to(rows, (P, 6 * HD)))
    s = sinks[0]
    put("sink", np.broadcast_to([s[order[2 * (2 * gi + c) + par]] for gi in range(3) for par in range(2)
                                 for c in range(2)], (P, QH)))
    col = np.zeros((P,), f)
    col[:96] = np.repeat(s, DS)
    put("sinkcol", col)
    arrays["small"] = small

    arrays["state"] = state_pool[0].transpose(2, 0, 1).reshape(POOLC, P, DB, PAD).transpose(1, 0, 2, 3)
    arrays["kc_tok"] = cache_swa_k.reshape(DB, BLK, 256)
    arrays["vc_tok"] = cache_swa_v.reshape(DB, BLK, 256)
    arrays["kc"] = cache_swa_k.reshape(DB, BLK, 2, P).transpose(3, 2, 0, 1)
    arrays["vc"] = cache_swa_v.reshape(DB, BLK, 256).transpose(1, 0, 2)
    arrays["mem_ks"] = cache_mem_k.reshape(2, DB, NMEM, 2, P).transpose(0, 1, 4, 3, 2)
    arrays["mem_vs"] = cache_mem_v.reshape(2, DB, MC, P, 256).transpose(0, 1, 3, 2, 4)

    outs = {"y": (TILES + 1, P, KC, NT), "pool_p": (P, POOLC, PAD), "pool_s": (P, POOLC, DB, PAD),
            "swa_k_p": (BLK, 256), "swa_v_p": (BLK, 256), "swa_k_s": (DB, BLK, 256), "swa_v_s": (DB, BLK, 256),
            "mem_k": (2, P, MC, 256), "mem_v": (2, P, MC, 256)}
    nc = _bacc.Bacc("TRN2", target_bir_lowering=False, num_devices=1)
    F = _mybir.dt.float32
    io = {}
    for name in arrays:
        arrays[name] = np.ascontiguousarray(arrays[name], dtype=f)
        io[name] = nc.dram_tensor(name, arrays[name].shape, F, kind="ExternalInput").ap()
    for name, shape in outs.items():
        io[name] = nc.dram_tensor(name, shape, F, kind="ExternalOutput").ap()
    io["x1"] = nc.dram_tensor("x1", (TILES + 1, P, KC, NT), F, kind="Internal").ap()
    io["parts"] = nc.dram_tensor("parts", (10, P, 2, KC, 256), _mybir.dt.float16, kind="Internal").ap()
    io["kt1"] = nc.dram_tensor("kt1", (P, 2, NMEM), F, kind="Internal").ap()
    build(nc, io)
    r = _run(nc, [arrays], core_ids=[0]).results[0]

    y = r["y"]
    y_prompt = y[:TILES].transpose(0, 3, 2, 1).reshape(1, SEQ, D)
    y_sample = y[TILES, :, :, :NS].transpose(2, 1, 0).reshape(DB, DS, D)
    pool_p = r["pool_p"].transpose(2, 1, 0).reshape(1, 1, PAD, W)
    pool_s = r["pool_s"].transpose(2, 3, 1, 0).reshape(1, DB, PAD, W)
    mem = [r[n].transpose(0, 2, 1, 3).reshape(2, 1, NMEM, 4, HD) for n in ("mem_k", "mem_v")]
    return (y_prompt, y_sample, pool_p, pool_s,
            r["swa_k_p"].reshape(1, BLK, 4, HD), r["swa_v_p"].reshape(1, BLK, 4, HD),
            r["swa_k_s"].reshape(DB, BLK, 4, HD), r["swa_v_s"].reshape(DB, BLK, 4, HD), *mem)
```
